# Optimizing a Trainium2 kernel written in Bass

```python
import jax, jax.numpy as jnp
from jax import lax
import numpy as np

D_MODEL = 1024
BATCH = 1
SEQ = 512
DEPTH = 2
DEC_BATCH = 8
DEC_SEQ = 1
PAST_LEN = 256
PAGE_SIZE = 128

N_EVEN = (DEPTH + 1) // 2
N_ODD = DEPTH // 2
MIX_W = D_MODEL
HALF_W = MIX_W // 2
D_FF = 4 * D_MODEL
CONV_W = 3
CONV_CH = HALF_W
ML_HEADS = 4
ML_DIM = HALF_W // ML_HEADS
ML_CHUNK = 64
HEAD_DIM = 64
KV_GROUPS = 2
NSA_HEADS = HALF_W // HEAD_DIM
DSA_HEADS = HALF_W // HEAD_DIM
BLK = 64
NSA_TOPN = 8
WINDOW = 256
IDX_HEADS = 4
IDX_DIM = 32
DSA_TOPK_MAX = 256
Q_BLOCK = 128
KV_SLOTS = 6
FORCE_SCORE = 1e4
ALPHA = (2.0 * DEPTH) ** 0.25
BETA = (8.0 * DEPTH) ** -0.25
LN_EPS = 1e-5
E_SIZES = (CONV_CH, CONV_CH, CONV_CH, HALF_W, HALF_W, HALF_W, HALF_W, ML_HEADS, ML_HEADS)
O_SIZES = (NSA_HEADS * HEAD_DIM, 2 * KV_GROUPS * HEAD_DIM, 2 * KV_GROUPS * HEAD_DIM, 2 * KV_GROUPS * HEAD_DIM, 3 * NSA_HEADS, DSA_HEADS * HEAD_DIM, 2 * KV_GROUPS * HEAD_DIM, IDX_HEADS * IDX_DIM, IDX_DIM, IDX_HEADS)
E_COLS = sum(E_SIZES)
O_COLS = sum(O_SIZES)

kernel_name = 'hybrid_conv_mlstm_nsa_dsa_step'

def _split(z, sizes):
    cuts = [int(c) for c in np.cumsum(sizes)[:-1]]
    return jnp.split(z, cuts, axis=-1)

def alibi_slopes(n):
    return jnp.asarray(np.power(2.0, -8.0 * np.arange(1, n + 1) / n), dtype=jnp.float32)

def layer_norm(x, g, b):
    xf = x.astype(jnp.float32)
    mu = jnp.mean(xf, axis=-1, keepdims=True)
    var = jnp.mean(jnp.square(xf - mu), axis=-1, keepdims=True)
    y = (xf - mu) * lax.rsqrt(var + LN_EPS) * g.astype(jnp.float32) + b.astype(jnp.float32)
    return y.astype(x.dtype)

def masked_softmax(s, mask):
    s = jnp.where(mask, s.astype(jnp.float32), -jnp.inf)
    m = jnp.max(s, axis=-1, keepdims=True)
    e = jnp.exp(s - jnp.where(jnp.isfinite(m), m, 0.0))
    return e / jnp.maximum(jnp.sum(e, axis=-1, keepdims=True), 1e-30)

def sq_relu_mlp(x, w_up, w_down):
    return jnp.square(jax.nn.relu(x @ w_up)) @ w_down

def short_conv(u_ext, w, b):
    t = u_ext.shape[1] - (CONV_W - 1)
    return b + sum(w[j] * u_ext[:, j:j + t] for j in range(CONV_W))

def mlstm_chunk(carry, inp):
    c_st, n_st, m_st = carry
    q, k, v, ig, lf = inp
    L = q.shape[2]
    b = jnp.cumsum(lf, axis=-1)
    causal = jnp.tril(jnp.ones((L, L), dtype=bool))
    dmat = jnp.where(causal, b[..., :, None] - b[..., None, :] + ig[..., None, :], -jnp.inf)
    inter = b + m_st[..., None]
    m_t = jnp.maximum(inter, jnp.max(dmat, axis=-1))
    w_intra = jnp.exp(dmat - m_t[..., None])
    w_inter = jnp.exp(inter - m_t)
    s = jnp.einsum('bhtd,bhsd->bhts', q, k) * w_intra
    num = jnp.einsum('bhts,bhsd->bhtd', s, v) + w_inter[..., None] * jnp.einsum('bhed,bhtd->bhte', c_st, q)
    den = jnp.sum(s, axis=-1) + w_inter * jnp.einsum('bhd,bhtd->bht', n_st, q)
    h = num / jnp.maximum(jnp.abs(den), jnp.exp(-m_t))[..., None]
    m_new = m_t[..., -1]
    w_state = jnp.exp(b[..., -1:] - b + ig - m_new[..., None])
    decay = jnp.exp(b[..., -1] + m_st - m_new)
    c_new = decay[..., None, None] * c_st + jnp.einsum('bhs,bhse,bhsd->bhed', w_state, v, k)
    n_new = decay[..., None] * n_st + jnp.einsum('bhs,bhsd->bhd', w_state, k)
    return (c_new, n_new, m_new), h

def even_mixer(x, w_in, gate_b, conv_w, conv_b, w_out, conv_prev, ml_state, chunk):
    f32 = jnp.float32
    bn, t, _ = x.shape
    h, bg, cg, q, k, v, og, ig, fg = _split(x @ w_in, E_SIZES)
    u = cg * h
    u_ext = jnp.concatenate([conv_prev.astype(u.dtype), u], axis=1)
    y_a = bg * short_conv(u_ext, conv_w, conv_b)
    new_conv = u_ext[:, u_ext.shape[1] - (CONV_W - 1):]
    heads = lambda a: a.reshape(bn, t, ML_HEADS, ML_DIM).astype(f32)
    q, k, v = heads(q), heads(k) * (ML_DIM ** -0.5), heads(v)
    ig = (ig + gate_b[:ML_HEADS]).astype(f32)
    lf = jax.nn.log_sigmoid((fg + gate_b[ML_HEADS:]).astype(f32))
    nc = t // chunk

    def to_chunks(a):
        a = jnp.moveaxis(a.reshape((bn, nc, chunk) + a.shape[2:]), 1, 0)
        return jnp.swapaxes(a, 2, 3)

    carry = tuple(s.astype(f32) for s in ml_state)
    carry, hs = lax.scan(mlstm_chunk, carry, tuple(to_chunks(a) for a in (q, k, v, ig, lf)))
    hs = jnp.swapaxes(jnp.moveaxis(hs, 0, 1), 2, 3).reshape(bn, t, HALF_W)
    y_b = jax.nn.sigmoid(og) * hs.astype(x.dtype)
    out = jnp.concatenate([y_a, y_b], axis=-1) @ w_out
    return out, new_conv, tuple(s.astype(x.dtype) for s in carry)

def odd_attend(qn, gates, qd, qi, wi, q_pos, kc, vc, slc, dsa_kv, kidx, kw, kw_pos, topn, topk):
    f32 = jnp.float32
    bn, tq, g, r, _ = qn.shape
    nb = kc.shape[1]
    L = kidx.shape[1]
    scale = HEAD_DIM ** -0.5
    m_n = alibi_slopes(NSA_HEADS).reshape(g, r)
    m_d = alibi_slopes(DSA_HEADS).reshape(KV_GROUPS, DSA_HEADS // KV_GROUPS)
    jb = jnp.arange(nb)
    dist_c = q_pos[:, None] - (jb * BLK + BLK - 1)[None, :]
    s_c = jnp.einsum('btgrd,bjgd->btgrj', qn, kc).astype(f32) * scale - m_n[:, :, None] * dist_c[:, None, None, :].astype(f32)
    p_c = masked_softmax(s_c, (dist_c >= 0)[:, None, None, :])
    o_c = jnp.einsum('btgrj,bjgd->btgrd', p_c.astype(vc.dtype), vc)
    cur = q_pos // BLK
    imp = jnp.sum(p_c, axis=3)
    forced = (jb[None, :] == 0) | (jb[None, :] == cur[:, None]) | (jb[None, :] == cur[:, None] - 1)
    imp = jnp.where(forced[:, None, :], FORCE_SCORE, imp)
    imp = jnp.where((jb[None, :] <= cur[:, None])[:, None, :], imp, -jnp.inf)
    top_val, top_idx = lax.top_k(imp, topn)
    b_ix = jnp.arange(bn)[:, None, None, None]
    g_ix = jnp.arange(g)[None, None, :, None]
    sel = slc[b_ix, g_ix, top_idx]
    pos = top_idx[..., None] * BLK + jnp.arange(BLK)
    dist_s = q_pos[None, :, None, None, None] - pos
    mask_s = (dist_s >= 0) & jnp.isfinite(top_val)[..., None]
    s_s = jnp.einsum('btgrd,btgnpd->btgrnp', qn, sel[..., 0, :]).astype(f32) * scale - m_n[None, None, :, :, None, None] * dist_s[:, :, :, None].astype(f32)
    shp = s_s.shape
    p_s = masked_softmax(s_s.reshape(shp[:4] + (-1,)), mask_s[:, :, :, None].reshape(bn, tq, g, 1, -1)).reshape(shp)
    o_s = jnp.einsum('btgrnp,btgnpd->btgrd', p_s.astype(sel.dtype), sel[..., 1, :])
    dist_w = q_pos[:, None] - kw_pos[None, :]
    mask_w = (dist_w >= 0) & (dist_w < WINDOW) & (kw_pos >= 0)[None, :]
    s_w = jnp.einsum('btgrd,blgd->btgrl', qn, kw[:, :, 0]).astype(f32) * scale - m_n[:, :, None] * dist_w[:, None, None, :].astype(f32)
    p_w = masked_softmax(s_w, mask_w[:, None, None, :])
    o_w = jnp.einsum('btgrl,blgd->btgrd', p_w.astype(kw.dtype), kw[:, :, 1])
    o_n = (gates[..., 0:1] * o_c + gates[..., 1:2] * o_s + gates[..., 2:3] * o_w).astype(qn.dtype).reshape(bn, tq, -1)
    k_pos = jnp.arange(L)
    isc = jnp.einsum('bthe,ble->bthl', qi, kidx).astype(f32) * (IDX_DIM ** -0.5)
    isc = jnp.einsum('bthl,bth->btl', jax.nn.relu(isc), wi.astype(f32)) * (IDX_HEADS ** -0.5)
    isc = jnp.where((k_pos[None, :] <= q_pos[:, None])[None], isc, -jnp.inf)
    i_val, i_idx = lax.top_k(isc, topk)
    sel_d = dsa_kv[jnp.arange(bn)[:, None, None], i_idx]
    dist_d = (q_pos[None, :, None] - i_idx).astype(f32)
    s_d = jnp.einsum('btgrd,btkgd->btgrk', qd, sel_d[:, :, :, 0]).astype(f32) * scale - m_d[None, None, :, :, None] * dist_d[:, :, None, None, :]
    p_d = masked_softmax(s_d, jnp.isfinite(i_val)[:, :, None, None, :])
    o_d = jnp.einsum('btgrk,btkgd->btgrd', p_d.astype(sel_d.dtype), sel_d[:, :, :, 1]).reshape(bn, tq, -1)
    return jnp.concatenate([o_n, o_d.astype(qn.dtype)], axis=-1)

def odd_mixer(x, w_in, w_cmp, w_out, past_kv, past_idx, past_win, keep):
    bn, t, _ = x.shape
    p_len = past_kv.shape[1]
    wp = past_win.shape[1]
    g, r = KV_GROUPS, NSA_HEADS // KV_GROUPS
    qn, kvc, kvs, kvw, gates, qd, kvd, qi, ki, wi = _split(x @ w_in, O_SIZES)
    qn = qn.reshape(bn, t, g, r, HEAD_DIM)
    qd = qd.reshape(bn, t, g, DSA_HEADS // g, HEAD_DIM)
    gates = jax.nn.sigmoid(gates.astype(jnp.float32)).reshape(bn, t, g, r, 3)
    qi = qi.reshape(bn, t, IDX_HEADS, IDX_DIM)
    kv_new = jnp.concatenate([kvc, kvs, kvd], axis=-1).reshape(bn, t, KV_SLOTS, g, HEAD_DIM)
    kvw_new = kvw.reshape(bn, t, 2, g, HEAD_DIM)
    kv = jnp.concatenate([past_kv.astype(kv_new.dtype), kv_new], axis=1)
    kidx = jnp.concatenate([past_idx.astype(ki.dtype), ki], axis=1)
    win_all = jnp.concatenate([past_win.astype(kvw_new.dtype), kvw_new], axis=1)
    L = p_len + t
    nb = -(-L // BLK)
    kvb = jnp.pad(kv[:, :, :4], ((0, 0), (0, nb * BLK - L), (0, 0), (0, 0), (0, 0)))
    kvb = kvb.reshape(bn, nb, BLK, 4, g, HEAD_DIM)
    kc = jnp.einsum('bjpgd,pd->bjgd', kvb[:, :, :, 0], w_cmp[0])
    vc = jnp.einsum('bjpgd,pd->bjgd', kvb[:, :, :, 1], w_cmp[1])
    slc = jnp.transpose(kvb[:, :, :, 2:4], (0, 4, 1, 2, 3, 5))
    dsa_kv = kv[:, :, 4:6]
    topn = min(NSA_TOPN, nb)
    topk = min(DSA_TOPK_MAX, L // 4)
    qb = t if t <= Q_BLOCK else Q_BLOCK
    nqb = t // qb

    def blocks(a):
        return jnp.moveaxis(a.reshape((bn, nqb, qb) + a.shape[2:]), 1, 0)

    def body(args):
        qn_b, g_b, qd_b, qi_b, wi_b, start = args
        q_pos = p_len + start + jnp.arange(qb)
        kw = lax.dynamic_slice_in_dim(win_all, start, wp + qb, axis=1)
        kw_pos = p_len - wp + start + jnp.arange(wp + qb)
        return odd_attend(qn_b, g_b, qd_b, qi_b, wi_b, q_pos, kc, vc, slc, dsa_kv, kidx, kw, kw_pos, topn, topk)

    starts = jnp.arange(nqb, dtype=jnp.int32) * qb
    o = lax.map(body, (blocks(qn), blocks(gates), blocks(qd), blocks(qi), blocks(wi), starts))
    o = jnp.moveaxis(o, 0, 1).reshape(bn, t, MIX_W)
    new_win = win_all[:, win_all.shape[1] - keep:]
    return o @ w_out, kv_new, ki, new_win

def setup_inputs(seed: int = 0) -> dict:
    key = jax.random.key(seed)
    ks = jax.random.split(key, 24)

    def nrm(k, shape, s=1.0):
        return s * jax.random.normal(k, shape, jnp.float32)

    n_pages = PAST_LEN // PAGE_SIZE
    n_used = DEC_BATCH * n_pages
    n_pool = n_used + max(1, n_used // 4)
    win_buf = min(WINDOW, PAST_LEN)
    x_prompt = nrm(ks[0], (BATCH, SEQ, D_MODEL))
    x_sample = nrm(ks[1], (DEC_BATCH, DEC_SEQ, D_MODEL))
    state_conv = nrm(ks[2], (N_EVEN, DEC_BATCH, CONV_W - 1, CONV_CH))
    state_C = nrm(ks[3], (N_EVEN, DEC_BATCH, ML_HEADS, ML_DIM, ML_DIM), 0.1)
    state_n = nrm(ks[4], (N_EVEN, DEC_BATCH, ML_HEADS, ML_DIM), 0.1)
    state_m = nrm(ks[5], (N_EVEN, DEC_BATCH, ML_HEADS))
    cache_kv = nrm(ks[6], (N_ODD, n_pool, PAGE_SIZE, KV_SLOTS, KV_GROUPS, HEAD_DIM))
    cache_idx = nrm(ks[7], (N_ODD, n_pool, PAGE_SIZE, IDX_DIM))
    cache_win = nrm(ks[8], (N_ODD, DEC_BATCH, win_buf, 2, KV_GROUPS, HEAD_DIM))
    page_table = jax.random.permutation(ks[9], n_pool)[:n_used].reshape(DEC_BATCH, n_pages).astype(jnp.int32)
    w_in_e = nrm(ks[10], (N_EVEN, D_MODEL, E_COLS), D_MODEL ** -0.5)
    gate_b_e = jnp.concatenate([nrm(ks[11], (N_EVEN, ML_HEADS), 0.1), 3.0 + nrm(ks[12], (N_EVEN, ML_HEADS), 0.1)], axis=-1)
    conv_w = nrm(ks[13], (N_EVEN, CONV_W, CONV_CH), CONV_W ** -0.5)
    conv_b = nrm(ks[14], (N_EVEN, CONV_CH), 0.01)
    w_out_e = nrm(ks[15], (N_EVEN, MIX_W, D_MODEL), BETA * MIX_W ** -0.5)
    w_in_o = nrm(ks[16], (N_ODD, D_MODEL, O_COLS), D_MODEL ** -0.5)
    w_cmp = (1.0 + nrm(ks[17], (N_ODD, 2, BLK, HEAD_DIM), 0.1)) / BLK
    w_out_o = nrm(ks[18], (N_ODD, MIX_W, D_MODEL), BETA * MIX_W ** -0.5)
    w_up = nrm(ks[19], (DEPTH, D_MODEL, D_FF), D_MODEL ** -0.5)
    w_down = nrm(ks[20], (DEPTH, D_FF, D_MODEL), BETA * D_FF ** -0.5)
    ln_g = 1.0 + nrm(ks[21], (DEPTH, 2, D_MODEL), 0.05)
    ln_b = nrm(ks[22], (DEPTH, 2, D_MODEL), 0.02)
    return {'x_prompt': x_prompt, 'x_sample': x_sample, 'state_conv': state_conv, 'state_C': state_C,
            'state_n': state_n, 'state_m': state_m, 'cache_kv': cache_kv, 'cache_idx': cache_idx,
            'cache_win': cache_win, 'page_table': page_table, 'w_in_e': w_in_e, 'gate_b_e': gate_b_e,
            'conv_w': conv_w, 'conv_b': conv_b, 'w_out_e': w_out_e, 'w_in_o': w_in_o, 'w_cmp': w_cmp,
            'w_out_o': w_out_o, 'w_up': w_up, 'w_down': w_down, 'ln_g': ln_g, 'ln_b': ln_b}

def reference(x_prompt, x_sample, state_conv, state_C, state_n, state_m, cache_kv, cache_idx, cache_win, page_table,
              w_in_e, gate_b_e, conv_w, conv_b, w_out_e, w_in_o, w_cmp, w_out_o, w_up, w_down, ln_g, ln_b):
    f32 = jnp.float32
    bp, dbs = x_prompt.shape[0], x_sample.shape[0]
    dt = x_prompt.dtype
    past = page_table.shape[1] * cache_kv.shape[2]
    keep = cache_win.shape[2]
    yp, ys = x_prompt, x_sample
    cv_pl, cv_sl, c_pl, c_sl, n_pl, n_sl, m_pl, m_sl = [], [], [], [], [], [], [], []
    kv_pl, kv_sl, ix_pl, ix_sl, w_pl, w_sl = [], [], [], [], [], []
    for layer in range(DEPTH):
        i = layer // 2
        if layer % 2 == 0:
            zero_state = (jnp.zeros((bp, ML_HEADS, ML_DIM, ML_DIM), f32), jnp.zeros((bp, ML_HEADS, ML_DIM), f32), jnp.zeros((bp, ML_HEADS), f32))
            mp, cvp, stp = even_mixer(yp, w_in_e[i], gate_b_e[i], conv_w[i], conv_b[i], w_out_e[i],
                                      jnp.zeros((bp, CONV_W - 1, CONV_CH), dt), zero_state, ML_CHUNK)
            ms, cvs, sts = even_mixer(ys, w_in_e[i], gate_b_e[i], conv_w[i], conv_b[i], w_out_e[i],
                                      state_conv[i], (state_C[i], state_n[i], state_m[i]), ys.shape[1])
            cv_pl.append(cvp); cv_sl.append(cvs)
            c_pl.append(stp[0]); c_sl.append(sts[0])
            n_pl.append(stp[1]); n_sl.append(sts[1])
            m_pl.append(stp[2]); m_sl.append(sts[2])
        else:
            past_kv = cache_kv[i][page_table].reshape(dbs, past, KV_SLOTS, KV_GROUPS, HEAD_DIM)
            past_idx = cache_idx[i][page_table].reshape(dbs, past, IDX_DIM)
            mp, kvp, ixp, wnp = odd_mixer(yp, w_in_o[i], w_cmp[i], w_out_o[i],
                                          jnp.zeros((bp, 0, KV_SLOTS, KV_GROUPS, HEAD_DIM), dt),
                                          jnp.zeros((bp, 0, IDX_DIM), dt),
                                          jnp.zeros((bp, WINDOW, 2, KV_GROUPS, HEAD_DIM), dt), keep)
            ms, kvs, ixs, wns = odd_mixer(ys, w_in_o[i], w_cmp[i], w_out_o[i], past_kv, past_idx, cache_win[i], keep)
            kv_pl.append(kvp); kv_sl.append(kvs)
            ix_pl.append(ixp); ix_sl.append(ixs)
            w_pl.append(wnp); w_sl.append(wns)
        yp = layer_norm(ALPHA * yp + mp, ln_g[layer, 0], ln_b[layer, 0])
        ys = layer_norm(ALPHA * ys + ms, ln_g[layer, 0], ln_b[layer, 0])
        yp = layer_norm(ALPHA * yp + sq_relu_mlp(yp, w_up[layer], w_down[layer]), ln_g[layer, 1], ln_b[layer, 1])
        ys = layer_norm(ALPHA * ys + sq_relu_mlp(ys, w_up[layer], w_down[layer]), ln_g[layer, 1], ln_b[layer, 1])
    conv_p, conv_s = jnp.stack(cv_pl), jnp.stack(cv_sl)
    c_p, c_s = jnp.stack(c_pl), jnp.stack(c_sl)
    n_p, n_s = jnp.stack(n_pl), jnp.stack(n_sl)
    m_p, m_s = jnp.stack(m_pl), jnp.stack(m_sl)
    kv_p, kv_s = jnp.stack(kv_pl), jnp.stack(kv_sl)
    idx_p, idx_s = jnp.stack(ix_pl), jnp.stack(ix_sl)
    win_p, win_s = jnp.stack(w_pl), jnp.stack(w_sl)
    return (yp, ys, conv_p, conv_s, c_p, c_s, n_p, n_s, m_p, m_s, kv_p, kv_s, idx_p, idx_s, win_p, win_s)


_drawn_inputs = setup_inputs


def setup_inputs(seed=0):
    import zlib

    import numpy as np

    out = dict(_drawn_inputs(seed))
    spreads = {}
    factors = {'conv_b': 14.452, 'w_cmp': 35.285}
    for name, (base, spread) in spreads.items():
        noise = np.random.default_rng([zlib.crc32(name.encode()), seed]).standard_normal(out[name].shape)
        drawn = base * np.exp(spread * noise) if base else spread * noise
        out[name] = __import__('jax').numpy.asarray(drawn.astype(out[name].dtype))
    for name, factor in factors.items():
        out[name] = (out[name] * factor).astype(out[name].dtype)
    return out
```

```python
from contextlib import ExitStack

import concourse.bass as bass
from concourse import mybir

F32 = mybir.dt.float32
I32 = mybir.dt.int32
ALU = mybir.AluOpType
ACT = mybir.ActivationFunctionType
AX = mybir.AxisListType

P = 128
D = 1024
KD = D // P
S = 512
B = 8
T = S + B
H2 = T // 2
QT = S // P
FF = 4096
KF = FF // P
MH = 4
NH = 8
HD = 64
NP = NH // 2
BLK = 64
NB = S // BLK
PAST = 256
PAGE = 128
NPG = PAST // PAGE
NT = B * NPG
NBS = PAST // BLK
LS = PAST + 1
TOPK = min(256, S // 4)
TOPK_S = min(256, LS // 4)
ALPHA = 4.0 ** 0.25
LN_EPS = 1e-5
NEG = -1e30
TAKEN = -3e38
MH_SCALE = 128.0 ** -0.5
SLOTS = ("kc", "vc", "ks", "vs", "kd", "vd", "kw", "vw")
IDX_SCALE = 32.0 ** -0.5
SLOPE = [2.0 ** -(h + 1) for h in range(NH)]
SLOT = 4096
NSLOT = 3
LN_POOL = (3, 6)
SMALL = 5120


def build(nc, x_prompt, x_sample, state_conv, state_C, state_n, state_m, cache_kv, cache_idx, cache_win, page_table,
          w_in_e, gate_b_e, conv_w, conv_b, w_out_e, w_in_o, w_cmp, w_out_o, w_up, w_down, ln_g, ln_b,
          y_p, y_s, conv_p, conv_s, c_p, c_s, n_p, n_s, m_p, m_s, kv_p, kv_s, idx_p, idx_s, win_p, win_s):
    E_TILE = [None] + [12 + i for i in range(12)] + [0, 1, 2, 3, 8, 9, 10, 11, 4, 5, 6, 7, 24, 25, 26, 27]
    G_IN0 = 0
    G_OUT0 = G_IN0 + len(E_TILE)
    G_UP0 = G_OUT0 + KD
    G_DN0 = G_UP0 + KF
    O_NAMES = ["misc", "ki4", "kd", "vd", "qi", "qd0", "qd1", "qd2", "qd3", "kc", "vc", "ks", "vs", "kw", "vw",
               "qn0", "qn1", "qn2", "qn3"]
    Z = {n: i for i, n in enumerate(O_NAMES)}
    G_IN1 = G_DN0 + KD
    G_OUT1 = G_IN1 + len(O_NAMES)
    G_UP1 = G_OUT1 + KD
    G_DN1 = G_UP1 + KF

    with ExitStack() as ctx:
        def sb(name, shape, dt=F32):
            return ctx.enter_context(nc.sbuf_tensor(name, shape, dt))

        def sem(name):
            return ctx.enter_context(nc.semaphore(name))

        ring = sb("ring", [P, NSLOT, SLOT])
        xT = sb("xT", [P, KD, T])
        ymix = sb("ymix", [P, KD, T])
        big = sb("big", [P, KF, T])
        cbuf = sb("cbuf", [P, 4096])
        att = sb("att", [P, 6144])
        ident = sb("ident", [P, P])
        ones = sb("ones", [P, P])
        meanM = sb("meanM", [P, P])
        colT = sb("colT", [P, 112])
        small = sb("small", [P, SMALL])
        ps = [ctx.enter_context(nc.psum_tensor(f"ps{i}", [P, 512], F32)) for i in range(8)]

        taken = [0]

        def piece(n):
            a = taken[0]
            taken[0] += n
            assert taken[0] <= SMALL, taken[0]
            return small[:, a:a + n]

        names = """x_in cols_in scs_in c_in pool_step small_in page_in consts_ok free_a free_b sq_done sum_r std_ok
            cen_p u_ok sp_ok outs c_new store_c nnew_ev ucol_ev p_raw p_ok cn_ev cen_v x_ready
            z_pool kiz_ok mm_done cw_ok kz_ok isc_used pvs_mm cmp_mm tm_a tm_b tms_ev y_a y_b hid_a
            hid_b mm_half stats_mm tin_a tin_b tin fg_mm rows_ok h12_mm prod_ok dots_mm nnew_ok
            head_used head_mm nnew_mm ucol_mm wt_ok pre_mm hd_fin vt_ok kt_ok s_mm pv_mm vw_ok cn_mm
            conv_ok smp_y isc_r isc_mm t1_mm t1_ev sel_mm sel_ev tm_mm tms_mm bt_ev bt_mm bs_mm
            qb_ok ix_r ixc_mm dsb_in dsb_mm cmp_ev cmpt_mm cmpt_ev pn_ok pb_mm pt_mm pt_ev os_ok
            kc_ok pc_mm vf_mm pc_n pct_mm pct_ev vf_ev q_sc q_mm q_n q_te q_t q_of q_o y_mm act_step
            std_in stats_ok nx_ok sg_e ws_ok gate_e sc_ok pe_ok pc_x pc_e q_m q_e dve_step""".split()
        sm = {n: sem(n) for n in names}
        gat = [sem(f"gathered{i}") for i in range(5)]
        w_sem = [sem(f"w_slot{i}") for i in range(NSLOT)]

        def rows(w, c0, c1):
            return w[:, c0:c1].rearrange("(k p) n -> p k n", p=P)

        chunks = []

        def chunk(parts, freed):
            chunks.append((parts, freed))
            return len(chunks) - 1

        def cols_of(slot, a, k, n):
            return ring[:, slot, a:a + k * n].rearrange("p (k n) -> p k n", k=k)

        def wide(w, c0, n, last_g):
            c = len(chunks)
            return chunk([(cols_of(c % NSLOT, 0, KD, n), rows(w, c0, c0 + n))], ("mm_done", last_g + 1))

        plan = {}

        def tile_plan(g, c, n, col, width=P, a=0):
            v = cols_of(c % NSLOT, a, KD, n)
            plan[g] = (c, lambda k, v=v, col=col, width=width: v[:, k, col:col + width])

        wi = w_in_e[0]
        c = wide(wi, 28 * P, 8, G_IN0)
        tile_plan(G_IN0, c, 8, 0, 8)
        for j in range(7):
            g = G_IN0 + 1 + 4 * j
            c = wide(wi, E_TILE[g - G_IN0] * P, 512, g + 3)
            for i in range(4):
                tile_plan(g + i, c, 512, i * P)

        def out_chunks(base, parts_of):
            for j in range(2):
                g = base + 4 * j
                c = len(chunks)
                chunk(parts_of(c % NSLOT, 512 * j), ("mm_done", g + 4))
                for i in range(4):
                    tile_plan(g + i, c, 512, i * P)

        out_chunks(G_OUT0, lambda slot, c0: [(cols_of(slot, 0, KD, 512), rows(w_out_e[0], c0, c0 + 512))])

        def mlp_chunks(layer, up, dn):
            for j in range(KF // 4):
                c = wide(w_up[layer], 512 * j, 512, up + 4 * j + 3)
                for i in range(4):
                    tile_plan(up + 4 * j + i, c, 512, i * P)
            for j in range(KD // 2):
                cc = []
                for half in range(2):
                    src = w_down[layer][half * 2048:(half + 1) * 2048, 256 * j:256 * (j + 1)]
                    c = len(chunks)
                    freed = ("mm_half", layer * (KD // 2) + j + 1) if half == 0 else ("mm_done", dn + 2 * j + 2)
                    cc.append(chunk([(cols_of(c % NSLOT, 0, 16, 256), src.rearrange("(k p) n -> p k n", p=P))], freed))
                for i in range(2):
                    plan[dn + 2 * j + i] = (cc, i)

        mlp_chunks(0, G_UP0, G_DN0)

        wo = w_in_o[0]
        c = len(chunks)
        slot = c % NSLOT
        misc = cols_of(slot, 0, KD, 60 + P)
        chunk([(misc[:, :, 0:24], rows(wo, 1280, 1304)), (misc[:, :, 24:60], rows(wo, 2200, 2236))] +
              [(misc[:, :, 60 + 32 * e:92 + 32 * e], rows(wo, 2200, 2232)) for e in range(4)],
              ("mm_done", G_IN1 + 2))
        plan[G_IN1 + Z["misc"]] = (c, lambda k, v=misc: v[:, k, 0:60])
        plan[G_IN1 + Z["ki4"]] = (c, lambda k, v=misc: v[:, k, 60:60 + P])
        c = wide(wo, 1816, 384, G_IN1 + Z["qi"])
        for i, n in enumerate(("kd", "vd", "qi")):
            tile_plan(G_IN1 + Z[n], c, 384, i * P)

        def pair_tiles(c0, first):
            c = len(chunks)
            v = cols_of(c % NSLOT, 0, KD, 512)
            chunk([(v[:, :, P * p + HD * g:P * p + HD * g + HD], rows(wo, c0 + HD * (NP * g + p), c0 + HD * (NP * g + p + 1)))
                   for p in range(NP) for g in range(2)], ("mm_done", first + 4))
            for p in range(NP):
                tile_plan(first + p, c, 512, P * p)

        pair_tiles(1304, G_IN1 + Z["qd0"])
        c = wide(wo, 512, 512, G_IN1 + Z["vs"])
        for i, n in enumerate(("kc", "vc", "ks", "vs")):
            tile_plan(G_IN1 + Z[n], c, 512, i * P)
        c = wide(wo, 1024, 256, G_IN1 + Z["vw"])
        for i, n in enumerate(("kw", "vw")):
            tile_plan(G_IN1 + Z[n], c, 256, i * P)
        pair_tiles(0, G_IN1 + Z["qn0"])

        def out_rows(slot, c0):
            w = w_out_o[0].rearrange("(s g q d) n -> s g d q n", s=2, g=2, q=NP)
            v = cols_of(slot, 0, KD, 512)
            return [(v[HD * g:HD * (g + 1), NP * s:NP * (s + 1), :], w[s, g, :, :, c0:c0 + 512])
                    for s in range(2) for g in range(2)]

        out_chunks(G_OUT1, out_rows)
        mlp_chunks(1, G_UP1, G_DN1)

        loads = [0] * NSLOT
        chunk_value = []
        for c, (parts, _) in enumerate(chunks):
            loads[c % NSLOT] += 16 * len(parts)
            chunk_value.append(loads[c % NSLOT])

        block = ctx.enter_context(nc.Block())

        def chain(eng, s):
            n = [0]

            def link(ins):
                n[0] += 1
                ins.then_inc(s, 1)
                eng.wait_ge(s, n[0])
            return link

        sel = piece(MH * P).rearrange("p (h m) -> p h m", h=MH)
        D0 = piece(S)
        Dw = piece(3 * P)
        Ds = piece(LS)
        Dws = piece(LS)
        Dc = piece(QT * NB)
        Mc = piece(QT * NB)
        Dcs = piece(NBS)
        BS = piece(62)
        selB = piece(B * NH)
        selE = piece(B * 4)
        slopes = piece(NH)
        slope8 = piece(NH)
        wcK = piece(2 * P)
        wcT = piece(2 * BLK)
        pages = ctx.enter_context(nc.sbuf_tensor("pages", [1, NT], I32))
        base = taken[0]

        xp_stage = ymix[:, :, :].rearrange("p a b -> p (a b)")[:, 0:QT * D].rearrange("p (t d) -> p t d", t=QT)
        xs_stage = att[0:B, 0:D]
        stg = att[0:112, 1024:1152]
        scs = att[0:2 * B, 1152:1152 + 512]
        stm = piece(B)
        gbc = piece(1)

        Ct = cbuf[:, :].rearrange("p (b h d) -> p h b d", h=MH, b=B)
        gz = att[0:8, 1664:1664 + T]
        fgt = att[0:4, 2184:2184 + T]
        nx = att[0:4, 2704:2704 + T]
        lg = att[0:4, 3224:3224 + T]
        Fc = att[0:4, 3744:3744 + S]
        at_ = att[0:4, 4256:4256 + S]
        Mr = att[0:4, 4768:4768 + S]
        nG = att[0:4, 5280:5280 + S]
        rowsP = piece(2 * S)
        rowsS = piece(3 * B)
        eS = piece(3 * B)
        interS = piece(B)
        mtS = piece(B)
        mpc = piece(1)
        aT = piece(QT * MH)
        bcS = piece(MH * 3 * B)
        scT = piece(4 * 2 * B)
        prod = piece(2 * MH * B)
        dts = piece(2 * MH * B)
        nnw = piece(MH * B)
        vwS = piece(MH * B)
        swa = piece(MH * B)
        recS = piece(MH * B)
        cq = piece(MH * B)
        hS = piece(MH * B)
        wsc = piece(QT)
        nml = piece(1)
        nno = piece(P)
        uo = piece(512)
        cst = piece(P)
        nrow = piece(P)
        OFF = [0, 512, 896, 1152]
        Wt = att[:, 0:1280]
        Pt = att[:, 1280:2560]
        vtm = att[:, 2560:3072]
        ktm = att[:, 3072:3584]
        vw = att[:, 3584:4096]
        tmpS = att[:, 4096:5120].rearrange("p (b d) -> p b d", b=B)
        dn = att[:, 5120:5632]

        racc = att[:, 0:T]
        sacc = att[:, T:2 * T]
        sq = [att[:, (2 + i) * T:(3 + i) * T] for i in range(2)]
        mu = att[:, 4 * T:5 * T]
        rs = att[:, 5 * T:6 * T]
        relA = [att[:, 6 * T + i * H2:6 * T + (i + 1) * H2] for i in range(2)]
        relB = [att[:, 7 * T + i * H2:7 * T + (i + 1) * H2] for i in range(2)]
        var = att[:, 8 * T:9 * T]

        after0 = taken[0]
        taken[0] = base
        flat = big[:, :, :].rearrange("p a b -> p (a b)")
        o = len(O_NAMES) * T
        tm = flat[:, o:o + QT * 1024].rearrange("p (i c) -> p i c", i=QT)
        o += QT * 1024
        tms = flat[0:B, o:o + 1024]
        o += 1024
        TAB = [None, flat[:, o:o + 256], flat[:, o + 256:o + 640], flat[:, o + 640:o + 1152]]
        assert o + 1152 <= KF * T
        KZ = {n: att[:, 1024 * i:1024 * (i + 1)].rearrange("p (g k) -> p g k", g=2) for i, n in enumerate(("kd", "ks", "kw"))}
        kiz = att[:, 3072:3072 + 2048].rearrange("p (e k) -> p e k", e=4)
        rl = [att[:, 5120 + 512 * i:5632 + 512 * i] for i in range(2)]
        kTs = [att[:, 3072 + 2 * LS * i:3072 + 2 * LS * (i + 1)].rearrange("p (b k) -> p b k", b=2) for i in range(2)]
        o = 3072 + 4 * LS
        sbs = att[0:64, o:o + LS]
        iscS = att[0:B, o + LS:o + 2 * LS]
        rS = att[0:32, o + 2 * LS:o + 3 * LS]
        DdS = att[0:64, o + 3 * LS:o + 4 * LS]
        o += 4 * LS
        PTs = att[:, o:o + 128].rearrange("p (t c) -> p t c", t=2)
        QI = att[:, o + 128:o + 128 + 256]
        kidx = att[:, o + 384:o + 384 + 512].rearrange("p (t e) -> p t e", t=NT)
        assert o + 896 <= 6144, o
        QB = {"d": piece(512), "n": piece(512)}
        mtm = piece(QT * 60).rearrange("p (i c) -> p i c", i=QT)
        gt = piece(QT * 24).rearrange("p (i c) -> p i c", i=QT)
        mts = piece(60)
        gsel = piece(60)
        gS = piece(3)
        g24 = piece(24)
        mask64 = piece(NH)
        sl64 = piece(1)
        mask32 = piece(4)
        bsel32 = piece(B)
        wE = piece(4)
        wi32 = piece(1)
        WI = piece(B)
        ixE = piece(60)
        m8 = piece(8)
        m8s = piece(8)
        nmx = [piece(1) for _ in range(2)]
        rsum = [piece(1) for _ in range(2)]
        rrec = [piece(1) for _ in range(2)]
        nms, rss, rcs = piece(1), piece(1), piece(1)
        kcT = piece(NB)
        vcT = piece(NB)
        KCZ = piece(2 * NB)
        kcTs = piece(B * NBS)
        vals = piece(6 * B)
        cmps = piece(2 * P)
        sc4 = piece(NBS)
        oN = piece(B * NH)
        mixc = piece(P)
        oD = piece(B * NH)
        assert taken[0] <= SMALL
        VF = cbuf[:, 0:256].rearrange("p (q c) -> p q c", q=NP)
        VCb = cbuf[0:64, 256:768].rearrange("p (q c) -> p q c", q=NP)
        PcT = cbuf[0:64, 768:1280]
        sc = cbuf[:, 1280:1536]
        sD = cbuf[:, 1536:1792]
        mxc = cbuf[:, 1792:1824]
        rcc = cbuf[:, 1824:1856]
        pbt = cbuf[:, 1856:2240]
        tmpc = cbuf[:, 2240:2752]
        Pb = [att[:, 3072 + 512 * i:3584 + 512 * i] for i in range(2)]
        PTb = [att[:, 4096 + 512 * i:4608 + 512 * i] for i in range(2)]
        sbb = [att[:, 5120 + 512 * i:5632 + 512 * i] for i in range(2)]
        cache = {"c": cbuf[:, :].rearrange("p (t x) -> p t x", t=NT),
                 "y": ymix[:, :, :].rearrange("p a b -> p (a b)")[:, 0:4096].rearrange("p (t x) -> p t x", t=NT)}
        BR = [("d", "y", "d", "kd", "vd"), ("c", "c", "n", "kc", "vc"), ("s", "y", "n", "ks", "vs"), ("w", "c", "n", "kw", "vw")]

        units = []
        for i in range(QT):
            for p in range(NP):
                for br in ("s", "w"):
                    for g in range(2):
                        units.append((i, p, g, br, 0 if br == "s" else max(0, i - 2), i * NP + p))
        for i in range(QT):
            for p in range(NP):
                for g in range(2):
                    units.append((i, p, g, "d", 0, (QT + i) * NP + p))
        first_of = {}
        last_of = {}
        for u, x in enumerate(units):
            first_of.setdefault((x[5], x[2]), u)
            last_of[x[5]] = u

        cm = mixc
        ytm = flat[:, 0:5 * D].rearrange("p (i d) -> p i d", i=5)

        def psA(g):
            return ps[2 * (g % 2)]

        def psB(g):
            return ps[2 * (g % 2) + 1]

        @block.sync
        def _(sp):
            sp.dma_start(xp_stage, x_prompt[0].rearrange("(t p) d -> p t d", p=P)).then_inc(sm["x_in"], 16)
            sp.dma_start(xs_stage, x_sample.rearrange("b o d -> (b o) d")).then_inc(sm["x_in"], 16)
            sp.dma_start(stg[0:32, :], ln_g.rearrange("l s (k d) -> (l s k) d", d=P)).then_inc(sm["cols_in"], 16)
            sp.dma_start(stg[32:64, :], ln_b.rearrange("l s (k d) -> (l s k) d", d=P)).then_inc(sm["cols_in"], 16)
            sp.dma_start(stg[64:76, :], conv_w.rearrange("o j (c d) -> (o j c) d", d=P)).then_inc(sm["cols_in"], 16)
            sp.dma_start(stg[76:80, :], conv_b.rearrange("o (c d) -> (o c) d", d=P)).then_inc(sm["cols_in"], 16)
            sp.dma_start(stg[80:112, :], state_n.rearrange("o b h d -> (o b h) d")).then_inc(sm["cols_in"], 16)
            sp.dma_start(scs, state_conv.rearrange("o b j c -> (o b j) c")).then_inc(sm["scs_in"], 16)
            for c, (parts, _) in enumerate(chunks):
                if c >= NSLOT:
                    s, v = chunks[c - NSLOT][1]
                    sp.wait_ge(sm[s], v)
                for dst, src in parts:
                    sp.dma_start(dst, src).then_inc(w_sem[c % NSLOT], 16)
                if c == 1:
                    for h in range(MH):
                        sp.dma_start(Ct[:, h, :, :], state_C[0, :, h].rearrange("b e d -> e b d")).then_inc(sm["c_in"], 16)

        @block.gpsimd
        def _(pool):
            link = chain(pool, sm["pool_step"])
            pool.dma_start(stm[0:MH, :], state_m[0].rearrange("b h -> h b"), allow_slow_non_contiguous=True).then_inc(sm["small_in"], 16)
            pool.dma_start(gbc[0:8, :], gate_b_e.rearrange("o c -> c o"), allow_slow_non_contiguous=True).then_inc(sm["small_in"], 16)
            pool.dma_start(pages[0:1, :], page_table.rearrange("(o b) t -> o (b t)", o=1)).then_inc(sm["page_in"], 16)
            for half in range(2):
                for s in range(2):
                    for g in range(2):
                        pool.dma_start(wcK[64 * half:64 * half + 64, P * s + HD * g:P * s + HD * g + HD],
                                       w_cmp[0, s]).then_inc(sm["small_in"], 16)
            link(pool.memset(ident[:, :], 0.0))
            pool.affine_select(out=ident[:, :], in_=ident[:, :], compare_op=ALU.not_equal, fill=1.0, base=0,
                               pattern=[[-1, P]], channel_multiplier=1).then_inc(sm["consts_ok"], 1)
            pool.memset(ones[:, :], 1.0)
            pool.memset(meanM[:, :], 1.0 / D).then_inc(sm["consts_ok"], 1)
            link(pool.memset(sel[:, :, :], 0.0))
            pool.affine_select(out=sel[:, :, :], in_=sel[:, :, :], compare_op=ALU.not_equal, fill=1.0, base=0,
                               pattern=[[-1, MH], [0, P]], channel_multiplier=1)
            link(pool.iota(D0, pattern=[[1, S]], base=-(S - P), channel_multiplier=-1, allow_small_or_imprecise_dtypes=True))
            link(pool.affine_select(out=D0, in_=D0, compare_op=ALU.is_ge, fill=NEG, base=S - P,
                                    pattern=[[-1, S]], channel_multiplier=1))
            pool.affine_select(out=Dw, in_=D0[:, P:S], compare_op=ALU.is_gt, fill=NEG, base=0,
                               pattern=[[1, 3 * P]], channel_multiplier=-1)
            pool.iota(Ds, pattern=[[1, LS]], base=-PAST, channel_multiplier=0, allow_small_or_imprecise_dtypes=True)
            link(pool.iota(Dws, pattern=[[1, LS]], base=-PAST, channel_multiplier=0, allow_small_or_imprecise_dtypes=True))
            pool.memset(Dws[:, 0:1], NEG)
            link(pool.iota(Dc.rearrange("p (i j) -> p i j", i=QT), pattern=[[-P, QT], [BLK, NB]], base=BLK - 1,
                           channel_multiplier=-1, allow_small_or_imprecise_dtypes=True))
            pool.affine_select(out=Dc.rearrange("p (i j) -> p i j", i=QT), in_=Dc.rearrange("p (i j) -> p i j", i=QT),
                               compare_op=ALU.is_ge, fill=NEG, base=-(BLK - 1), pattern=[[P, QT], [-BLK, NB]],
                               channel_multiplier=1)
            pool.iota(Dcs, pattern=[[BLK, NBS]], base=BLK - 1 - PAST, channel_multiplier=0,
                      allow_small_or_imprecise_dtypes=True)
            link(pool.memset(BS, 0.0))
            link(pool.memset(BS[0:64, 30:31], 1.0))
            link(pool.memset(BS[64:128, 31:32], 1.0))
            link(pool.memset(selB, 0.0))
            pool.affine_select(out=selB.rearrange("p (b h) -> p b h", b=B), in_=selB.rearrange("p (b h) -> p b h", b=B),
                               compare_op=ALU.not_equal, fill=1.0, base=0, pattern=[[-1, B], [0, NH]], channel_multiplier=1)
            link(pool.memset(selE, 0.0))
            pool.affine_select(out=selE.rearrange("p (b h) -> p b h", b=B), in_=selE.rearrange("p (b h) -> p b h", b=B),
                               compare_op=ALU.not_equal, fill=1.0, base=0, pattern=[[-1, B], [0, 4]], channel_multiplier=1)
            for h in range(NH):
                g, p = divmod(h, NP)
                pool.memset(slopes[:, 2 * p + g:2 * p + g + 1], SLOPE[h])
                last = pool.memset(slope8[:, h:h + 1], SLOPE[h])
            last.then_inc(sm["consts_ok"], 1)

            def sums(n_ln, g0):
                for m in range(KD):
                    pool.wait_ge(sm["free_a"], g0 + m + 1)
                    pool.wait_ge(sm["free_b"], g0 + m + 1)
                    if m == 0:
                        link(pool.tensor_copy(racc, xT[:, 0, :]))
                    else:
                        link(pool.tensor_tensor(racc, racc, xT[:, m, :], ALU.add))
                    pool.wait_ge(sm["sq_done"], KD * n_ln + m + 1)
                    last = (pool.tensor_copy(sacc, sq[0]) if m == 0
                            else pool.tensor_tensor(sacc, sacc, sq[m % 2], ALU.add))
                    last.then_inc(sm["sum_r"], 1)
                    pool.wait_ge(sm["sum_r"], KD * n_ln + m + 1)
                pool.wait_ge(sm["std_ok"], n_ln + 1)
                for n, m in enumerate(LN_POOL):
                    link(pool.tensor_tensor(xT[:, m, :], xT[:, m, :], mu, ALU.subtract))
                    pool.tensor_tensor(xT[:, m, :], xT[:, m, :], rs, ALU.mult).then_inc(sm["cen_p"], 1)

            for i in range(4):
                g = G_IN0 + 17 + i
                pool.wait_ge(sm["free_a"], g + 1)
                pool.wait_ge(sm["free_b"], g + 1)
                pool.tensor_tensor(big[:, i, :], big[:, i, :], big[:, 8 + i, :], ALU.mult).then_inc(sm["u_ok"], 1)
            pool.wait_ge(sm["sp_ok"], 1)
            pool.dma_start(m_p.rearrange("o b h -> h (o b)"), mpc[0:MH, :], allow_slow_non_contiguous=True).then_inc(sm["outs"], 16)
            pool.dma_start(m_s[0].rearrange("b h -> h b"), mtS[0:MH, :], allow_slow_non_contiguous=True).then_inc(sm["outs"], 16)
            for h in range(MH):
                pool.wait_ge(sm["c_new"], h + 1)
                pool.dma_start(c_s[0, :, h].rearrange("b e d -> e b d"), Ct[:, h, :, :]).then_inc(sm["store_c"], 16)
            pool.wait_ge(sm["nnew_ev"], 1)
            pool.dma_start(n_s.rearrange("o b h d -> (o b h) d"), nno[0:MH * B, :]).then_inc(sm["outs"], 16)
            pool.wait_ge(sm["ucol_ev"], 1)
            pool.dma_start(conv_p.rearrange("o b j c -> (o b j) c"), uo[0:2, :]).then_inc(sm["outs"], 16)
            pool.dma_start(conv_s[0, :, 1, :], uo[2:2 + B, :]).then_inc(sm["outs"], 16)
            pool.dma_start(conv_s[0, :, 0, :], state_conv[0, :, 1, :]).then_inc(sm["outs"], 16)
            for h in range(MH):
                for i in range(QT):
                    pool.wait_ge(sm["p_raw"], QT * h + i + 1)
                    d = Pt[:, OFF[i]:OFF[i] + P]
                    pool.affine_select(out=d, in_=d, compare_op=ALU.is_ge, fill=0.0, base=0, pattern=[[1, P]],
                                       channel_multiplier=-1).then_inc(sm["p_ok"], 1)
                pool.wait_ge(sm["cn_ev"], 2 * h + 2)
                pool.dma_start(c_p[0, 0, h], cst).then_inc(sm["store_c"], 16)
                pool.dma_start(n_p[0, :, h, :], nrow[0:1, :]).then_inc(sm["store_c"], 16)
            sums(0, G_OUT0)
            sums(1, G_DN0)

            pool.wait_ge(sm["cen_v"], 2 * (KD - len(LN_POOL)))
            pool.wait_ge(sm["x_ready"], 2 * KD)
            pool.memset(kiz[:, :, :], 0.0)
            last = pool.memset(att[:, 0:3072], 0.0)
            last.then_inc(sm["z_pool"], 1)
            pool.wait_ge(sm["z_pool"], 1)

            def tile_ready(name):
                pool.wait_ge(sm["free_a"], G_IN1 + Z[name] + 1)
                pool.wait_ge(sm["free_b"], G_IN1 + Z[name] + 1)

            tile_ready("ki4")
            for e in range(4):
                pool.tensor_copy(kiz[32 * e:32 * e + 32, e, :], big[32 * e:32 * e + 32, Z["ki4"], 0:S]).then_inc(sm["kiz_ok"], 1)
                pool.wait_ge(sm["kiz_ok"], e + 1)
            pool.wait_ge(sm["page_in"], 16)

            def gather(n, src_of, dst):
                for t in range(NT):
                    r = pool.value_load(pages[0:1, t:t + 1], min_val=0, max_val=cache_kv.shape[1] - 1)
                    pool.dma_start(dst[:, t, :], src_of(r)).then_inc(gat[n], 16)

            kv_rows = cache_kv[0].rearrange("n p s g d -> n p (s g d)")

            def kv_page(c0):
                return lambda r: kv_rows[bass.ds(r, 1), :, c0:c0 + 256].rearrange("n p x -> p (n x)")

            pool.wait_ge(sm["mm_done"], G_OUT0 + KD)
            pool.wait_ge(sm["store_c"], 16 * 3 * MH)
            gather(0, kv_page(4 * P), cache["y"])
            gather(1, kv_page(0), cache["c"])
            pool.wait_ge(gat[1], 16 * NT)
            for t in range(NT):
                last = pool.tensor_tensor(cache["c"][:, t, :], cache["c"][:, t, :], wcK, ALU.mult)
            last.then_inc(sm["cw_ok"], 1)
            pool.wait_ge(sm["cw_ok"], 1)
            for n, name in enumerate(("kd", "ks", "kw")):
                tile_ready(name)
                for g in range(2):
                    pool.tensor_copy(KZ[name][HD * g:HD * g + HD, g, :],
                                     big[HD * g:HD * g + HD, Z[name], 0:S]).then_inc(sm["kz_ok"], 1)
                    pool.wait_ge(sm["kz_ok"], 2 * n + g + 1)
            pool.wait_ge(sm["isc_used"], 12)
            gather(4, lambda r: cache_idx[0][bass.ds(r, 1), :, :].rearrange("n p e -> p (n e)"), kidx)
            pool.wait_ge(sm["pvs_mm"], 1)
            gather(2, kv_page(2 * P), cache["y"])
            pool.wait_ge(sm["cmp_mm"], 1)
            pool.dma_start(cache["c"], cache_win[0].rearrange("b (t p) s g d -> p (b t) (s g d)", p=P)).then_inc(gat[3], 16)
            pool.wait_ge(sm["tm_a"], 4)
            pool.wait_ge(sm["tm_b"], 4)
            pool.dma_start(kv_p[0, 0].rearrange("(i p) s g d -> p i (s g d)", p=P), tm[:, :, 0:768]).then_inc(sm["outs"], 16)
            pool.dma_start(win_p[0, 0].rearrange("(i p) s g d -> p i (s g d)", p=P), tm[:, 2:4, 768:1024]).then_inc(sm["outs"], 16)
            pool.wait_ge(sm["tms_ev"], 2)
            pool.dma_start(kv_s[0].rearrange("b t s g d -> (b t) (s g d)"), tms[:, 0:768]).then_inc(sm["outs"], 16)
            pool.dma_start(win_s[0, :, PAST - 1].rearrange("b s g d -> b (s g d)"), tms[:, 768:1024]).then_inc(sm["outs"], 16)
            pool.dma_start(win_s[0, :, 0:PAST - 1].rearrange("b t s g d -> b t (s g d)"),
                           cache_win[0, :, 1:PAST].rearrange("b t s g d -> b t (s g d)")).then_inc(sm["outs"], 16)
            pool.dma_start(idx_p[0, 0].rearrange("(i p) e -> p i e", p=P), mtm[:, :, 24:56]).then_inc(sm["outs"], 16)
            pool.dma_start(idx_s[0].rearrange("b t e -> (b t) e"), mts[0:B, 24:56]).then_inc(sm["outs"], 16)
            pool.wait_ge(sm["outs"], 16 * 13)
            sums(2, G_OUT1)
            sums(3, G_DN1)
            for i in range(QT):
                pool.wait_ge(sm["y_a"], i + 1)
                pool.wait_ge(sm["y_b"], i + 1)
                pool.dma_start(y_p[0, P * i:P * (i + 1), :], ytm[:, i, :]).then_inc(sm["outs"], 16)
            pool.wait_ge(sm["y_a"], QT + 1)
            pool.wait_ge(sm["y_b"], QT + 1)
            pool.dma_start(y_s.rearrange("b o d -> (b o) d"), ytm[0:B, QT, :]).then_inc(sm["outs"], 16)
            pool.wait_ge(sm["outs"], 16 * 18)
            pool.wait_ge(sm["store_c"], 16 * 3 * MH)

        @block.tensor
        def _(pe):
            def tr(out, in_, n):
                return pe.matmul(out, in_, ident[0:n, 0:n], start=True, stop=True, is_transpose=True,
                                 skip_group_check=True)

            def mm(out, lhsT, rhs, start=True, stop=True):
                return pe.matmul(out, lhsT, rhs, start=start, stop=stop, skip_group_check=True)

            loaded = [-1]

            def chunk_here(c):
                if c > loaded[0]:
                    pe.wait_ge(w_sem[c % NSLOT], chunk_value[c])
                    loaded[0] = c

            def banks_free(g):
                if g >= 2:
                    pe.wait_ge(sm["free_a"], g - 1)
                    pe.wait_ge(sm["free_b"], g - 1)

            def tile(g, rhs, m, ready=None):
                c, lhsT = plan[g]
                banks_free(g)
                chunk_here(c)
                for k in range(KD):
                    if ready:
                        ready(k)
                    for half, bank in ((0, psA(g)), (1, psB(g))):
                        last = pe.matmul(bank[0:m, 0:H2], lhsT(k), rhs[:, k, half * H2:(half + 1) * H2],
                                         start=(k == 0), stop=(k == KD - 1))
                last.then_inc(sm["mm_done"], 1)

            def x_here(n_ln):
                return lambda k: pe.wait_ge(sm["x_ready"], KD * n_ln + k + 1)

            def mlp_up(g0, n_ln):
                for j in range(KF):
                    tile(g0 + j, xT, P, x_here(n_ln) if j == 0 else None)

            def mlp_down(layer, g0):
                for j in range(KD // 2):
                    for half in range(2):
                        for i in range(2):
                            g = g0 + 2 * j + i
                            (cs, col) = plan[g]
                            if half == 0:
                                banks_free(g)
                            chunk_here(cs[half])
                            w = cols_of(cs[half] % NSLOT, 0, 16, 256)
                            for k in range(16):
                                kk = 16 * half + k
                                if j == 0 and i == 0:
                                    pe.wait_ge(sm["hid_a"], KF * layer + kk + 1)
                                    pe.wait_ge(sm["hid_b"], KF * layer + kk + 1)
                                for hf, bank in ((0, psA(g)), (1, psB(g))):
                                    last = pe.matmul(bank[:, 0:H2], w[:, k, P * col:P * col + P],
                                                     big[:, kk, hf * H2:(hf + 1) * H2],
                                                     start=(kk == 0), stop=(kk == KF - 1))
                            if half == 1:
                                last.then_inc(sm["mm_done"], 1)
                        if half == 0:
                            last.then_inc(sm["mm_half"], 1)

            def norm_sums(n_ln):
                pe.wait_ge(sm["sum_r"], KD * (n_ln + 1))
                for n, src in ((4, racc), (6, sacc)):
                    for half in range(2):
                        last = mm(ps[n + half][:, 0:H2], meanM[:, :], src[:, half * H2:(half + 1) * H2])
                last.then_inc(sm["stats_mm"], 1)

            pe.wait_ge(sm["consts_ok"], 3)
            pe.wait_ge(sm["x_in"], 32)
            for k in range(KD):
                if k >= 6:
                    pe.wait_ge(sm["tin_a"] if k % 2 == 0 else sm["tin_b"], (k - 6) // 2 + 1)
                for t in range(QT):
                    last = tr(ps[k % 6][:, P * t:P * t + P], xp_stage[:, t, P * k:P * k + P], P)
                last.then_inc(sm["tin"], 1)
            for k in range(KD):
                last = tr(ps[6][:, B * k:B * k + B], xs_stage[:, P * k:P * k + P], B)
            last.then_inc(sm["tin"], 1)
            pe.wait_ge(sm["cols_in"], 80)
            tr(ps[7][:, 0:112], stg, 112)
            pe.wait_ge(sm["small_in"], 16 * 10)
            for s in range(2):
                last = tr(ps[7][:, 112 + BLK * s:112 + BLK * (s + 1)], wcK[0:64, P * s:P * s + P], 64)
            last.then_inc(sm["tin"], 1)
            pe.wait_ge(sm["tin_a"], KD // 2)
            pe.wait_ge(sm["tin_b"], KD // 2 + 2)

            for idx in range(len(E_TILE)):
                tile(G_IN0 + idx, xT, 8 if idx == 0 else P)
                if idx == 2:
                    pe.wait_ge(sm["free_a"], 1)
                    pe.wait_ge(sm["free_b"], 1)
                    for half in range(2):
                        last = mm(ps[4 + half][0:4, 0:H2], ident[0:8, 4:8], gz[:, half * H2:(half + 1) * H2])
                    last.then_inc(sm["fg_mm"], 1)
                if idx == 12:
                    pe.wait_ge(sm["scs_in"], 16)
                    pe.wait_ge(sm["rows_ok"], 1)
                    for i in range(QT):
                        tr(ps[4][:, MH * i:MH * i + MH], at_[:, P * i:P * i + P], MH)
                    for h in range(MH):
                        mm(ps[5][:, 24 * h:24 * h + 24], sel[0:MH, h, :], eS[0:MH, :])
                    for i in range(4):
                        last = tr(ps[7][:, 16 * i:16 * i + 16], scs[:, P * i:P * i + P], 2 * B)
                    last.then_inc(sm["h12_mm"], 1)
                if idx == 14:
                    pe.wait_ge(sm["prod_ok"], 1)
                    mm(ps[4][:, 0:64], ones[:, :], prod).then_inc(sm["dots_mm"], 1)
                if idx in (16, 18, 20, 22):
                    h = (idx - 16) // 2
                    if h == 0:
                        pe.wait_ge(sm["nnew_ok"], 1)
                    else:
                        pe.wait_ge(sm["head_used"], h)
                    for n, t0 in ((4, 12), (6, 16)):
                        for b in range(B):
                            last = mm(ps[n + b // 4][:, P * (b % 4):P * (b % 4) + P],
                                      big[:, t0 + h, S + b:S + b + 1].to_broadcast([P, P]), ident[:, :])
                    last.then_inc(sm["head_mm"], 1)
                if idx == 25:
                    pe.wait_ge(sm["head_used"], MH)
                    tr(ps[4][0:MH * B, 0:P], nnw, P).then_inc(sm["nnew_mm"], 1)
                    pe.wait_ge(sm["u_ok"], 4)
                    for i in range(4):
                        last = tr(ps[5][0:B + 2, P * i:P * i + P], big[:, i, S - 2:T], P)
                    last.then_inc(sm["ucol_mm"], 1)

            pe.wait_ge(sm["free_a"], G_OUT0)
            pe.wait_ge(sm["free_b"], G_OUT0)
            pe.wait_ge(sm["nnew_ev"], 1)
            pe.wait_ge(sm["ucol_ev"], 1)
            pe.wait_ge(sm["c_new"], MH)
            for h in range(MH):
                if h:
                    pe.wait_ge(sm["wt_ok"], QT * h)
                mm(ps[0][:, :], sel[0:MH, h, :], rowsP[0:MH, 0:S]).then_inc(sm["pre_mm"], 1)
                if h:
                    pe.wait_ge(sm["hd_fin"], h)
                mm(ps[1][:, :], sel[0:MH, h, :], rowsP[0:MH, S:2 * S]).then_inc(sm["pre_mm"], 1)
                if h:
                    pe.wait_ge(sm["vt_ok"], h)
                    pe.wait_ge(sm["kt_ok"], h)
                for n, t0 in ((2, 20), (3, 16)):
                    for i in range(QT):
                        last = tr(ps[n][:, P * i:P * i + P], big[:, t0 + h, P * i:P * i + P], P)
                    last.then_inc(sm["pre_mm"], 1)
                if h:
                    pe.wait_ge(sm["cn_ev"], 2 * h)
                for i in range(QT + 1):
                    if i < QT:
                        if i >= 2:
                            pe.wait_ge(sm["p_raw"], QT * h + i - 1)
                        mm(ps[4 + i % 2][:, 0:S - P * i], big[:, 16 + h, P * i:P * i + P],
                           big[:, 12 + h, P * i:S]).then_inc(sm["s_mm"], 1)
                    if i >= 1:
                        j = i - 1
                        pe.wait_ge(sm["p_ok"], QT * h + j + 1)
                        if j == 0:
                            pe.wait_ge(sm["vt_ok"], h + 1)
                        pp = Pt[:, OFF[j]:OFF[j] + S - P * j]
                        mm(ps[6][:, P * j:S], ones[:, :], pp, start=(j == 0), stop=(j == QT - 1))
                        mm(ps[7][:, P * j:S], vtm[:, P * j:P * j + P], pp, start=(j == 0),
                           stop=(j == QT - 1)).then_inc(sm["pv_mm"], 1)
                pe.wait_ge(sm["vw_ok"], h + 1)
                pe.wait_ge(sm["kt_ok"], h + 1)
                for j in range(QT):
                    last = mm(ps[4][:, 0:P], vw[:, P * j:P * j + P], ktm[:, P * j:P * j + P], start=(j == 0),
                              stop=(j == QT - 1))
                last.then_inc(sm["cn_mm"], 1)
                for j in range(QT):
                    last = mm(ps[5][0:1, 0:P], wsc[:, j:j + 1], ktm[:, P * j:P * j + P], start=(j == 0),
                              stop=(j == QT - 1))
                last.then_inc(sm["cn_mm"], 1)

            def conv_here(k):
                if k < 4:
                    pe.wait_ge(sm["conv_ok"], k + 1)
                else:
                    pe.wait_ge(sm["hd_fin"], k - 3)
                    if k == 4:
                        pe.wait_ge(sm["smp_y"], 1)

            for j in range(KD):
                tile(G_OUT0 + j, ymix, P, conv_here if j == 0 else None)
            pe.wait_ge(sm["cn_ev"], 2 * MH)
            norm_sums(0)
            mlp_up(G_UP0, 0)
            mlp_down(0, G_DN0)
            norm_sums(1)

            for idx, name in enumerate(O_NAMES):
                tile(G_IN1 + idx, xT, 60 if name == "misc" else P, x_here(1) if idx == 0 else None)
                if 4 <= idx <= 6:
                    n = idx - 4
                    i = 3 - n
                    g = G_IN1 + Z["qi"]
                    pe.wait_ge(sm["free_a"], g + 1)
                    pe.wait_ge(sm["free_b"], g + 1)
                    pe.wait_ge(sm["kiz_ok"], 4)
                    for e in range(4):
                        if n:
                            pe.wait_ge(sm["isc_r"], 4 * (n - 1) + e + 1)
                        mm(ps[4 + e][:, 0:P * (i + 1)], big[:, Z["qi"], P * i:P * i + P],
                           kiz[:, e, 0:P * (i + 1)]).then_inc(sm["isc_mm"], 1)
                if idx == 3:
                    pe.wait_ge(sm["free_a"], G_IN1 + 1)
                    pe.wait_ge(sm["free_b"], G_IN1 + 1)
                    for i in range(QT):
                        tr(ps[4][:, 60 * i:60 * i + 60], big[0:60, Z["misc"], P * i:P * i + P], 60)
                    tr(ps[5][0:B, 0:60], big[0:60, Z["misc"], S:T], 60).then_inc(sm["t1_mm"], 1)
                    pe.wait_ge(sm["t1_ev"], 1)
                    mm(ps[6][0:64, 0:60], selB[0:B, :], mts[0:B, :])
                    mm(ps[7][0:32, 0:60], selE[0:B, :], mts[0:B, :]).then_inc(sm["sel_mm"], 1)
                    pe.wait_ge(sm["sel_ev"], 1)

            pe.wait_ge(sm["free_a"], G_OUT1)
            pe.wait_ge(sm["free_b"], G_OUT1)
            pe.wait_ge(sm["isc_r"], 12)
            for s, name in enumerate(SLOTS):
                if s >= 4:
                    pe.wait_ge(sm["tm_a"] if s % 2 == 0 else sm["tm_b"], (s - 4) // 2 + 1)
                for i in range(QT):
                    last = tr(ps[s % 4][:, P * i:P * i + P], big[:, Z[name], P * i:P * i + P], P)
                last.then_inc(sm["tm_mm"], 1)
            for s, name in enumerate(SLOTS):
                last = tr(ps[4 + s // 4][0:B, P * (s % 4):P * (s % 4) + P], big[:, Z[name], S:T], P)
            last.then_inc(sm["tms_mm"], 1)
            pe.wait_ge(sm["tm_a"], 4)
            pe.wait_ge(sm["tm_b"], 4)
            pe.wait_ge(sm["tms_ev"], 2)

            def cached_keys(lhs_of, src_of, key_rows, acc_rows, step0):
                for st in range(4):
                    if st >= 2:
                        pe.wait_ge(sm["bt_ev"], step0 + st - 1)
                    for b in range(2):
                        for t in range(2):
                            last = tr(ps[4 + st % 2][0:key_rows, 256 * b + P * t:256 * b + P * t + P],
                                      src_of(2 * (2 * st + b) + t), P)
                    last.then_inc(sm["bt_mm"], 1)
                    if st >= 1:
                        scores(lhs_of, key_rows, acc_rows, step0, st - 1)
                scores(lhs_of, key_rows, acc_rows, step0, 3)

            def scores(lhs_of, key_rows, acc_rows, step0, st):
                pe.wait_ge(sm["bt_ev"], step0 + st + 1)
                for b in range(2):
                    bb = 2 * st + b
                    last = mm(ps[6][0:acc_rows, 0:LS], lhs_of(bb), kTs[st % 2][0:key_rows, b, :], start=(bb == 0), stop=(bb == B - 1))
                last.then_inc(sm["bs_mm"], 1)

            pe.wait_ge(gat[4], 16 * NT)
            pe.wait_ge(sm["qb_ok"], 1)
            cached_keys(lambda b: QI[0:32, 32 * b:32 * b + 32], lambda t: kidx[:, t, :], 32, 32, 0)
            pe.wait_ge(sm["ix_r"], 1)
            mm(ps[7][0:B, 0:LS], WI[0:32, :], rS).then_inc(sm["ixc_mm"], 1)
            pe.wait_ge(sm["dsb_in"], 1)
            mm(ps[7][0:64, 0:LS], selB[0:B, :], iscS).then_inc(sm["dsb_mm"], 1)

            def new_col(j, col):
                return mm(ps[2][:, 64 * j:64 * j + 64], col.to_broadcast([64, P]), ident[0:64, 0:64])

            for n, (br, where, q, kn, vn) in enumerate(BR):
                pe.wait_ge(gat[n], 16 if br == "w" else 16 * NT)
                if br == "c":
                    pe.wait_ge(sm["cw_ok"], 1)
                    for t in range(NT):
                        last = mm(ps[3][0:32, 0:256], BS[:, 30 - 2 * t:62 - 2 * t], cache["c"][:, t, :],
                                  start=(t == 0), stop=(t == NT - 1))
                    last.then_inc(sm["cmp_mm"], 1)
                    pe.wait_ge(sm["cmp_ev"], 1)
                    for s in range(2):
                        last = tr(ps[3][:, 256 + 32 * s:288 + 32 * s], cmps[0:32, P * s:P * s + P], 32)
                    last.then_inc(sm["cmpt_mm"], 1)
                    pe.wait_ge(sm["cmpt_ev"], 1)
                    pe.wait_ge(sm["qb_ok"], 3)
                    for b in range(B):
                        last = mm(ps[6][0:64, 0:NBS], QB["n"][:, 64 * b:64 * b + 64], kcTs[:, NBS * b:NBS * (b + 1)],
                                  start=(b == 0), stop=(b == B - 1))
                    last.then_inc(sm["bs_mm"], 1)
                    pe.wait_ge(sm["pn_ok"], 2)
                    for j in range(NBS):
                        last = new_col(j, sc4[0:64, j:j + 1])
                    last.then_inc(sm["pb_mm"], 1)
                    continue
                cb = cache[where]
                if br == "d":
                    pe.wait_ge(sm["qb_ok"], 2)
                step0 = {"d": 4, "s": 8, "w": 12}[br]
                cached_keys(lambda b, q=q: QB[q][:, 64 * b:64 * b + 64], lambda t, cb=cb: cb[:, t, 0:P], P, 64, step0)
                pe.wait_ge(sm["pn_ok"], n + 1)
                for t in range(2):
                    tr(ps[7][:, 64 * t:64 * t + 64], sbs[:, P * t:P * t + P], 64)
                new_col({"s": 4, "w": 5, "d": 6}[br], sbs[:, PAST:LS]).then_inc(sm["pt_mm"], 1)
                pe.wait_ge(sm["pt_ev"], {"d": 1, "s": 2, "w": 3}[br])
                acc = ps[1] if br == "d" else ps[0]
                for b in range(B):
                    for t in range(2):
                        last = mm(acc[:, 8 * b:8 * b + 8], cb[:, 2 * b + t, P:2 * P], PTs[:, t, 8 * b:8 * b + 8],
                                  start=(b == 0 and t == 0 and br != "w"), stop=True)
                last.then_inc(sm["pvs_mm"], 1)
            pe.wait_ge(sm["os_ok"], 2)

            pe.wait_ge(sm["kc_ok"], 1)
            for i in range(QT):
                for p in range(NP):
                    last = mm(ps[7][:, 64 * i + 16 * p:64 * i + 16 * p + 16], big[:, Z["qn0"] + p, P * i:P * i + P], KCZ)
            last.then_inc(sm["pc_mm"], 1)
            for p in range(NP):
                last = tr(ps[4][0:64, P * p:P * p + P], VF[:, p, :], P)
            last.then_inc(sm["vf_mm"], 1)
            pe.wait_ge(sm["pc_n"], 1)
            for i in range(QT):
                last = tr(ps[5][0:64, P * i:P * i + P], sc[:, 64 * i:64 * i + 64], P)
            last.then_inc(sm["pct_mm"], 1)
            pe.wait_ge(sm["pct_ev"], 1)
            pe.wait_ge(sm["vf_ev"], 1)

            VS = {"s": SLOTS.index("vs"), "w": SLOTS.index("vw"), "d": SLOTS.index("vd")}
            for t in range(len(units) + 3):
                if t < len(units):
                    i, p, g, br, k0, o = units[t]
                    if t >= 2:
                        pe.wait_ge(sm["q_sc"], t - 1)
                    if t == 0:
                        pe.wait_ge(sm["kz_ok"], 6)
                    qn = "qd0" if br == "d" else "qn0"
                    mm(ps[t % 2][:, 0:P * (i + 1 - k0)], big[:, Z[qn] + p, P * i:P * i + P],
                       KZ["k" + br][:, g, P * k0:P * (i + 1)]).then_inc(sm["q_mm"], 1)
                u = t - 2
                if 0 <= u < len(units):
                    i, p, g, br, k0, o = units[u]
                    pe.wait_ge(sm["q_n"], u + 1)
                    if u >= 2:
                        pe.wait_ge(sm["q_te"], u - 1)
                    for b in range(i + 1 - k0):
                        last = tr(ps[2 + u % 2][:, P * b:P * b + P], Pb[u % 2][:, P * b:P * b + P], P)
                    last.then_inc(sm["q_t"], 1)
                u = t - 3
                if 0 <= u < len(units):
                    i, p, g, br, k0, o = units[u]
                    acc = ps[5 + o % 2]
                    if u == first_of[(o, 0)]:
                        if o >= 2:
                            pe.wait_ge(sm["q_of"], o - 1)
                        if br != "d":
                            mm(acc[:, 0:P], VCb[:, p, :], PcT[:, P * i:P * i + P], stop=False)
                    pe.wait_ge(sm["q_te"], u + 1)
                    for b in range(i + 1 - k0):
                        v = tm[:, k0 + b, P * VS[br] + HD * g:P * VS[br] + HD * g + HD]
                        last = mm(acc[HD * g:HD * g + HD, 0:P], v, PTb[u % 2][:, P * b:P * b + P],
                                  start=(br == "d" and b == 0), stop=(b == i - k0))
                    last.then_inc(sm["q_o"], 1)

            def attended(k):
                pe.wait_ge(sm["q_of"], 16 if k < NP else 32)

            for j in range(KD):
                tile(G_OUT1 + j, ymix, P, attended if j == 0 else None)
            norm_sums(2)
            mlp_up(G_UP1, 2)
            mlp_down(1, G_DN1)
            norm_sums(3)

            pe.wait_ge(sm["x_ready"], 4 * KD)
            for n in range(2 * QT + 2):
                i, half = divmod(n, 2)
                if n >= 4:
                    pe.wait_ge(sm["y_a"] if n % 2 == 0 else sm["y_b"], (n - 4) // 2 + 1)
                m = P if i < QT else B
                for k in range(4):
                    last = tr(ps[n % 4][0:m, P * k:P * k + P], xT[:, 4 * half + k, P * i:P * i + m], P)
                last.then_inc(sm["y_mm"], 1)

        @block.scalar
        def _(act):
            link = chain(act, sm["act_step"])
            one = ones[:, 0:1]

            def copy(out, in_, scale=1.0):
                return act.activation(out, in_, ACT.Copy, scale=scale)

            def tile_done(g):
                act.wait_ge(sm["mm_done"], g + 1)

            def mlp_up(layer, g0):
                for j in range(KF):
                    g = g0 + j
                    tile_done(g)
                    act.activation(relA[j % 2], psA(g)[:, 0:H2], ACT.Relu).then_inc(sm["free_a"], 1)
                    act.wait_ge(sm["free_a"], g + 1)
                    act.activation(big[:, j, 0:H2], relA[j % 2], ACT.Square).then_inc(sm["hid_a"], 1)

            def squares(n_ln, g0):
                for m in range(KD):
                    act.wait_ge(sm["free_a"], g0 + m + 1)
                    act.wait_ge(sm["free_b"], g0 + m + 1)
                    if m >= 2:
                        act.wait_ge(sm["sum_r"], KD * n_ln + m - 1)
                    act.activation(sq[m % 2], xT[:, m, :], ACT.Square).then_inc(sm["sq_done"], 1)

            def norm(n_ln):
                act.wait_ge(sm["std_in"], n_ln + 1)
                act.activation(rs, var, ACT.Sqrt).then_inc(sm["stats_ok"], 1)
                nv = KD - len(LN_POOL)
                v = q = 0
                for m in range(KD):
                    if m in LN_POOL:
                        q += 1
                        act.wait_ge(sm["cen_p"], len(LN_POOL) * n_ln + q)
                    else:
                        v += 1
                        act.wait_ge(sm["cen_v"], nv * n_ln + v)
                    act.activation(xT[:, m, :], xT[:, m, :], ACT.Identity, scale=colT[:, KD * n_ln + m:KD * n_ln + m + 1],
                                   bias=colT[:, 32 + KD * n_ln + m:33 + KD * n_ln + m]).then_inc(sm["x_ready"], 1)

            for k in range(0, KD, 2):
                act.wait_ge(sm["tin"], k + 1)
                copy(xT[:, k, 0:S], ps[k % 6][:, :]).then_inc(sm["tin_a"], 1)

            for idx, t in enumerate(E_TILE):
                g = G_IN0 + idx
                tile_done(g)
                if idx == 0:
                    act.wait_ge(sm["small_in"], 16 * 10)
                    act.activation(gz[:, 0:H2], psA(g)[0:8, 0:H2], ACT.Identity, bias=gbc[0:8, :]).then_inc(sm["free_a"], 1)
                else:
                    copy(big[:, t, 0:H2], psA(g)[:, 0:H2], MH_SCALE if 16 <= t < 20 else 1.0).then_inc(sm["free_a"], 1)
                if idx == 2:
                    act.wait_ge(sm["nx_ok"], 1)
                    link(act.activation(lg, nx, ACT.Exp))
                    act.activation(lg, lg, ACT.Ln, bias=one[0:4, :]).then_inc(sm["sg_e"], 1)
                    act.wait_ge(sm["sp_ok"], 1)
                    act.activation(rowsP[0:MH, S:2 * S], nG, ACT.Exp)
                    act.activation(eS[0:MH, :], rowsS[0:MH, :], ACT.Exp).then_inc(sm["rows_ok"], 1)
                if idx >= 25:
                    act.wait_ge(sm["free_a"], g + 1)
                    act.wait_ge(sm["free_b"], g + 1)
                    act.activation(big[:, t, :], big[:, t, :], ACT.Exp, scale=-1.0).then_inc(sm["sg_e"], 1)
            act.wait_ge(sm["nnew_mm"], 1)
            copy(nno[0:MH * B, :], ps[4][0:MH * B, 0:P]).then_inc(sm["nnew_ev"], 1)
            act.wait_ge(sm["ucol_mm"], 1)
            copy(uo[0:B + 2, :], ps[5][0:B + 2, :]).then_inc(sm["ucol_ev"], 1)
            for h in range(MH):
                act.wait_ge(sm["pre_mm"], 4 * h + 1)
                if h:
                    act.wait_ge(sm["ws_ok"], h)
                link(copy(nml, ps[0][:, S - 1:S]))
                for i in range(QT):
                    if h:
                        act.wait_ge(sm["p_raw"], QT * (h - 1) + i + 1)
                    act.activation(Wt[:, OFF[i]:OFF[i] + S - P * i], ps[0][:, P * i:S], ACT.Exp,
                                   bias=aT[:, MH * i + h:MH * i + h + 1]).then_inc(sm["wt_ok"], 1)
                if h:
                    act.wait_ge(sm["cn_mm"], 2 * h)
                act.activation(wsc, aT.rearrange("p (i h) -> p i h", h=MH)[:, :, h], ACT.Exp, bias=nml).then_inc(sm["ws_ok"], 1)
                act.wait_ge(sm["pre_mm"], 4 * h + 4)
                copy(ktm, ps[3][:, :]).then_inc(sm["kt_ok"], 1)
                for n, (dst, src) in enumerate(((cst, ps[4][:, 0:P]), (nrow[0:1, :], ps[5][0:1, 0:P]))):
                    act.wait_ge(sm["cn_mm"], 2 * h + n + 1)
                    if h:
                        act.wait_ge(sm["store_c"], 16 * (MH + 2 * h))
                    copy(dst, src).then_inc(sm["cn_ev"], 1)
            squares(0, G_OUT0)
            norm(0)
            mlp_up(0, G_UP0)
            squares(1, G_DN0)
            norm(1)

            for idx, name in enumerate(O_NAMES):
                g = G_IN1 + idx
                tile_done(g)
                m = 60 if name == "misc" else P
                copy(big[0:m, idx, 0:H2], psA(g)[0:m, 0:H2], 0.125 if name[:2] in ("qn", "qd") else 1.0).then_inc(sm["free_a"], 1)
                if idx == 3:
                    act.wait_ge(sm["gate_e"], 1)
                    act.activation(gt[:, :, :], gt[:, :, :], ACT.Exp, scale=-1.0)
                    act.activation(gS[0:64, :], gS[0:64, :], ACT.Exp, scale=-1.0).then_inc(sm["gate_e"], 1)
                if 4 <= idx <= 6:
                    n = idx - 4
                    i = 3 - n
                    for e in range(4):
                        act.wait_ge(sm["isc_mm"], 4 * n + e + 1)
                        if 4 * n + e >= 2:
                            act.wait_ge(sm["isc_used"], 4 * n + e - 1)
                        act.activation(rl[e % 2][:, 0:P * (i + 1)], ps[4 + e][:, 0:P * (i + 1)], ACT.Relu,
                                       scale=IDX_SCALE).then_inc(sm["isc_r"], 1)
            for s in range(0, 8, 2):
                act.wait_ge(sm["tm_mm"], s + 1)
                copy(tm[:, :, P * s:P * s + P], ps[s % 4][:, :].rearrange("p (i c) -> p i c", i=QT)).then_inc(sm["tm_a"], 1)
            act.wait_ge(sm["tms_mm"], 1)
            for n in range(2):
                copy(tms[:, 512 * n:512 * n + 512], ps[4 + n][0:B, :]).then_inc(sm["tms_ev"], 1)

            def keys(step0, newkey, m=P):
                for st in range(4):
                    act.wait_ge(sm["bt_mm"], step0 + st + 1)
                    x = step0 + st
                    if x >= 2:
                        pe_count = x - 1 + (1 if x >= 10 else 0)
                        act.wait_ge(sm["bs_mm"], pe_count)
                    copy(kTs[st % 2][0:m, :, 0:PAST], ps[4 + st % 2][0:m, :].rearrange("p (b k) -> p b k", b=2))
                    copy(kTs[st % 2][0:m, :, PAST:LS], big[0:m, Z[newkey], S + 2 * st:S + 2 * st + 2].rearrange("p (b o) -> p b o", o=1)).then_inc(sm["bt_ev"], 1)

            keys(0, "ki4", 32)
            act.wait_ge(sm["bs_mm"], 4)
            act.activation(rS, ps[6][0:32, 0:LS], ACT.Relu, scale=IDX_SCALE).then_inc(sm["ix_r"], 1)
            for n, (br, where, q, kn, vn) in enumerate(BR):
                if br != "c":
                    keys({"d": 4, "s": 8, "w": 12}[br], kn)
                act.wait_ge(sm["sc_ok"], n + 1)
                dst = sc4[0:64, :] if br == "c" else sbs
                act.activation(dst, dst, ACT.Exp, bias=nms[0:64, :], accum_out=rss[0:64, :]).then_inc(sm["pe_ok"], 1)

            act.wait_ge(sm["pc_x"], 1)
            act.activation(sc, sc, ACT.Exp).then_inc(sm["pc_e"], 1)
            act.wait_ge(sm["pct_mm"], 1)
            copy(PcT, ps[5][0:64, :]).then_inc(sm["pct_ev"], 1)

            for t in range(len(units) + 2):
                if t < len(units):
                    i, p, g, br, k0, o = units[t]
                    n = P * (i + 1 - k0)
                    act.wait_ge(sm["q_sc"], 0 + t + 1)
                    act.wait_ge(sm["q_m"], t + 1)
                    if t >= 2:
                        act.wait_ge(sm["q_t"], t - 1)
                    act.activation(Pb[t % 2][:, 0:n], sbb[t % 2][:, 0:n], ACT.Exp, bias=nmx[t % 2],
                                   accum_out=rsum[t % 2]).then_inc(sm["q_e"], 1)
                u = t - 2
                if u >= 0:
                    i, p, g, br, k0, o = units[u]
                    n = P * (i + 1 - k0)
                    act.wait_ge(sm["q_t"], u + 1)
                    if u >= 2:
                        act.wait_ge(sm["q_o"], u - 1)
                    copy(PTb[u % 2][:, 0:n], ps[2 + u % 2][:, 0:n]).then_inc(sm["q_te"], 1)
            squares(2, G_OUT1)
            norm(2)
            mlp_up(1, G_UP1)
            squares(3, G_DN1)
            norm(3)
            for n in range(0, 2 * QT + 2, 2):
                i = n // 2
                m = P if i < QT else B
                act.wait_ge(sm["y_mm"], n + 1)
                copy(ytm[0:m, i, 0:512], ps[n % 4][0:m, :]).then_inc(sm["y_a"], 1)

        @block.vector
        def _(dve):
            link = chain(dve, sm["dve_step"])

            def tile_done(g):
                dve.wait_ge(sm["mm_done"], g + 1)

            def mlp_up(layer, g0):
                for j in range(KF):
                    g = g0 + j
                    tile_done(g)
                    dve.tensor_scalar(relB[j % 2], psB(g)[:, 0:H2], 0.0, None, ALU.max).then_inc(sm["free_b"], 1)
                    dve.wait_ge(sm["free_b"], g + 1)
                    dve.tensor_tensor(big[:, j, H2:T], relB[j % 2], relB[j % 2], ALU.mult).then_inc(sm["hid_b"], 1)

            def residual(g0):
                for m in range(KD):
                    g = g0 + m
                    tile_done(g)
                    dve.scalar_tensor_tensor(xT[:, m, 0:H2], xT[:, m, 0:H2], ALPHA, psA(g)[:, 0:H2], ALU.mult,
                                             ALU.add).then_inc(sm["free_a"], 1)
                    dve.scalar_tensor_tensor(xT[:, m, H2:T], xT[:, m, H2:T], ALPHA, psB(g)[:, 0:H2], ALU.mult,
                                             ALU.add).then_inc(sm["free_b"], 1)

            def norm(n_ln):
                dve.wait_ge(sm["stats_mm"], n_ln + 1)
                dve.tensor_copy(mu[:, 0:H2], ps[4][:, 0:H2])
                link(dve.tensor_copy(mu[:, H2:T], ps[5][:, 0:H2]))
                link(dve.tensor_tensor(var, mu, mu, ALU.mult))
                dve.tensor_tensor(var[:, 0:H2], ps[6][:, 0:H2], var[:, 0:H2], ALU.subtract)
                link(dve.tensor_tensor(var[:, H2:T], ps[7][:, 0:H2], var[:, H2:T], ALU.subtract))
                dve.tensor_scalar(var, var, 0.0, LN_EPS, ALU.max, ALU.add).then_inc(sm["std_in"], 1)
                dve.wait_ge(sm["stats_ok"], n_ln + 1)
                dve.reciprocal(rs, rs).then_inc(sm["std_ok"], 1)
                dve.wait_ge(sm["std_ok"], n_ln + 1)
                for m in range(KD):
                    if m not in LN_POOL:
                        link(dve.tensor_tensor(xT[:, m, :], xT[:, m, :], mu, ALU.subtract))
                        dve.tensor_tensor(xT[:, m, :], xT[:, m, :], rs, ALU.mult).then_inc(sm["cen_v"], 1)

            for k in range(1, KD, 2):
                dve.wait_ge(sm["tin"], k + 1)
                dve.tensor_copy(xT[:, k, 0:S], ps[k % 6][:, :]).then_inc(sm["tin_b"], 1)
            dve.wait_ge(sm["tin"], KD + 1)
            dve.tensor_copy(xT[:, :, S:T], ps[6][:, 0:KD * B].rearrange("p (k b) -> p k b", k=KD)).then_inc(sm["tin_b"], 1)
            dve.wait_ge(sm["tin"], KD + 2)
            dve.tensor_copy(colT[:, :], ps[7][:, 0:112])
            dve.tensor_copy(wcT, ps[7][:, 112:240]).then_inc(sm["tin_b"], 1)
            dve.wait_ge(sm["tin_b"], KD // 2 + 2)

            def bc(kind):
                return bcS.rearrange("p (h k b) -> p h k b", h=MH, k=3)[:, :, kind, :]

            def hb(v):
                return v.rearrange("p (h b) -> p h b", h=MH)

            def gates():
                dve.wait_ge(sm["fg_mm"], 1)
                dve.tensor_copy(fgt[:, 0:H2], ps[4][0:4, 0:H2])
                link(dve.tensor_copy(fgt[:, H2:T], ps[5][0:4, 0:H2]))
                dve.scalar_tensor_tensor(nx, fgt, -1.0, fgt, ALU.mult, ALU.min).then_inc(sm["nx_ok"], 1)
                dve.wait_ge(sm["sg_e"], 1)
                link(dve.scalar_tensor_tensor(lg, fgt, 0.0, lg, ALU.min, ALU.subtract))
                link(dve.tensor_tensor_scan(Fc, ones[0:4, 0:1].to_broadcast([4, S]), lg[:, 0:S], 0.0, ALU.mult, ALU.add))
                dve.wait_ge(sm["free_a"], 1)
                link(dve.tensor_tensor(at_, gz[0:4, 0:S], Fc, ALU.subtract))
                link(dve.tensor_tensor_scan(Mr, at_, at_, 0.0, ALU.max, ALU.max))
                dve.tensor_scalar(rowsP[0:MH, 0:S], Mr, -1.0, None, ALU.mult)
                link(dve.scalar_tensor_tensor(nG, Fc, -1.0, Mr, ALU.mult, ALU.subtract))
                dve.tensor_scalar(mpc[0:MH, :], nG[:, S - 1:S], -1.0, None, ALU.mult)
                link(dve.tensor_tensor(interS[0:MH, :], lg[:, S:T], stm[0:MH, :], ALU.add))
                link(dve.tensor_tensor(mtS[0:MH, :], interS[0:MH, :], gz[0:4, S:T], ALU.max))
                dve.tensor_tensor(rowsS[0:MH, 0:B], interS[0:MH, :], mtS[0:MH, :], ALU.subtract)
                dve.tensor_tensor(rowsS[0:MH, B:2 * B], gz[0:4, S:T], mtS[0:MH, :], ALU.subtract)
                dve.tensor_scalar(rowsS[0:MH, 2 * B:3 * B], mtS[0:MH, :], -1.0, None, ALU.mult).then_inc(sm["sp_ok"], 1)

            def sample_products():
                dve.wait_ge(sm["h12_mm"], 1)
                dve.tensor_copy(aT, ps[4][:, 0:16])
                dve.tensor_copy(bcS, ps[5][:, 0:96])
                dve.tensor_copy(scT, ps[7][:, 0:64])
                dve.wait_ge(sm["free_b"], 13)
                n_hb = colT[:, 80:112].rearrange("p (b h) -> p h b", h=MH)
                dve.tensor_tensor(hb(prod[:, 0:32]), n_hb, big[:, 12:16, S:T], ALU.mult)
                dve.tensor_tensor(hb(prod[:, 32:64]), big[:, 16:20, S:T], big[:, 12:16, S:T],
                                  ALU.mult).then_inc(sm["prod_ok"], 1)

            def sample_weights():
                n_hb = colT[:, 80:112].rearrange("p (b h) -> p h b", h=MH)
                nn_hb = nnw.rearrange("p (b h) -> p h b", h=MH)
                dve.wait_ge(sm["dots_mm"], 1)
                link(dve.tensor_copy(dts, ps[4][:, 0:64]))
                dve.tensor_tensor(hb(swa), hb(dts[:, 32:64]), bc(1), ALU.mult)
                link(dve.tensor_tensor(hb(recS), hb(dts[:, 0:32]), bc(0), ALU.mult))
                link(dve.tensor_tensor(recS, recS, swa, ALU.add))
                link(dve.scalar_tensor_tensor(recS, recS, -1.0, recS, ALU.mult, ALU.max))
                link(dve.tensor_tensor(hb(recS), hb(recS), bc(2), ALU.max))
                dve.reciprocal(recS, recS)
                dve.tensor_tensor(nn_hb, n_hb, bc(0), ALU.mult)
                link(dve.tensor_tensor(hb(vwS), big[:, 16:20, S:T], bc(1), ALU.mult))
                link(dve.tensor_tensor(nn_hb, nn_hb, hb(vwS), ALU.add))
                dve.tensor_tensor(hb(vwS), big[:, 20:24, S:T], bc(1), ALU.mult).then_inc(sm["nnew_ok"], 1)
                dve.wait_ge(sm["nnew_ok"], 1)

            def sample_head(h):
                def bd(bank):
                    return bank[:, :].rearrange("p (b d) -> p b d", b=4)
                dve.wait_ge(sm["head_mm"], h + 1)
                if h == 0:
                    dve.wait_ge(sm["c_in"], 16 * MH)
                for j in range(2):
                    last = dve.tensor_tensor(tmpS[:, 4 * j:4 * j + 4, :], Ct[:, h, 4 * j:4 * j + 4, :], bd(ps[4 + j]), ALU.mult)
                link(last)
                dve.tensor_reduce(cq[:, B * h:B * h + B], tmpS, AX.X, ALU.add)
                link(dve.tensor_tensor(Ct[:, h], Ct[:, h], bc(0)[:, h, :].unsqueeze(2).to_broadcast([P, B, P]), ALU.mult))
                for j in range(2):
                    v = vwS[:, B * h + 4 * j:B * h + 4 * j + 4]
                    last = dve.tensor_tensor(tmpS[:, 4 * j:4 * j + 4, :], bd(ps[6 + j]), v.unsqueeze(2).to_broadcast([P, 4, P]), ALU.mult)
                last.then_inc(sm["head_used"], 1)
                dve.wait_ge(sm["head_used"], h + 1)
                dve.tensor_tensor(Ct[:, h], Ct[:, h], tmpS, ALU.add).then_inc(sm["c_new"], 1)
                dve.wait_ge(sm["c_new"], h + 1)

            def convolve(i):
                def w(j):
                    return colT[:, 64 + 4 * j + i:65 + 4 * j + i]
                u, y = big[:, i, :], ymix[:, i, :]
                old = scT.rearrange("p (c b j) -> p c b j", c=4, b=B)[:, i]
                dve.wait_ge(sm["u_ok"], i + 1)
                dve.wait_ge(sm["free_a"], G_IN0 + 22 + i)
                link(dve.tensor_scalar(y, u, w(2), colT[:, 76 + i:77 + i], ALU.mult, ALU.add))
                dve.scalar_tensor_tensor(y[:, 1:S], u[:, 0:S - 1], w(1), y[:, 1:S], ALU.mult, ALU.add)
                link(dve.scalar_tensor_tensor(y[:, S:T], old[:, :, 1], w(1), y[:, S:T], ALU.mult, ALU.add))
                dve.scalar_tensor_tensor(y[:, 2:S], u[:, 0:S - 2], w(0), y[:, 2:S], ALU.mult, ALU.add)
                link(dve.scalar_tensor_tensor(y[:, S:T], old[:, :, 0], w(0), y[:, S:T], ALU.mult, ALU.add))
                dve.tensor_tensor(y, y, big[:, 4 + i, :], ALU.mult).then_inc(sm["conv_ok"], 1)

            for idx, t in enumerate(E_TILE):
                g = G_IN0 + idx
                tile_done(g)
                if idx == 0:
                    dve.wait_ge(sm["small_in"], 16 * 10)
                    dve.tensor_scalar(gz[:, H2:T], psB(g)[0:8, 0:H2], gbc[0:8, :], None, ALU.add).then_inc(sm["free_b"], 1)
                    dve.wait_ge(sm["free_b"], 1)
                elif 16 <= t < 20:
                    dve.tensor_scalar(big[:, t, H2:T], psB(g)[:, 0:H2], MH_SCALE, None, ALU.mult).then_inc(sm["free_b"], 1)
                else:
                    dve.tensor_copy(big[:, t, H2:T], psB(g)[:, 0:H2]).then_inc(sm["free_b"], 1)
                if idx == 2:
                    gates()
                if idx == 12:
                    sample_products()
                if idx == 14:
                    sample_weights()
                if idx in (16, 18, 20, 22):
                    sample_head((idx - 16) // 2)
                if 21 <= idx <= 24:
                    dve.wait_ge(sm["free_b"], g + 1)
                    convolve(idx - 21)
                if idx >= 25:
                    dve.wait_ge(sm["sg_e"], idx - 23)
                    link(dve.tensor_scalar(big[:, t, :], big[:, t, :], 1.0, None, ALU.add))
                    link(dve.reciprocal(big[:, t, :], big[:, t, :]))
            dve.tensor_tensor(hb(hS), hb(cq), bc(0), ALU.mult)
            link(dve.tensor_tensor(hb(prod[:, 0:32]), big[:, 20:24, S:T], hb(swa), ALU.mult))
            link(dve.tensor_tensor(hS, hS, prod[:, 0:32], ALU.add))
            link(dve.tensor_tensor(hS, hS, recS, ALU.mult))
            dve.tensor_tensor(ymix[:, 4:8, S:T], hb(hS), big[:, 24:28, S:T], ALU.mult).then_inc(sm["smp_y"], 1)
            for h in range(MH):
                dve.wait_ge(sm["pre_mm"], 4 * h + 3)
                if h:
                    dve.wait_ge(sm["pv_mm"], QT * h)
                dve.tensor_copy(vtm, ps[2][:, :]).then_inc(sm["vt_ok"], 1)
                for i in range(QT):
                    dve.wait_ge(sm["s_mm"], QT * h + i + 1)
                    dve.wait_ge(sm["wt_ok"], QT * h + i + 1)
                    n = S - P * i
                    dve.tensor_tensor(Pt[:, OFF[i]:OFF[i] + n], ps[4 + i % 2][:, 0:n], Wt[:, OFF[i]:OFF[i] + n],
                                      ALU.mult).then_inc(sm["p_raw"], 1)
                dve.wait_ge(sm["ws_ok"], h + 1)
                dve.wait_ge(sm["vt_ok"], h + 1)
                if h:
                    dve.wait_ge(sm["cn_mm"], 2 * h)
                dve.tensor_tensor(vw.rearrange("p (i d) -> p i d", i=QT), vtm.rearrange("p (i d) -> p i d", i=QT),
                                  wsc.unsqueeze(2).to_broadcast([P, QT, P]), ALU.mult).then_inc(sm["vw_ok"], 1)
                dve.wait_ge(sm["pv_mm"], QT * h + QT)
                link(dve.tensor_scalar(dn, ps[6][:, :], -1.0, None, ALU.mult))
                link(dve.tensor_tensor(dn, dn, ps[6][:, :], ALU.max))
                link(dve.tensor_tensor(dn, dn, ps[1][:, :], ALU.max))
                link(dve.reciprocal(dn, dn))
                link(dve.tensor_tensor(dn, ps[7][:, :], dn, ALU.mult))
                dve.tensor_tensor(ymix[:, 4 + h, 0:S], dn, big[:, 24 + h, 0:S], ALU.mult).then_inc(sm["hd_fin"], 1)
            residual(G_OUT0)
            norm(0)
            mlp_up(0, G_UP0)
            residual(G_DN0)
            norm(1)

            def small_odd():
                dve.wait_ge(sm["t1_mm"], 1)
                src = ps[4][:, 0:240].rearrange("p (i c) -> p i c", i=QT)
                dve.tensor_copy(mtm[:, :, :], src)
                dve.tensor_copy(gt[:, :, :], src[:, :, 0:24])
                dve.tensor_copy(mts[0:B, :], ps[5][0:B, 0:60]).then_inc(sm["t1_ev"], 1)
                i64, i32 = ident[0:64, 0:64], ident[0:32, 0:32]
                dve.tensor_reduce(mask64[0:64, :], i64.rearrange("p (b h) -> p h b", h=NH), AX.X, ALU.add)
                dve.tensor_reduce(mask32[0:32, :], i32.rearrange("p (b e) -> p e b", e=4), AX.X, ALU.add)
                dve.tensor_reduce(bsel32[0:32, :], i32.rearrange("p (b e) -> p b e", e=4), AX.X, ALU.add)
                dve.wait_ge(sm["sel_mm"], 1)
                dve.tensor_copy(gsel[0:64, :], ps[6][0:64, 0:60])
                dve.tensor_copy(ixE[0:32, :], ps[7][0:32, 0:60]).then_inc(sm["sel_ev"], 1)
                dve.wait_ge(sm["sel_ev"], 1)
                link(dve.tensor_tensor(g24[0:64, :].rearrange("p (h c) -> p h c", c=3),
                                       gsel[0:64, 0:24].rearrange("p (h c) -> p h c", c=3),
                                       mask64[0:64, :].unsqueeze(2).to_broadcast([64, NH, 3]), ALU.mult))
                dve.tensor_reduce(gS[0:64, :], g24[0:64, :].rearrange("p (h c) -> p c h", c=3), AX.X,
                                  ALU.add).then_inc(sm["gate_e"], 1)
                link(dve.tensor_tensor(wE[0:32, :], ixE[0:32, 56:60], mask32[0:32, :], ALU.mult))
                link(dve.tensor_reduce(wi32[0:32, :], wE[0:32, :], AX.X, ALU.add))
                dve.tensor_scalar(WI[0:32, :], bsel32[0:32, :], wi32[0:32, :], 0.5, ALU.mult, ALU.mult)
                link(dve.tensor_tensor(mask64[0:64, :], mask64[0:64, :], slope8[0:64, :], ALU.mult))
                dve.tensor_reduce(sl64[0:64, :], mask64[0:64, :], AX.X, ALU.add)
                dve.tensor_scalar(cm, D0[:, S - P:S], 0.5 * NEG, NEG, ALU.is_lt, ALU.mult)
                dve.tensor_scalar(Mc, Dc, 0.5 * NEG, None, ALU.is_ge)
                dve.wait_ge(sm["gate_e"], 2)
                dve.tensor_scalar(gt[:, :, :], gt[:, :, :], 1.0, None, ALU.add)
                link(dve.tensor_scalar(gS[0:64, :], gS[0:64, :], 1.0, None, ALU.add))
                dve.reciprocal(gt[:, :, :], gt[:, :, :])
                link(dve.reciprocal(gS[0:64, :], gS[0:64, :]))

            def indexer_scores(n):
                i = 3 - n
                w = P * (i + 1)
                tab = TAB[i]
                for e in range(4):
                    dve.wait_ge(sm["isc_r"], 4 * n + e + 1)
                    wie = mtm[:, i, 56 + e:57 + e]
                    last = (dve.tensor_scalar(tab, rl[0][:, 0:w], wie, None, ALU.mult) if e == 0
                            else dve.scalar_tensor_tensor(tab, rl[e % 2][:, 0:w], wie, tab, ALU.mult, ALU.add))
                    last.then_inc(sm["isc_used"], 1)
                    dve.wait_ge(sm["isc_used"], 4 * n + e + 1)
                dve.tensor_scalar(tab[:, 0:P * i], tab[:, 0:P * i], 0.5, None, ALU.mult)
                link(dve.scalar_tensor_tensor(tab[:, P * i:w], tab[:, P * i:w], 0.5, cm, ALU.mult, ALU.add))

            steps = [(i, r) for i in (3, 2, 1) for r in range(TOPK // 8)]

            def top_keys(n):
                for i, r in steps[:n]:
                    tab = TAB[i]
                    link(dve.max(m8, tab))
                    link(dve.match_replace(tab, m8, tab, TAKEN))
                    if r == TOPK // 8 - 1:
                        link(dve.tensor_scalar(tab, tab, 0.5 * TAKEN, NEG, ALU.is_gt, ALU.mult))
                        link(dve.tensor_tensor(tab, tab, D0[:, S - P * (i + 1):S], ALU.add))
                del steps[:n]

            for idx, name in enumerate(O_NAMES):
                g = G_IN1 + idx
                tile_done(g)
                m = 60 if name == "misc" else P
                if name[:2] in ("qn", "qd"):
                    dve.tensor_scalar(big[:, idx, H2:T], psB(g)[:, 0:H2], 0.125, None, ALU.mult).then_inc(sm["free_b"], 1)
                else:
                    dve.tensor_copy(big[0:m, idx, H2:T], psB(g)[0:m, 0:H2]).then_inc(sm["free_b"], 1)
                if idx == 3:
                    small_odd()
                if 4 <= idx <= 6:
                    indexer_scores(idx - 4)
                if idx >= 7:
                    top_keys(4)
            dve.wait_ge(sm["free_b"], G_OUT1)
            link(dve.memset(QI, 0.0))
            for e in range(4):
                r = slice(32 * e, 32 * e + 32)
                last = dve.tensor_copy(QI[0:32, e:e + 36 * 7 + 1:36], big[r, Z["qi"], S:T])
            last.then_inc(sm["qb_ok"], 1)
            for s in range(1, 8, 2):
                dve.wait_ge(sm["tm_mm"], s + 1)
                dve.tensor_copy(tm[:, :, P * s:P * s + P], ps[s % 4][:, :].rearrange("p (i c) -> p i c", i=QT)).then_inc(sm["tm_b"], 1)
            for br in ("d", "n"):
                link(dve.memset(QB[br], 0.0))
                for g in range(2):
                    r = slice(HD * g, HD * g + HD)
                    for p in range(NP):
                        h = NP * g + p
                        last = dve.tensor_copy(QB[br][r, h:h + 72 * 7 + 1:72], big[r, Z[f"q{br}0"] + p, S:T])
                last.then_inc(sm["qb_ok"], 1)
            dve.tensor_copy(vals[:, 32:40], big[:, Z["vs"], S:T])
            dve.tensor_copy(vals[:, 40:48], big[:, Z["vw"], S:T])
            link(dve.memset(KCZ, 0.0))
            dve.wait_ge(sm["ixc_mm"], 1)
            link(dve.tensor_copy(iscS, ps[7][0:B, 0:LS]))
            for r in range(TOPK_S // 8):
                link(dve.max(m8s[0:B, :], iscS))
                link(dve.match_replace(iscS, m8s[0:B, :], iscS, TAKEN))
            link(dve.tensor_scalar(iscS, iscS, 0.5 * TAKEN, NEG, ALU.is_gt, ALU.mult))
            dve.tensor_tensor(iscS, iscS, Ds[0:B, :], ALU.add).then_inc(sm["dsb_in"], 1)
            dve.wait_ge(sm["dsb_mm"], 1)
            link(dve.tensor_copy(DdS, ps[7][0:64, 0:LS]))
            for n, (br, where, q, kn, vn) in enumerate(BR):
                if br == "c":
                    dve.wait_ge(sm["cmp_mm"], 1)
                    dve.tensor_copy(cmps[0:32, :], ps[3][0:32, 0:256]).then_inc(sm["cmp_ev"], 1)
                    dve.wait_ge(sm["cmpt_mm"], 1)
                    dve.tensor_copy(kcTs, ps[3][:, 256:288])
                    dve.tensor_copy(vals[:, 0:32].rearrange("p (j b) -> p j b", b=B),
                                    ps[3][:, 288:320].rearrange("p (b j) -> p j b", b=B)).then_inc(sm["cmpt_ev"], 1)
                dve.wait_ge(sm["bs_mm"], {"d": 8, "c": 9, "s": 13, "w": 17}[br])
                tab = {"d": DdS, "c": Dcs[0:64, :], "s": Ds[0:64, :], "w": Dws[0:64, :]}[br]
                dst, w = (sc4[0:64, :], NBS) if br == "c" else (sbs, LS)
                if br in "sw":
                    dve.wait_ge(sm["pt_mm"], 1 if br == "s" else 2)
                link(dve.scalar_tensor_tensor(dst, tab, sl64[0:64, :], ps[6][0:64, 0:w], ALU.mult, ALU.add))
                dve.tensor_reduce(nms[0:64, :], dst, AX.X, ALU.max, negate=True).then_inc(sm["sc_ok"], 1)
                dve.wait_ge(sm["pe_ok"], n + 1)
                link(dve.tensor_scalar(rss[0:64, :], rss[0:64, :], 1e-30, None, ALU.max))
                link(dve.reciprocal(rcs[0:64, :], rss[0:64, :]))
                if br != "d":
                    k = "csw".index(br)
                    link(dve.tensor_tensor(rcs[0:64, :], rcs[0:64, :], gS[0:64, k:k + 1], ALU.mult))
                dve.tensor_scalar(dst, dst, rcs[0:64, :], None, ALU.mult).then_inc(sm["pn_ok"], 1)
                if br != "c":
                    k = "dsw".index(br) + 1
                    dve.wait_ge(sm["pt_mm"], k)
                    if k > 1:
                        dve.wait_ge(sm["pvs_mm"], k - 1)
                    dve.tensor_copy(PTs[:, :, :], ps[7][:, 0:128].rearrange("p (t c) -> p t c", t=2)).then_inc(sm["pt_ev"], 1)
            dve.wait_ge(sm["pvs_mm"], 3)
            link(dve.tensor_tensor(pbt.rearrange("p (j h) -> p j h", h=NH), ps[2][:, 0:384].rearrange("p (j h) -> p j h", h=NH),
                                   vals.unsqueeze(2).to_broadcast([P, 6 * B, NH]), ALU.mult))
            link(dve.tensor_reduce(oN, pbt.rearrange("p (j c) -> p c j", j=6), AX.X, ALU.add))
            dve.tensor_tensor(oN, oN, ps[0][:, 0:64], ALU.add).then_inc(sm["os_ok"], 1)
            link(dve.tensor_tensor(oD.rearrange("p (b h) -> p b h", h=NH), ps[2][:, 384:448].rearrange("p (b h) -> p b h", h=NH),
                                   big[:, Z["vd"], S:T].unsqueeze(2).to_broadcast([P, B, NH]), ALU.mult))
            dve.tensor_tensor(oD, oD, ps[1][:, 0:64], ALU.add).then_inc(sm["os_ok"], 1)
            dve.wait_ge(sm["os_ok"], 2)
            for n, o in enumerate((oN, oD)):
                for g in range(2):
                    r = slice(HD * g, HD * g + HD)
                    dve.tensor_copy(ymix[r, NP * n:NP * n + NP, S:T],
                                    o[r, :].rearrange("x (b g p) -> x g p b", g=2, p=NP)[:, g])
            for src, dst in (("kc", kcT), ("vc", vcT)):
                w = wcT[:, 0:BLK] if src == "kc" else wcT[:, BLK:2 * BLK]
                link(dve.tensor_tensor(tmpc.rearrange("p (j t) -> p j t", t=BLK),
                                       big[:, Z[src], 0:S].rearrange("p (j t) -> p j t", t=BLK),
                                       w.unsqueeze(1).to_broadcast([P, NB, BLK]), ALU.mult))
                link(dve.tensor_reduce(dst, tmpc.rearrange("p (j t) -> p j t", t=BLK), AX.X, ALU.add))
            link(dve.memset(cbuf[:, 0:256], 0.0))
            for g in range(2):
                r = slice(HD * g, HD * g + HD)
                last = dve.tensor_copy(KCZ[r, NB * g:NB * g + NB], kcT[r, :])
                for p in range(NP):
                    last = dve.tensor_copy(VF[r, p, 16 * p + NB * g:16 * p + NB * g + NB], vcT[r, :])
            last.then_inc(sm["kc_ok"], 1)
            c4 = "p (i c j) -> p i c j"
            slop = slopes.unsqueeze(1).unsqueeze(3).to_broadcast([P, QT, NH, NB])
            dcv = Dc.rearrange("p (i j) -> p i j", i=QT).unsqueeze(2).to_broadcast([P, QT, NH, NB])
            mcv = Mc.rearrange("p (i j) -> p i j", i=QT).unsqueeze(2).to_broadcast([P, QT, NH, NB])
            link(dve.tensor_tensor(sD.rearrange(c4, i=QT, c=NH), dcv, slop, ALU.mult))
            dve.wait_ge(sm["pc_mm"], 1)
            link(dve.tensor_tensor(sc, ps[7][:, 0:256], sD, ALU.add))
            link(dve.tensor_reduce(mxc, sc.rearrange("p (c j) -> p c j", j=NB), AX.X, ALU.max))
            dve.tensor_tensor(sc.rearrange("p (c j) -> p c j", j=NB), sc.rearrange("p (c j) -> p c j", j=NB),
                              mxc.unsqueeze(2).to_broadcast([P, 32, NB]), ALU.subtract).then_inc(sm["pc_x"], 1)
            dve.wait_ge(sm["vf_mm"], 1)
            dve.tensor_copy(VCb.rearrange("p q c -> p (q c)"), ps[4][0:64, :]).then_inc(sm["vf_ev"], 1)
            dve.wait_ge(sm["pc_e"], 1)
            link(dve.tensor_tensor(sc.rearrange(c4, i=QT, c=NH), sc.rearrange(c4, i=QT, c=NH), mcv, ALU.mult))
            link(dve.tensor_reduce(rcc, sc.rearrange("p (c j) -> p c j", j=NB), AX.X, ALU.add))
            link(dve.tensor_scalar(rcc, rcc, 1e-30, None, ALU.max))
            link(dve.reciprocal(rcc, rcc))
            link(dve.tensor_tensor(rcc.rearrange("x (i p g) -> x i p g", i=QT, p=NP),
                                   rcc.rearrange("x (i p g) -> x i p g", i=QT, p=NP),
                                   gt[:, :, :].rearrange("x i (g p c) -> x i p g c", g=2, p=NP)[:, :, :, :, 0], ALU.mult))
            dve.tensor_tensor(sc.rearrange("p (c j) -> p c j", j=NB), sc.rearrange("p (c j) -> p c j", j=NB),
                              rcc.unsqueeze(2).to_broadcast([P, 32, NB]), ALU.mult).then_inc(sm["pc_n"], 1)

            for t in range(len(units) + 4):
                if t < len(units):
                    i, p, g, br, k0, o = units[t]
                    n = P * (i + 1 - k0)
                    if br == "d" and steps:
                        top_keys(len(steps))
                    tab = (Dw[:, 3 * P - n:3 * P] if br == "w" else
                           D0[:, S - n:S] if br == "s" or i == 0 else TAB[i])
                    dve.wait_ge(sm["q_mm"], t + 1)
                    if t >= 2:
                        dve.wait_ge(sm["q_e"], t - 1)
                    dve.scalar_tensor_tensor(sbb[t % 2][:, 0:n], tab, SLOPE[NP * g + p], ps[t % 2][:, 0:n], ALU.mult,
                                             ALU.add).then_inc(sm["q_sc"], 1)
                    dve.wait_ge(sm["q_sc"], t + 1)
                    dve.tensor_reduce(nmx[t % 2], sbb[t % 2][:, 0:n], AX.X, ALU.max, negate=True).then_inc(sm["q_m"], 1)
                u = t - 1
                if 0 <= u < len(units):
                    i, p, g, br, k0, o = units[u]
                    n = P * (i + 1 - k0)
                    dve.wait_ge(sm["q_e"], u + 1)
                    link(dve.tensor_scalar(rsum[u % 2], rsum[u % 2], 1e-30, None, ALU.max))
                    link(dve.reciprocal(rrec[u % 2], rsum[u % 2]))
                    if br != "d":
                        c = 3 * (NP * g + p) + (1 if br == "s" else 2)
                        link(dve.tensor_tensor(rrec[u % 2], rrec[u % 2], gt[:, i, c:c + 1], ALU.mult))
                    dve.tensor_scalar(Pb[u % 2][:, 0:n], Pb[u % 2][:, 0:n], rrec[u % 2], None, ALU.mult).then_inc(sm["q_n"], 1)
                u = t - 4
                if u >= 0 and last_of[units[u][5]] == u:
                    i, p, g, br, k0, o = units[u]
                    dve.wait_ge(sm["q_o"], u + 1)
                    dve.tensor_copy(ymix[:, p + (NP if br == "d" else 0), P * i:P * i + P],
                                    ps[5 + o % 2][:, 0:P]).then_inc(sm["q_of"], 1)
            residual(G_OUT1)
            norm(2)
            mlp_up(1, G_UP1)
            residual(G_DN1)
            norm(3)
            for n in range(1, 2 * QT + 2, 2):
                i = n // 2
                m = P if i < QT else B
                dve.wait_ge(sm["y_mm"], n + 1)
                dve.tensor_copy(ytm[0:m, i, 512:1024], ps[n % 4][0:m, :]).then_inc(sm["y_b"], 1)


_INS = ['x_prompt', 'x_sample', 'state_conv', 'state_C', 'state_n', 'state_m', 'cache_kv', 'cache_idx', 'cache_win',
        'page_table', 'w_in_e', 'gate_b_e', 'conv_w', 'conv_b', 'w_out_e', 'w_in_o', 'w_cmp', 'w_out_o', 'w_up',
        'w_down', 'ln_g', 'ln_b']
_OUTS = [('y_p', (1, S, D)), ('y_s', (B, 1, D)), ('conv_p', (1, 1, 2, 512)), ('conv_s', (1, B, 2, 512)),
         ('c_p', (1, 1, MH, P, P)), ('c_s', (1, B, MH, P, P)), ('n_p', (1, 1, MH, P)), ('n_s', (1, B, MH, P)),
         ('m_p', (1, 1, MH)), ('m_s', (1, B, MH)), ('kv_p', (1, 1, S, 6, 2, HD)), ('kv_s', (1, B, 1, 6, 2, HD)),
         ('idx_p', (1, 1, S, 32)), ('idx_s', (1, B, 1, 32)), ('win_p', (1, 1, PAST, 2, 2, HD)),
         ('win_s', (1, B, PAST, 2, 2, HD))]


def kernel(**inputs):
    import numpy as _np
    import concourse.bacc as _bacc
    from concourse.bass_utils import run_bass_kernel_spmd as _run

    nc = _bacc.Bacc("TRN2", target_bir_lowering=False, num_devices=1)
    arrays, args = {}, []
    for name in _INS:
        a = _np.ascontiguousarray(inputs[name])
        arrays[f"in_{name}"] = a
        args.append(nc.dram_tensor(f"in_{name}", a.shape, mybir.dt.from_np(a.dtype), kind="ExternalInput").ap())
    for name, shape in _OUTS:
        args.append(nc.dram_tensor(f"out_{name}", shape, F32, kind="ExternalOutput").ap())
    build(nc, *args)
    r = _run(nc, [arrays], core_ids=[0])
    return tuple(r.results[0][f"out_{name}"] for name, _ in _OUTS)
```

```python
from contextlib import ExitStack

import concourse.bass as bass
from concourse import mybir

F32 = mybir.dt.float32
F32R = mybir.dt.float32r
I32 = mybir.dt.int32
ALU = mybir.AluOpType
ACT = mybir.ActivationFunctionType
AX = mybir.AxisListType

P = 128
D = 1024
KD = D // P
S = 512
B = 8
T = S + B
H2 = T // 2
QT = S // P
FF = 4096
KF = FF // P
NFC = FF // D
MH = 4
NH = 8
HD = 64
NP = NH // 2
BLK = 64
NB = S // BLK
PAST = 256
PAGE = 128
NPG = PAST // PAGE
NT = B * NPG
NBS = PAST // BLK
LS = PAST + 1
TOPK = min(256, S // 4)
TOPK_S = min(256, LS // 4)
ALPHA = 4.0 ** 0.25
LN_EPS = 1e-5
NEG = -1e30
TAKEN = -3e38
MH_SCALE = 128.0 ** -0.5
SLOTS = ("kc", "vc", "ks", "vs", "kd", "vd", "kw", "vw")
IDX_SCALE = 32.0 ** -0.5
SLOPE = [2.0 ** -(h + 1) for h in range(NH)]
SLOT = 4096
NSLOT = 3
NW = 4
LN_POOL = (3, 6)
XL_POOL = (1, 3, 5, 7)
XL_DVE = (0, 2, 4, 6)
SMALL = 5120


def build(nc, x_prompt, x_sample, state_conv, state_C, state_n, state_m, cache_kv, cache_idx, cache_win, page_table,
          w_in_e, gate_b_e, conv_w, conv_b, w_out_e, w_in_o, w_cmp, w_out_o, w_up, w_down, ln_g, ln_b,
          y_p, y_s, conv_p, conv_s, c_p, c_s, n_p, n_s, m_p, m_s, kv_p, kv_s, idx_p, idx_s, win_p, win_s):
    E_TILE = [None] + [12 + i for i in range(12)] + [0, 1, 2, 3, 8, 9, 10, 11, 4, 5, 6, 7, 24, 25, 26, 27]
    G_IN0 = 0
    G_OUT0 = G_IN0 + len(E_TILE)
    G_MLP0 = G_OUT0 + KD
    O_NAMES = ["misc", "ki4", "kd", "vd", "qi", "qd0", "qd1", "qd2", "qd3", "kc", "vc", "ks", "vs", "kw", "vw",
               "qn0", "qn1", "qn2", "qn3"]
    Z = {n: i for i, n in enumerate(O_NAMES)}
    L = {n: i for i, n in enumerate(["misc", "ki4", "kd", "vd", "qi", "kc", "vc", "ks", "qn0", "qn1", "qn2", "qn3",
                                     "qd0", "qd1", "qd2", "qd3", "vs", "kw", "vw"])}
    G_IN1 = G_MLP0 + 2 * KF
    G_OUT1 = G_IN1 + len(O_NAMES)
    G_MLP1 = G_OUT1 + KD

    with ExitStack() as ctx:
        def sb(name, shape, dt=F32):
            return ctx.enter_context(nc.sbuf_tensor(name, shape, dt))

        def sem(name):
            return ctx.enter_context(nc.semaphore(name))

        ring = sb("ring", [P, NSLOT, SLOT])
        xT = sb("xT", [P, KD, T])
        with ExitStack() as mixer:
            big = mixer.enter_context(nc.sbuf_tensor("big", [P, KF, T], F32))
            ymix = mixer.enter_context(nc.sbuf_tensor("ymix", [P, KD, T], F32))
            cbuf = mixer.enter_context(nc.sbuf_tensor("cbuf", [P, 4096], F32))
        xh = sb("xh", [P, KD, T], F32R)
        xl = sb("xl", [P, KD, T], F32R)
        hh = sb("hh", [P, KD, T], F32R)
        hl = sb("hl", [P, KD, T], F32R)
        wr2 = sb("wr2", [P, 2, 2, KD, P], F32R)
        sb("gap", [P, KD * T - 4096])
        wr0 = sb("wr0", [P, 2, 2, KD, P], F32R)
        att = sb("att", [P, 6144])
        ident = sb("ident", [P, P])
        ones = sb("ones", [P, P])
        meanM = sb("meanM", [P, P])
        colT = sb("colT", [P, 112])
        small = sb("small", [P, SMALL])
        ps = [ctx.enter_context(nc.psum_tensor(f"ps{i}", [P, 512], F32)) for i in range(8)]

        taken = [0]

        def piece(n):
            a = taken[0]
            taken[0] += n
            assert taken[0] <= SMALL, taken[0]
            return small[:, a:a + n]

        names = """x_in cols_in scs_in c_in pool_step small_in page_in consts_ok free_a free_b sq_done sum_r std_ok
            cen_p y_split x_ready xl_p hid_lo hid_sq u_ok sp_ok outs c_new store_c nnew_ev ucol_ev
            smp_y p_raw p_ok cn_ev cen_v z_pool kiz_ok kz_ok cw_ok mm_done tm_a tm_b tms_ev cmp_mm
            pvs_mm y_a y_b w_hi w_lo xl_v hid_hi stats_mm tin_a tin_b tin fg_mm rows_ok h12_mm
            prod_ok dots_mm nnew_ok head_used head_mm nnew_mm ucol_mm wt_ok pre_mm hd_fin vt_ok
            kt_ok s_mm pv_mm vw_ok cn_mm isc_r isc_mm t1_mm t1_ev sel_mm sel_ev tm_mm tms_mm bt_ev
            bt_mm bs_mm qb_ok ix_r ixc_mm dsb_in dsb_mm cmp_ev cmpt_mm cmpt_ev ixs_ev pn_ok dsd_ev
            pb_mm pb_ev pt_mm pt_ev kc_ok pc_mm vf_mm pc_n pct_mm pct_ev vf_ev q_sc q_mm q_n q_te
            q_t q_of q_o y_mm act_step std_in stats_ok x_hi nx_ok sg_e ws_ok gate_e isc_used sc_ok
            pe_ok pc_x pc_e q_m q_e dve_step conv_ok q_g mm_half""".split()
        sm = {n: sem(n) for n in names}
        gat = [sem(f"gathered{i}") for i in range(5)]
        w_sem = [sem(f"w_slot{i}") for i in range(NSLOT)]

        def rows(w, c0, c1):
            return w[:, c0:c1].rearrange("(k p) n -> p k n", p=P)

        chunks = []

        def chunk(parts, freed):
            chunks.append((parts, freed))
            return len(chunks) - 1

        def cols_of(slot, a, k, n):
            return ring[:, slot, a:a + k * n].rearrange("p (k n) -> p k n", k=k)

        def wide(w, c0, n, last_g):
            c = len(chunks)
            return chunk([(cols_of(c % NSLOT, 0, KD, n), rows(w, c0, c0 + n))], ("mm_done", last_g + 1))

        SMP_DONE = NP * QT + 6
        plan = {}

        def tile_plan(g, c, n, col, width=P, a=0):
            v = cols_of(c % NSLOT, a, KD, n)
            plan[g] = (c, lambda k, v=v, col=col, width=width: v[:, k, col:col + width], v[:, :, col:col + width])

        wi = w_in_e[0]
        c = wide(wi, 28 * P, 8, G_IN0)
        tile_plan(G_IN0, c, 8, 0, 8)
        for j in range(7):
            g = G_IN0 + 1 + 4 * j
            c = wide(wi, E_TILE[g - G_IN0] * P, 512, g + 3)
            for i in range(4):
                tile_plan(g + i, c, 512, i * P)

        split = []
        split_of = {}

        def split_chunk(parts_of, g):
            c = len(chunks)
            chunk(parts_of(c % NSLOT), ("w_lo", len(split) + 4))
            for i in range(4):
                tile_plan(g + i, c, 512, i * P)
                split_of[g + i] = len(split)
                split.append(g + i)

        def out_chunks(base, parts_of):
            for j in range(2):
                split_chunk(lambda slot: parts_of(slot, 512 * j), base + 4 * j)

        out_chunks(G_OUT0, lambda slot, c0: [(cols_of(slot, 0, KD, 512), rows(w_out_e[0], c0, c0 + 512))])

        def mlp_chunks(layer, g):
            for c in range(NFC):
                for w, r0, c0 in ((w_up[layer], 0, D * c), (w_down[layer], D * c, 0)):
                    for j in range(2):
                        split_chunk(lambda slot: [(cols_of(slot, 0, KD, 512),
                                                   rows(w[r0:r0 + D, :], c0 + 512 * j, c0 + 512 * j + 512))], g)
                        g += 4

        mlp_chunks(0, G_MLP0)

        wo = w_in_o[0]
        c = len(chunks)
        slot = c % NSLOT
        misc = cols_of(slot, 0, KD, 60 + P)
        chunk([(misc[:, :, 0:24], rows(wo, 1280, 1304)), (misc[:, :, 24:60], rows(wo, 2200, 2236))] +
              [(misc[:, :, 60 + 32 * e:92 + 32 * e], rows(wo, 2200, 2232)) for e in range(4)],
              ("mm_done", G_IN1 + 2))
        plan[G_IN1 + Z["misc"]] = (c, lambda k, v=misc: v[:, k, 0:60], None)
        plan[G_IN1 + Z["ki4"]] = (c, lambda k, v=misc: v[:, k, 60:60 + P], None)
        c = wide(wo, 1816, 384, G_IN1 + Z["qi"])
        for i, n in enumerate(("kd", "vd", "qi")):
            tile_plan(G_IN1 + Z[n], c, 384, i * P)

        def pair_tiles(c0, first):
            c = len(chunks)
            v = cols_of(c % NSLOT, 0, KD, 512)
            chunk([(v[:, :, P * p + HD * g:P * p + HD * g + HD], rows(wo, c0 + HD * (NP * g + p), c0 + HD * (NP * g + p + 1)))
                   for p in range(NP) for g in range(2)], ("mm_done", first + 4))
            for p in range(NP):
                tile_plan(first + p, c, 512, P * p)

        pair_tiles(1304, G_IN1 + Z["qd0"])
        c = wide(wo, 512, 512, G_IN1 + Z["vs"])
        for i, n in enumerate(("kc", "vc", "ks", "vs")):
            tile_plan(G_IN1 + Z[n], c, 512, i * P)
        c = wide(wo, 1024, 256, G_IN1 + Z["vw"])
        chunks[c] = (chunks[c][0], ("pvs_mm", 3))
        CACHE_SLOT = c % NSLOT
        for i, n in enumerate(("kw", "vw")):
            tile_plan(G_IN1 + Z[n], c, 256, i * P)
        pair_tiles(0, G_IN1 + Z["qn0"])
        c = len(chunks) - 1
        chunks[c] = (chunks[c][0], ("q_of", SMP_DONE))
        SCRATCH_SLOT = c % NSLOT

        def out_rows(slot, c0):
            w = w_out_o[0].rearrange("(s g q d) n -> s g d q n", s=2, g=2, q=NP)
            v = cols_of(slot, 0, KD, 512)
            return [(v[HD * g:HD * (g + 1), NP * s:NP * (s + 1), :], w[s, g, :, :, c0:c0 + 512])
                    for s in range(2) for g in range(2)]

        out_chunks(G_OUT1, out_rows)
        mlp_chunks(1, G_MLP1)

        loads = [0] * NSLOT
        chunk_value = []
        for c, (parts, _) in enumerate(chunks):
            loads[c % NSLOT] += 16 * len(parts)
            chunk_value.append(loads[c % NSLOT])

        NS1 = split_of[G_OUT1]

        def w_split(u):
            return [(wr0 if u % NW < 2 else wr2)[:, u % 2, part] for part in range(2)]

        def w_raw(u):
            return plan[split[u]][2]

        block = ctx.enter_context(nc.Block())

        def chain(eng, s):
            n = [0]

            def link(ins):
                n[0] += 1
                ins.then_inc(s, 1)
                eng.wait_ge(s, n[0])
            return link

        sel = piece(MH * P).rearrange("p (h m) -> p h m", h=MH)
        D0 = piece(S)
        Dw = piece(3 * P)
        Ds = piece(LS)
        Dws = piece(LS)
        Dc = piece(QT * NB)
        Mc = piece(QT * NB)
        Dcs = piece(NBS)
        BS = piece(62)
        selB = piece(B * NH)
        selE = piece(B * 4)
        slopes = piece(NH)
        slope8 = piece(NH)
        wcK = piece(2 * P)
        wcT = piece(2 * BLK)
        pages = ctx.enter_context(nc.sbuf_tensor("pages", [1, NT], I32))
        base = taken[0]

        xp_stage = ymix[:, :, :].rearrange("p a b -> p (a b)")[:, 0:QT * D].rearrange("p (t d) -> p t d", t=QT)
        xs_stage = att[0:B, 0:D]
        stg = att[0:112, 1024:1152]
        scs = att[0:2 * B, 1152:1152 + 512]
        stm = piece(B)
        gbc = piece(1)

        Ct = cbuf[:, :].rearrange("p (b h d) -> p h b d", h=MH, b=B)
        gz = att[0:8, 1664:1664 + T]
        fgt = att[0:4, 2184:2184 + T]
        nx = att[0:4, 2704:2704 + T]
        lg = att[0:4, 3224:3224 + T]
        Fc = att[0:4, 3744:3744 + S]
        at_ = att[0:4, 4256:4256 + S]
        Mr = att[0:4, 4768:4768 + S]
        nG = att[0:4, 5280:5280 + S]
        rowsP = piece(2 * S)
        rowsS = piece(3 * B)
        eS = piece(3 * B)
        interS = piece(B)
        mtS = piece(B)
        mpc = piece(1)
        aT = piece(QT * MH)
        bcS = piece(MH * 3 * B)
        scT = piece(4 * 2 * B)
        prod = piece(2 * MH * B)
        dts = piece(2 * MH * B)
        nnw = piece(MH * B)
        vwS = piece(MH * B)
        swa = piece(MH * B)
        recS = piece(MH * B)
        cq = piece(MH * B)
        hS = piece(MH * B)
        wsc = piece(QT)
        nml = piece(1)
        nno = piece(P)
        uo = piece(512)
        cst = piece(P)
        nrow = piece(P)
        OFF = [0, 512, 896, 1152]
        Wt = att[:, 0:1280]
        Pt = att[:, 1280:2560]
        vtm = att[:, 2560:3072]
        ktm = att[:, 3072:3584]
        vw = att[:, 3584:4096]
        tmpS = att[:, 4096:5120].rearrange("p (b d) -> p b d", b=B)
        dn = att[:, 5120:5632]

        racc = att[:, 0:T]
        sacc = att[:, T:2 * T]
        sq = [att[:, (2 + i) * T:(3 + i) * T] for i in range(2)]
        mu = att[:, 4 * T:5 * T]
        rs = att[:, 5 * T:6 * T]
        rel = [att[:, (6 + i) * T:(7 + i) * T] for i in range(2)]
        var = att[:, 8 * T:9 * T]
        hid = [att[:, (9 + i) * T:(10 + i) * T] for i in range(2)]

        after0 = taken[0]
        taken[0] = base
        flat = big[:, :, :].rearrange("p a b -> p (a b)")
        o = len(O_NAMES) * T
        tm = flat[:, o:o + QT * 1024].rearrange("p (i c) -> p i c", i=QT)
        o += QT * 1024
        tms = flat[0:B, o:o + 1024]
        o += 1024
        TAB = [None, flat[:, o:o + 256], flat[:, o + 256:o + 640], flat[:, o + 640:o + 1152]]
        assert o + 1152 <= KF * T
        KZ = {n: att[:, 1024 * i:1024 * (i + 1)].rearrange("p (g k) -> p g k", g=2) for i, n in enumerate(("kd", "ks", "kw"))}
        kiz = att[:, 3072:3072 + 2048].rearrange("p (e k) -> p e k", e=4)
        rl = [att[:, 5120 + 512 * i:5632 + 512 * i] for i in range(2)]
        room = ring[:, SCRATCH_SLOT, :]
        kTs = [room[:, 2 * LS * i:2 * LS * (i + 1)].rearrange("p (b k) -> p b k", b=2) for i in range(2)]
        o = 4 * LS
        sbs = room[0:64, o:o + LS]
        iscS = room[0:B, o + LS:o + 2 * LS]
        rS = room[0:32, o + 2 * LS:o + 3 * LS]
        DdS = room[0:64, o + 3 * LS:o + 4 * LS]
        o += 4 * LS
        PTs = room[:, o:o + 128].rearrange("p (t c) -> p t c", t=2)
        QI = room[:, o + 128:o + 128 + 256]
        kidx = room[:, o + 384:o + 384 + 512].rearrange("p (t e) -> p t e", t=NT)
        o += 896
        VCb = room[0:64, o:o + 512].rearrange("p (q c) -> p q c", q=NP)
        PcT = room[0:64, o + 512:o + 1024]
        assert o + 1024 <= SLOT, o
        pbt = flat[:, len(O_NAMES) * T + QT * 1024 + 1024 + 1152:][:, 0:384]
        QB = {"d": piece(512), "n": piece(512)}
        mtm = piece(QT * 60).rearrange("p (i c) -> p i c", i=QT)
        gt = piece(QT * 24).rearrange("p (i c) -> p i c", i=QT)
        mts = piece(60)
        gsel = piece(60)
        gS = piece(3)
        g24 = piece(24)
        mask64 = piece(NH)
        sl64 = piece(1)
        mask32 = piece(4)
        bsel32 = piece(B)
        wE = piece(4)
        wi32 = piece(1)
        WI = piece(B)
        ixE = piece(60)
        m8 = piece(8)
        m8s = piece(8)
        nmx = [piece(1) for _ in range(2)]
        rsum = [piece(1) for _ in range(2)]
        rrec = [piece(1) for _ in range(2)]
        nms, rss, rcs = piece(1), piece(1), piece(1)
        kcT = piece(NB)
        vcT = piece(NB)
        KCZ = piece(2 * NB)
        kcTs = piece(B * NBS)
        vals = piece(6 * B)
        cmps = piece(2 * P)
        sc4 = piece(NBS)
        oN = piece(B * NH)
        mixc = piece(P)
        oD = piece(B * NH)
        rsN = piece(B * NH)
        assert taken[0] <= SMALL
        o = 3072
        VF = att[:, o:o + 256].rearrange("p (q c) -> p q c", q=NP)
        sc = att[:, o + 256:o + 512]
        sD = att[:, o + 512:o + 768]
        mxc = att[:, o + 768:o + 800]
        rcc = att[:, o + 800:o + 832]
        tmpc = att[:, o + 832:o + 1344]
        Pb = [att[:, 3072 + 512 * i:3584 + 512 * i] for i in range(2)]
        PTb = [att[:, 4096 + 512 * i:4608 + 512 * i] for i in range(2)]
        sbb = [att[:, 5120 + 512 * i:5632 + 512 * i] for i in range(2)]
        cache = {"c": cbuf[:, :].rearrange("p (t x) -> p t x", t=NT),
                 "y": ring[:, CACHE_SLOT, :].rearrange("p (t x) -> p t x", t=NT)}
        STEP = {"s": (10, 4, "y", "n", 0), "d": (18, 8, "c", "d", 2), "w": (26, 12, "y", "n", 3)}
        EVERY, START = 2, 8

        units = []
        for i in range(QT):
            for p in range(NP):
                for br in ("s", "w"):
                    for g in range(2):
                        units.append((i, p, g, br, 0 if br == "s" else max(0, i - 2), i * NP + p))
        for i in range(QT):
            for p in range(NP):
                for g in range(2):
                    units.append((i, p, g, "d", 0, (QT + i) * NP + p))
        EARLY = len(units) - 16
        first_of = {}
        last_of = {}
        for u, x in enumerate(units):
            first_of.setdefault((x[5], x[2]), u)
            last_of[x[5]] = u

        cm = mixc
        ytm = flat[:, 0:5 * D].rearrange("p (i d) -> p i d", i=5)

        def psA(g):
            return ps[2 * (g % 2)]

        def psB(g):
            return ps[2 * (g % 2) + 1]

        @block.sync
        def _(sp):
            sp.dma_start(xp_stage, x_prompt[0].rearrange("(t p) d -> p t d", p=P)).then_inc(sm["x_in"], 16)
            sp.dma_start(xs_stage, x_sample.rearrange("b o d -> (b o) d")).then_inc(sm["x_in"], 16)
            sp.dma_start(stg[0:32, :], ln_g.rearrange("l s (k d) -> (l s k) d", d=P)).then_inc(sm["cols_in"], 16)
            sp.dma_start(stg[32:64, :], ln_b.rearrange("l s (k d) -> (l s k) d", d=P)).then_inc(sm["cols_in"], 16)
            sp.dma_start(stg[64:76, :], conv_w.rearrange("o j (c d) -> (o j c) d", d=P)).then_inc(sm["cols_in"], 16)
            sp.dma_start(stg[76:80, :], conv_b.rearrange("o (c d) -> (o c) d", d=P)).then_inc(sm["cols_in"], 16)
            sp.dma_start(stg[80:112, :], state_n.rearrange("o b h d -> (o b h) d")).then_inc(sm["cols_in"], 16)
            sp.dma_start(scs, state_conv.rearrange("o b j c -> (o b j) c")).then_inc(sm["scs_in"], 16)
            for c, (parts, _) in enumerate(chunks):
                if c >= NSLOT:
                    s, v = chunks[c - NSLOT][1]
                    sp.wait_ge(sm[s], v)
                for dst, src in parts:
                    sp.dma_start(dst, src).then_inc(w_sem[c % NSLOT], 16)
                if c == 1:
                    for h in range(MH):
                        sp.dma_start(Ct[:, h, :, :], state_C[0, :, h].rearrange("b e d -> e b d")).then_inc(sm["c_in"], 16)

        @block.gpsimd
        def _(pool):
            link = chain(pool, sm["pool_step"])
            pool.dma_start(stm[0:MH, :], state_m[0].rearrange("b h -> h b"), allow_slow_non_contiguous=True).then_inc(sm["small_in"], 16)
            pool.dma_start(gbc[0:8, :], gate_b_e.rearrange("o c -> c o"), allow_slow_non_contiguous=True).then_inc(sm["small_in"], 16)
            pool.dma_start(pages[0:1, :], page_table.rearrange("(o b) t -> o (b t)", o=1)).then_inc(sm["page_in"], 16)
            for half in range(2):
                for s in range(2):
                    for g in range(2):
                        pool.dma_start(wcK[64 * half:64 * half + 64, P * s + HD * g:P * s + HD * g + HD],
                                       w_cmp[0, s]).then_inc(sm["small_in"], 16)
            link(pool.memset(ident[:, :], 0.0))
            pool.affine_select(out=ident[:, :], in_=ident[:, :], compare_op=ALU.not_equal, fill=1.0, base=0,
                               pattern=[[-1, P]], channel_multiplier=1).then_inc(sm["consts_ok"], 1)
            pool.memset(ones[:, :], 1.0)
            pool.memset(meanM[:, :], 1.0 / D).then_inc(sm["consts_ok"], 1)
            link(pool.memset(sel[:, :, :], 0.0))
            pool.affine_select(out=sel[:, :, :], in_=sel[:, :, :], compare_op=ALU.not_equal, fill=1.0, base=0,
                               pattern=[[-1, MH], [0, P]], channel_multiplier=1)
            link(pool.iota(D0, pattern=[[1, S]], base=-(S - P), channel_multiplier=-1, allow_small_or_imprecise_dtypes=True))
            link(pool.affine_select(out=D0, in_=D0, compare_op=ALU.is_ge, fill=NEG, base=S - P,
                                    pattern=[[-1, S]], channel_multiplier=1))
            pool.affine_select(out=Dw, in_=D0[:, P:S], compare_op=ALU.is_gt, fill=NEG, base=0,
                               pattern=[[1, 3 * P]], channel_multiplier=-1)
            pool.iota(Ds, pattern=[[1, LS]], base=-PAST, channel_multiplier=0, allow_small_or_imprecise_dtypes=True)
            link(pool.iota(Dws, pattern=[[1, LS]], base=-PAST, channel_multiplier=0, allow_small_or_imprecise_dtypes=True))
            pool.memset(Dws[:, 0:1], NEG)
            link(pool.iota(Dc.rearrange("p (i j) -> p i j", i=QT), pattern=[[-P, QT], [BLK, NB]], base=BLK - 1,
                           channel_multiplier=-1, allow_small_or_imprecise_dtypes=True))
            pool.affine_select(out=Dc.rearrange("p (i j) -> p i j", i=QT), in_=Dc.rearrange("p (i j) -> p i j", i=QT),
                               compare_op=ALU.is_ge, fill=NEG, base=-(BLK - 1), pattern=[[P, QT], [-BLK, NB]],
                               channel_multiplier=1)
            pool.iota(Dcs, pattern=[[BLK, NBS]], base=BLK - 1 - PAST, channel_multiplier=0,
                      allow_small_or_imprecise_dtypes=True)
            link(pool.memset(BS, 0.0))
            link(pool.memset(BS[0:64, 30:31], 1.0))
            link(pool.memset(BS[64:128, 31:32], 1.0))
            link(pool.memset(selB, 0.0))
            pool.affine_select(out=selB.rearrange("p (b h) -> p b h", b=B), in_=selB.rearrange("p (b h) -> p b h", b=B),
                               compare_op=ALU.not_equal, fill=1.0, base=0, pattern=[[-1, B], [0, NH]], channel_multiplier=1)
            link(pool.memset(selE, 0.0))
            pool.affine_select(out=selE.rearrange("p (b h) -> p b h", b=B), in_=selE.rearrange("p (b h) -> p b h", b=B),
                               compare_op=ALU.not_equal, fill=1.0, base=0, pattern=[[-1, B], [0, 4]], channel_multiplier=1)
            for h in range(NH):
                g, p = divmod(h, NP)
                pool.memset(slopes[:, 2 * p + g:2 * p + g + 1], SLOPE[h])
                last = pool.memset(slope8[:, h:h + 1], SLOPE[h])
            last.then_inc(sm["consts_ok"], 1)

            def sums(n_ln, g0):
                for m in range(KD):
                    pool.wait_ge(sm["free_a"], g0 + m + 1)
                    pool.wait_ge(sm["free_b"], g0 + m + 1)
                    if m == 0:
                        link(pool.tensor_copy(racc, xT[:, 0, :]))
                    else:
                        link(pool.tensor_tensor(racc, racc, xT[:, m, :], ALU.add))
                    pool.wait_ge(sm["sq_done"], KD * n_ln + m + 1)
                    last = (pool.tensor_copy(sacc, sq[0]) if m == 0
                            else pool.tensor_tensor(sacc, sacc, sq[m % 2], ALU.add))
                    last.then_inc(sm["sum_r"], 1)
                    pool.wait_ge(sm["sum_r"], KD * n_ln + m + 1)
                pool.wait_ge(sm["std_ok"], n_ln + 1)
                for n, m in enumerate(LN_POOL):
                    link(pool.tensor_tensor(xT[:, m, :], xT[:, m, :], mu, ALU.subtract))
                    pool.tensor_tensor(xT[:, m, :], xT[:, m, :], rs, ALU.mult).then_inc(sm["cen_p"], 1)

            def split_y(k, s, v):
                pool.wait_ge(sm[s], v)
                link(pool.tensor_copy(xh[:, k, :], ymix[:, k, :]))
                pool.tensor_tensor(xl[:, k, :], ymix[:, k, :], xh[:, k, :].bitcast(F32), ALU.subtract).then_inc(sm["y_split"], 1)

            def x_low(layer):
                for n, m in enumerate(XL_POOL):
                    pool.wait_ge(sm["x_ready"], 2 * KD * layer + m + 1)
                    pool.tensor_tensor(xl[:, m, :], xT[:, m, :], xh[:, m, :].bitcast(F32), ALU.subtract).then_inc(sm["xl_p"], 1)

            def mlp(layer, g):
                for c in range(NFC):
                    for j in range(KD):
                        n = KF * layer + KD * c + j
                        pool.wait_ge(sm["free_a"], g + 1)
                        pool.wait_ge(sm["free_b"], g + 1)
                        if n >= 2:
                            pool.wait_ge(sm["hid_lo"], n - 1)
                        pool.tensor_tensor(hid[j % 2], rel[j % 2], rel[j % 2], ALU.mult).then_inc(sm["hid_sq"], 1)
                        g += 1
                    g += KD

            for i in range(4):
                g = G_IN0 + 17 + i
                pool.wait_ge(sm["free_a"], g + 1)
                pool.wait_ge(sm["free_b"], g + 1)
                pool.tensor_tensor(big[:, i, :], big[:, i, :], big[:, 8 + i, :], ALU.mult).then_inc(sm["u_ok"], 1)
            pool.wait_ge(sm["sp_ok"], 1)
            pool.dma_start(m_p.rearrange("o b h -> h (o b)"), mpc[0:MH, :], allow_slow_non_contiguous=True).then_inc(sm["outs"], 16)
            pool.dma_start(m_s[0].rearrange("b h -> h b"), mtS[0:MH, :], allow_slow_non_contiguous=True).then_inc(sm["outs"], 16)
            for h in range(MH):
                pool.wait_ge(sm["c_new"], h + 1)
                pool.dma_start(c_s[0, :, h].rearrange("b e d -> e b d"), Ct[:, h, :, :]).then_inc(sm["store_c"], 16)
            pool.wait_ge(sm["nnew_ev"], 1)
            pool.dma_start(n_s.rearrange("o b h d -> (o b h) d"), nno[0:MH * B, :]).then_inc(sm["outs"], 16)
            pool.wait_ge(sm["ucol_ev"], 1)
            pool.dma_start(conv_p.rearrange("o b j c -> (o b j) c"), uo[0:2, :]).then_inc(sm["outs"], 16)
            pool.dma_start(conv_s[0, :, 1, :], uo[2:2 + B, :]).then_inc(sm["outs"], 16)
            pool.dma_start(conv_s[0, :, 0, :], state_conv[0, :, 1, :]).then_inc(sm["outs"], 16)
            for k in range(4):
                split_y(k, "conv_ok", k + 1)
            pool.wait_ge(sm["smp_y"], 1)
            for h in range(MH):
                for i in range(QT):
                    pool.wait_ge(sm["p_raw"], QT * h + i + 1)
                    d = Pt[:, OFF[i]:OFF[i] + P]
                    pool.affine_select(out=d, in_=d, compare_op=ALU.is_ge, fill=0.0, base=0, pattern=[[1, P]],
                                       channel_multiplier=-1).then_inc(sm["p_ok"], 1)
                if h:
                    split_y(MH + h - 1, "hd_fin", h)
                pool.wait_ge(sm["cn_ev"], 2 * h + 2)
                pool.dma_start(c_p[0, 0, h], cst).then_inc(sm["store_c"], 16)
                pool.dma_start(n_p[0, :, h, :], nrow[0:1, :]).then_inc(sm["store_c"], 16)
            split_y(KD - 1, "hd_fin", MH)
            sums(0, G_OUT0)
            x_low(0)
            mlp(0, G_MLP0)
            sums(1, G_MLP0 + 2 * KF - KD)

            pool.wait_ge(sm["cen_v"], 2 * (KD - len(LN_POOL)))
            pool.wait_ge(sm["x_ready"], 2 * KD)
            pool.memset(kiz[:, :, :], 0.0)
            last = pool.memset(att[:, 0:3072], 0.0)
            last.then_inc(sm["z_pool"], 1)
            pool.wait_ge(sm["z_pool"], 1)

            def tile_ready(name):
                pool.wait_ge(sm["free_a"], G_IN1 + Z[name] + 1)
                pool.wait_ge(sm["free_b"], G_IN1 + Z[name] + 1)

            tile_ready("ki4")
            for e in range(4):
                pool.tensor_copy(kiz[32 * e:32 * e + 32, e, :], big[32 * e:32 * e + 32, L["ki4"], 0:S]).then_inc(sm["kiz_ok"], 1)
                pool.wait_ge(sm["kiz_ok"], e + 1)
            pool.wait_ge(sm["page_in"], 16)

            def gather(n, src_of, dst):
                for t in range(NT):
                    r = pool.value_load(pages[0:1, t:t + 1], min_val=0, max_val=cache_kv.shape[1] - 1)
                    pool.dma_start(dst[:, t, :], src_of(r)).then_inc(gat[n], 16)

            kv_rows = cache_kv[0].rearrange("n p s g d -> n p (s g d)")

            def kv_page(c0):
                return lambda r: kv_rows[bass.ds(r, 1), :, c0:c0 + 256].rearrange("n p x -> p (n x)")

            gather(1, kv_page(0), cache["c"])
            for n, name in enumerate(("kd", "ks", "kw")):
                tile_ready(name)
                for g in range(2):
                    pool.tensor_copy(KZ[name][HD * g:HD * g + HD, g, :],
                                     big[HD * g:HD * g + HD, L[name], 0:S]).then_inc(sm["kz_ok"], 1)
                    pool.wait_ge(sm["kz_ok"], 2 * n + g + 1)
                if n == 0:
                    pool.wait_ge(gat[1], 16 * NT)
                    for t in range(NT):
                        last = pool.tensor_tensor(cache["c"][:, t, :], cache["c"][:, t, :], wcK, ALU.mult)
                    last.then_inc(sm["cw_ok"], 1)
                    pool.wait_ge(sm["cw_ok"], 1)
            pool.wait_ge(sm["mm_done"], G_IN1 + Z["vw"] + 1)
            gather(0, kv_page(2 * P), cache["y"])
            pool.wait_ge(sm["mm_done"], G_OUT1)
            gather(4, lambda r: cache_idx[0][bass.ds(r, 1), :, :].rearrange("n p e -> p (n e)"), kidx)
            pool.wait_ge(sm["tm_a"], 4)
            pool.wait_ge(sm["tm_b"], 4)
            pool.dma_start(kv_p[0, 0].rearrange("(i p) s g d -> p i (s g d)", p=P), tm[:, :, 0:768]).then_inc(sm["outs"], 16)
            pool.dma_start(win_p[0, 0].rearrange("(i p) s g d -> p i (s g d)", p=P), tm[:, 2:4, 768:1024]).then_inc(sm["outs"], 16)
            pool.wait_ge(sm["tms_ev"], 2)
            pool.dma_start(kv_s[0].rearrange("b t s g d -> (b t) (s g d)"), tms[:, 0:768]).then_inc(sm["outs"], 16)
            pool.dma_start(win_s[0, :, PAST - 1].rearrange("b s g d -> b (s g d)"), tms[:, 768:1024]).then_inc(sm["outs"], 16)
            pool.dma_start(win_s[0, :, 0:PAST - 1].rearrange("b t s g d -> b t (s g d)"),
                           cache_win[0, :, 1:PAST].rearrange("b t s g d -> b t (s g d)")).then_inc(sm["outs"], 16)
            pool.dma_start(idx_p[0, 0].rearrange("(i p) e -> p i e", p=P), mtm[:, :, 24:56]).then_inc(sm["outs"], 16)
            pool.dma_start(idx_s[0].rearrange("b t e -> (b t) e"), mts[0:B, 24:56]).then_inc(sm["outs"], 16)
            pool.wait_ge(sm["cmp_mm"], 1)
            gather(2, kv_page(4 * P), cache["c"])
            pool.wait_ge(sm["pvs_mm"], 1)
            pool.dma_start(cache["y"], cache_win[0].rearrange("b (t p) s g d -> p (b t) (s g d)", p=P)).then_inc(gat[3], 16)
            pool.wait_ge(sm["outs"], 16 * 13)
            for k in range(KD):
                split_y(k, "q_of", SMP_DONE if k < NP else (2 * QT - 1) * NP + k - NP + 1)
            sums(2, G_OUT1)
            x_low(1)
            mlp(1, G_MLP1)
            sums(3, G_MLP1 + 2 * KF - KD)
            for i in range(QT):
                pool.wait_ge(sm["y_a"], i + 1)
                pool.wait_ge(sm["y_b"], i + 1)
                pool.dma_start(y_p[0, P * i:P * (i + 1), :], ytm[:, i, :]).then_inc(sm["outs"], 16)
            pool.wait_ge(sm["y_a"], QT + 1)
            pool.wait_ge(sm["y_b"], QT + 1)
            pool.dma_start(y_s.rearrange("b o d -> (b o) d"), ytm[0:B, QT, :]).then_inc(sm["outs"], 16)
            pool.wait_ge(sm["outs"], 16 * 18)
            pool.wait_ge(sm["store_c"], 16 * 3 * MH)

        @block.tensor
        def _(pe):
            def tr(out, in_, n):
                return pe.matmul(out, in_, ident[0:n, 0:n], start=True, stop=True, is_transpose=True,
                                 skip_group_check=True)

            def mm(out, lhsT, rhs, start=True, stop=True):
                return pe.matmul(out, lhsT, rhs, start=start, stop=stop, skip_group_check=True)

            loaded = [-1]

            def chunk_here(c):
                if c > loaded[0]:
                    pe.wait_ge(w_sem[c % NSLOT], chunk_value[c])
                    loaded[0] = c

            def banks_free(g):
                if g >= 2:
                    pe.wait_ge(sm["free_a"], g - 1)
                    pe.wait_ge(sm["free_b"], g - 1)

            def tile(g, rhs, m, ready=None):
                c, lhsT, _ = plan[g]
                banks_free(g)
                chunk_here(c)
                for k in range(KD):
                    if ready:
                        ready(k)
                    for half, bank in ((0, psA(g)), (1, psB(g))):
                        last = pe.matmul(bank[0:m, 0:H2], lhsT(k), rhs[:, k, half * H2:(half + 1) * H2],
                                         start=(k == 0), stop=(k == KD - 1))
                last.then_inc(sm["mm_done"], 1)

            def x_here(n_ln):
                return lambda k: pe.wait_ge(sm["x_ready"], KD * n_ln + k + 1)

            def split_tile(g, hi, lo, ready=None):
                u = split_of[g]
                banks_free(g)
                pe.wait_ge(sm["w_hi"], u + 1)
                pe.wait_ge(sm["w_lo"], u + 1)
                w_h, w_l = w_split(u)
                for k in range(KD):
                    if ready:
                        ready(k)
                    for n, (w, x) in enumerate(((w_h, hi), (w_h, lo), (w_l, hi))):
                        for half, bank in ((0, psA(g)), (1, psB(g))):
                            last = pe.matmul(bank[:, 0:H2], w[:, k, :], x[:, k, half * H2:(half + 1) * H2],
                                             start=(k == 0 and n == 0), stop=(k == KD - 1 and n == 2))
                last.then_inc(sm["mm_done"], 1)

            def x_split_here(layer):
                def ready(k):
                    pe.wait_ge(sm["x_ready"], 2 * KD * layer + k + 1)
                    if k in XL_POOL:
                        pe.wait_ge(sm["xl_p"], len(XL_POOL) * layer + XL_POOL.index(k) + 1)
                    else:
                        pe.wait_ge(sm["xl_v"], len(XL_DVE) * layer + XL_DVE.index(k) + 1)
                return ready

            def hidden_here(layer, c):
                def ready(k):
                    pe.wait_ge(sm["hid_hi"], KF * layer + KD * c + k + 1)
                    pe.wait_ge(sm["hid_lo"], KF * layer + KD * c + k + 1)
                return ready

            def mlp(layer, g):
                for c in range(NFC):
                    for j in range(KD):
                        split_tile(g, xh, xl, x_split_here(layer) if c == 0 and j == 0 else None)
                        g += 1
                    for j in range(KD):
                        split_tile(g, hh, hl, hidden_here(layer, c) if j == 0 else None)
                        g += 1

            def norm_sums(n_ln):
                pe.wait_ge(sm["sum_r"], KD * (n_ln + 1))
                for n, src in ((4, racc), (6, sacc)):
                    for half in range(2):
                        last = mm(ps[n + half][:, 0:H2], meanM[:, :], src[:, half * H2:(half + 1) * H2])
                last.then_inc(sm["stats_mm"], 1)

            pe.wait_ge(sm["consts_ok"], 3)
            pe.wait_ge(sm["x_in"], 32)
            for k in range(KD):
                if k >= 6:
                    pe.wait_ge(sm["tin_a"] if k % 2 == 0 else sm["tin_b"], (k - 6) // 2 + 1)
                for t in range(QT):
                    last = tr(ps[k % 6][:, P * t:P * t + P], xp_stage[:, t, P * k:P * k + P], P)
                last.then_inc(sm["tin"], 1)
            for k in range(KD):
                last = tr(ps[6][:, B * k:B * k + B], xs_stage[:, P * k:P * k + P], B)
            last.then_inc(sm["tin"], 1)
            pe.wait_ge(sm["cols_in"], 80)
            tr(ps[7][:, 0:112], stg, 112)
            pe.wait_ge(sm["small_in"], 16 * 10)
            for s in range(2):
                last = tr(ps[7][:, 112 + BLK * s:112 + BLK * (s + 1)], wcK[0:64, P * s:P * s + P], 64)
            last.then_inc(sm["tin"], 1)
            pe.wait_ge(sm["tin_a"], KD // 2)
            pe.wait_ge(sm["tin_b"], KD // 2 + 2)

            for idx in range(len(E_TILE)):
                tile(G_IN0 + idx, xT, 8 if idx == 0 else P)
                if idx == 2:
                    pe.wait_ge(sm["free_a"], 1)
                    pe.wait_ge(sm["free_b"], 1)
                    for half in range(2):
                        last = mm(ps[4 + half][0:4, 0:H2], ident[0:8, 4:8], gz[:, half * H2:(half + 1) * H2])
                    last.then_inc(sm["fg_mm"], 1)
                if idx == 12:
                    pe.wait_ge(sm["scs_in"], 16)
                    pe.wait_ge(sm["rows_ok"], 1)
                    for i in range(QT):
                        tr(ps[4][:, MH * i:MH * i + MH], at_[:, P * i:P * i + P], MH)
                    for h in range(MH):
                        mm(ps[5][:, 24 * h:24 * h + 24], sel[0:MH, h, :], eS[0:MH, :])
                    for i in range(4):
                        last = tr(ps[7][:, 16 * i:16 * i + 16], scs[:, P * i:P * i + P], 2 * B)
                    last.then_inc(sm["h12_mm"], 1)
                if idx == 14:
                    pe.wait_ge(sm["prod_ok"], 1)
                    mm(ps[4][:, 0:64], ones[:, :], prod).then_inc(sm["dots_mm"], 1)
                if idx in (16, 18, 20, 22):
                    h = (idx - 16) // 2
                    if h == 0:
                        pe.wait_ge(sm["nnew_ok"], 1)
                    else:
                        pe.wait_ge(sm["head_used"], h)
                    for n, t0 in ((4, 12), (6, 16)):
                        for b in range(B):
                            last = mm(ps[n + b // 4][:, P * (b % 4):P * (b % 4) + P],
                                      big[:, t0 + h, S + b:S + b + 1].to_broadcast([P, P]), ident[:, :])
                    last.then_inc(sm["head_mm"], 1)
                if idx == 25:
                    pe.wait_ge(sm["head_used"], MH)
                    tr(ps[4][0:MH * B, 0:P], nnw, P).then_inc(sm["nnew_mm"], 1)
                    pe.wait_ge(sm["u_ok"], 4)
                    for i in range(4):
                        last = tr(ps[5][0:B + 2, P * i:P * i + P], big[:, i, S - 2:T], P)
                    last.then_inc(sm["ucol_mm"], 1)

            pe.wait_ge(sm["free_a"], G_OUT0)
            pe.wait_ge(sm["free_b"], G_OUT0)
            pe.wait_ge(sm["nnew_ev"], 1)
            pe.wait_ge(sm["ucol_ev"], 1)
            pe.wait_ge(sm["c_new"], MH)
            for h in range(MH):
                if h:
                    pe.wait_ge(sm["wt_ok"], QT * h)
                mm(ps[0][:, :], sel[0:MH, h, :], rowsP[0:MH, 0:S]).then_inc(sm["pre_mm"], 1)
                if h:
                    pe.wait_ge(sm["hd_fin"], h)
                mm(ps[1][:, :], sel[0:MH, h, :], rowsP[0:MH, S:2 * S]).then_inc(sm["pre_mm"], 1)
                if h:
                    pe.wait_ge(sm["vt_ok"], h)
                    pe.wait_ge(sm["kt_ok"], h)
                for n, t0 in ((2, 20), (3, 16)):
                    for i in range(QT):
                        last = tr(ps[n][:, P * i:P * i + P], big[:, t0 + h, P * i:P * i + P], P)
                    last.then_inc(sm["pre_mm"], 1)
                if h:
                    pe.wait_ge(sm["cn_ev"], 2 * h)
                for i in range(QT + 1):
                    if i < QT:
                        if i >= 2:
                            pe.wait_ge(sm["p_raw"], QT * h + i - 1)
                        mm(ps[4 + i % 2][:, 0:S - P * i], big[:, 16 + h, P * i:P * i + P],
                           big[:, 12 + h, P * i:S]).then_inc(sm["s_mm"], 1)
                    if i >= 1:
                        j = i - 1
                        pe.wait_ge(sm["p_ok"], QT * h + j + 1)
                        if j == 0:
                            pe.wait_ge(sm["vt_ok"], h + 1)
                        pp = Pt[:, OFF[j]:OFF[j] + S - P * j]
                        mm(ps[6][:, P * j:S], ones[:, :], pp, start=(j == 0), stop=(j == QT - 1))
                        mm(ps[7][:, P * j:S], vtm[:, P * j:P * j + P], pp, start=(j == 0),
                           stop=(j == QT - 1)).then_inc(sm["pv_mm"], 1)
                pe.wait_ge(sm["vw_ok"], h + 1)
                pe.wait_ge(sm["kt_ok"], h + 1)
                for j in range(QT):
                    last = mm(ps[4][:, 0:P], vw[:, P * j:P * j + P], ktm[:, P * j:P * j + P], start=(j == 0),
                              stop=(j == QT - 1))
                last.then_inc(sm["cn_mm"], 1)
                for j in range(QT):
                    last = mm(ps[5][0:1, 0:P], wsc[:, j:j + 1], ktm[:, P * j:P * j + P], start=(j == 0),
                              stop=(j == QT - 1))
                last.then_inc(sm["cn_mm"], 1)

            def y_here(layer):
                return lambda k: pe.wait_ge(sm["y_split"], KD * layer + k + 1)

            for j in range(KD):
                split_tile(G_OUT0 + j, xh, xl, y_here(0) if j == 0 else None)
            pe.wait_ge(sm["cn_ev"], 2 * MH)
            norm_sums(0)
            mlp(0, G_MLP0)
            norm_sums(1)

            for idx, name in enumerate(O_NAMES):
                tile(G_IN1 + idx, xT, 60 if name == "misc" else P, x_here(1) if idx == 0 else None)
                if 4 <= idx <= 6:
                    n = idx - 4
                    i = 3 - n
                    g = G_IN1 + Z["qi"]
                    pe.wait_ge(sm["free_a"], g + 1)
                    pe.wait_ge(sm["free_b"], g + 1)
                    pe.wait_ge(sm["kiz_ok"], 4)
                    for e in range(4):
                        if n:
                            pe.wait_ge(sm["isc_r"], 4 * (n - 1) + e + 1)
                        mm(ps[4 + e][:, 0:P * (i + 1)], big[:, L["qi"], P * i:P * i + P],
                           kiz[:, e, 0:P * (i + 1)]).then_inc(sm["isc_mm"], 1)
                if idx == 3:
                    pe.wait_ge(sm["free_a"], G_IN1 + 1)
                    pe.wait_ge(sm["free_b"], G_IN1 + 1)
                    for i in range(QT):
                        tr(ps[4][:, 60 * i:60 * i + 60], big[0:60, L["misc"], P * i:P * i + P], 60)
                    tr(ps[5][0:B, 0:60], big[0:60, L["misc"], S:T], 60).then_inc(sm["t1_mm"], 1)
                    pe.wait_ge(sm["t1_ev"], 1)
                    mm(ps[6][0:64, 0:60], selB[0:B, :], mts[0:B, :])
                    mm(ps[7][0:32, 0:60], selE[0:B, :], mts[0:B, :]).then_inc(sm["sel_mm"], 1)
                    pe.wait_ge(sm["sel_ev"], 1)

            pe.wait_ge(sm["free_a"], G_OUT1)
            pe.wait_ge(sm["free_b"], G_OUT1)
            pe.wait_ge(sm["isc_r"], 12)
            for s, name in enumerate(SLOTS):
                if s >= 4:
                    pe.wait_ge(sm["tm_a"] if s % 2 == 0 else sm["tm_b"], (s - 4) // 2 + 1)
                for i in range(QT):
                    last = tr(ps[s % 4][:, P * i:P * i + P], big[:, L[name], P * i:P * i + P], P)
                last.then_inc(sm["tm_mm"], 1)
            for s, name in enumerate(SLOTS):
                last = tr(ps[4 + s // 4][0:B, P * (s % 4):P * (s % 4) + P], big[:, L[name], S:T], P)
            last.then_inc(sm["tms_mm"], 1)
            pe.wait_ge(sm["tm_a"], 4)
            pe.wait_ge(sm["tm_b"], 4)
            pe.wait_ge(sm["tms_ev"], 2)

            def cached_keys(st, n0, lhs_of, src_of, key_rows, acc_rows):
                if 0 <= st < 4:
                    if n0 + st:
                        pe.wait_ge(sm["bt_ev"], n0 + st)
                    for b in range(2):
                        for t in range(2):
                            last = tr(ps[4][0:key_rows, 256 * b + P * t:256 * b + P * t + P], src_of(2 * (2 * st + b) + t), P)
                    last.then_inc(sm["bt_mm"], 1)
                if 1 <= st <= 4:
                    pe.wait_ge(sm["bt_ev"], n0 + st)
                    for b in range(2):
                        bb = 2 * (st - 1) + b
                        last = mm(ps[7][0:acc_rows, 0:LS], lhs_of(bb), kTs[(st - 1) % 2][0:key_rows, b, :],
                                  start=(bb == 0), stop=(bb == B - 1))
                    last.then_inc(sm["bs_mm"], 1)

            def new_col(j, col):
                return mm(ps[7][:, 64 * j:64 * j + 64], col.to_broadcast([64, P]), ident[0:64, 0:64])

            def sample_step(k):
                if k == 0:
                    pe.wait_ge(gat[4], 16 * NT)
                    pe.wait_ge(sm["qb_ok"], 1)
                if k <= 4:
                    cached_keys(k, 0, lambda b: QI[0:32, 32 * b:32 * b + 32], lambda t: kidx[:, t, :], 32, 32)
                if k == 5:
                    pe.wait_ge(sm["ix_r"], 1)
                    mm(ps[7][0:B, 0:LS], WI[0:32, :], rS).then_inc(sm["ixc_mm"], 1)
                if k == 9:
                    pe.wait_ge(sm["dsb_in"], 1)
                    mm(ps[7][0:64, 0:LS], selB[0:B, :], iscS).then_inc(sm["dsb_mm"], 1)
                if k == 5:
                    pe.wait_ge(sm["cw_ok"], 1)
                    pe.wait_ge(sm["bt_ev"], 4)
                    for t in range(NT):
                        last = mm(ps[4][0:32, 0:256], BS[:, 30 - 2 * t:62 - 2 * t], cache["c"][:, t, :],
                                  start=(t == 0), stop=(t == NT - 1))
                    last.then_inc(sm["cmp_mm"], 1)
                if k == 6:
                    pe.wait_ge(sm["cmp_ev"], 1)
                    for s in range(2):
                        last = tr(ps[4][:, 256 + 32 * s:288 + 32 * s], cmps[0:32, P * s:P * s + P], 32)
                    last.then_inc(sm["cmpt_mm"], 1)
                if k == 7:
                    pe.wait_ge(sm["cmpt_ev"], 1)
                    pe.wait_ge(sm["ixs_ev"], 1)
                    pe.wait_ge(sm["qb_ok"], 3)
                    for b in range(B):
                        last = mm(ps[7][0:64, 0:NBS], QB["n"][:, 64 * b:64 * b + 64], kcTs[:, NBS * b:NBS * (b + 1)],
                                  start=(b == 0), stop=(b == B - 1))
                    last.then_inc(sm["bs_mm"], 1)
                if k == 10:
                    pe.wait_ge(sm["pn_ok"], 1)
                    pe.wait_ge(sm["dsd_ev"], 1)
                    for j in range(NBS):
                        last = new_col(j, sc4[0:64, j:j + 1])
                    last.then_inc(sm["pb_mm"], 1)
                for x, (br, (base, n0, where, q, n)) in enumerate(STEP.items()):
                    cb = cache[where]
                    if base <= k <= base + 4:
                        if k == base:
                            pe.wait_ge(gat[n], 16 if br == "w" else 16 * NT)
                        if k == base + 1:
                            pe.wait_ge(sm["pb_ev"], x + 1)
                        cached_keys(k - base, n0, lambda b, q=q: QB[q][:, 64 * b:64 * b + 64],
                                    lambda t, cb=cb: cb[:, t, 0:P], P, 64)
                    if k == base + 7:
                        pe.wait_ge(sm["pn_ok"], x + 2)
                        for t in range(2):
                            tr(ps[7][:, 64 * t:64 * t + 64], sbs[:, P * t:P * t + P], 64)
                        new_col(2, sbs[:, PAST:LS]).then_inc(sm["pt_mm"], 1)
                    if k == base + 8:
                        pe.wait_ge(sm["pt_ev"], x + 1)
                        for b in range(B):
                            for t in range(2):
                                last = mm(ps[7][:, 192 + 8 * b:200 + 8 * b], cb[:, 2 * b + t, P:2 * P],
                                          PTs[:, t, 8 * b:8 * b + 8], start=(b == 0 and t == 0), stop=True)
                        last.then_inc(sm["pvs_mm"], 1)

            pe.wait_ge(sm["kc_ok"], 1)
            for i in range(QT):
                for p in range(NP):
                    last = mm(ps[7][:, 64 * i + 16 * p:64 * i + 16 * p + 16], big[:, L["qn0"] + p, P * i:P * i + P], KCZ)
            last.then_inc(sm["pc_mm"], 1)
            for p in range(NP):
                last = tr(ps[4][0:64, P * p:P * p + P], VF[:, p, :], P)
            last.then_inc(sm["vf_mm"], 1)
            pe.wait_ge(sm["pc_n"], 1)
            for i in range(QT):
                last = tr(ps[5][0:64, P * i:P * i + P], sc[:, 64 * i:64 * i + 64], P)
            last.then_inc(sm["pct_mm"], 1)
            pe.wait_ge(sm["pct_ev"], 1)
            pe.wait_ge(sm["vf_ev"], 1)

            VS = {"s": SLOTS.index("vs"), "w": SLOTS.index("vw"), "d": SLOTS.index("vd")}
            for t in range(len(units) + 3):
                if t < len(units):
                    i, p, g, br, k0, o = units[t]
                    if t >= 2:
                        pe.wait_ge(sm["q_sc"], t - 1)
                    if t == 0:
                        pe.wait_ge(sm["kz_ok"], 6)
                    qn = "qd0" if br == "d" else "qn0"
                    mm(ps[t % 2][:, 0:P * (i + 1 - k0)], big[:, L[qn] + p, P * i:P * i + P],
                       KZ["k" + br][:, g, P * k0:P * (i + 1)]).then_inc(sm["q_mm"], 1)
                    if t >= START and (t - START) % EVERY == 0:
                        sample_step((t - START) // EVERY)
                u = t - 2
                if 0 <= u < len(units):
                    i, p, g, br, k0, o = units[u]
                    pe.wait_ge(sm["q_n"], u + 1)
                    if u >= 2:
                        pe.wait_ge(sm["q_te"], u - 1)
                    for b in range(i + 1 - k0):
                        last = tr(ps[2 + u % 2][:, P * b:P * b + P], Pb[u % 2][:, P * b:P * b + P], P)
                    last.then_inc(sm["q_t"], 1)
                u = t - 3
                if 0 <= u < len(units):
                    i, p, g, br, k0, o = units[u]
                    acc = ps[5 + o % 2]
                    if u == first_of[(o, 0)]:
                        if o >= 2:
                            pe.wait_ge(sm["q_of"], o - 1)
                        if br != "d":
                            mm(acc[:, 0:P], VCb[:, p, :], PcT[:, P * i:P * i + P], stop=False)
                    pe.wait_ge(sm["q_te"], u + 1)
                    for b in range(i + 1 - k0):
                        v = tm[:, k0 + b, P * VS[br] + HD * g:P * VS[br] + HD * g + HD]
                        last = mm(acc[HD * g:HD * g + HD, 0:P], v, PTb[u % 2][:, P * b:P * b + P],
                                  start=(br == "d" and b == 0), stop=(b == i - k0))
                    last.then_inc(sm["q_o"], 1)

            for j in range(KD):
                split_tile(G_OUT1 + j, xh, xl, y_here(1) if j == 0 else None)
            norm_sums(2)
            mlp(1, G_MLP1)
            norm_sums(3)

            pe.wait_ge(sm["x_ready"], 4 * KD)
            for n in range(2 * QT + 2):
                i, half = divmod(n, 2)
                if n >= 4:
                    pe.wait_ge(sm["y_a"] if n % 2 == 0 else sm["y_b"], (n - 4) // 2 + 1)
                m = P if i < QT else B
                for k in range(4):
                    last = tr(ps[n % 4][0:m, P * k:P * k + P], xT[:, 4 * half + k, P * i:P * i + m], P)
                last.then_inc(sm["y_mm"], 1)

        @block.scalar
        def _(act):
            link = chain(act, sm["act_step"])
            one = ones[:, 0:1]

            def copy(out, in_, scale=1.0):
                return act.activation(out, in_, ACT.Copy, scale=scale)

            def tile_done(g):
                act.wait_ge(sm["mm_done"], g + 1)

            def w_hi(u, extra=None):
                c = plan[split[u]][0]
                act.wait_ge(w_sem[c % NSLOT], chunk_value[c])
                if extra:
                    act.wait_ge(sm[extra[0]], extra[1])
                elif u % NS1 >= NW:
                    tile_done(split[u - NW])
                copy(w_split(u)[0], w_raw(u)).then_inc(sm["w_hi"], 1)

            def w_hi_ahead(g):
                if (split_of[g] + NW) // NS1 == split_of[g] // NS1:
                    w_hi(split_of[g] + NW)

            def squares(n_ln, g0):
                for m in range(KD):
                    act.wait_ge(sm["free_a"], g0 + m + 1)
                    act.wait_ge(sm["free_b"], g0 + m + 1)
                    if m >= 2:
                        act.wait_ge(sm["sum_r"], KD * n_ln + m - 1)
                    act.activation(sq[m % 2], xT[:, m, :], ACT.Square).then_inc(sm["sq_done"], 1)
                    w_hi_ahead(g0 + m)

            def mlp(layer, g):
                for c in range(NFC):
                    for j in range(KD):
                        n = KF * layer + KD * c + j
                        tile_done(g)
                        if n >= 2:
                            act.wait_ge(sm["hid_sq"], n - 1)
                            act.wait_ge(sm["hid_hi"], n - 1)
                        act.activation(rel[j % 2][:, 0:H2], psA(g)[:, 0:H2], ACT.Relu).then_inc(sm["free_a"], 1)
                        w_hi_ahead(g)
                        act.wait_ge(sm["free_a"], g + 1)
                        act.wait_ge(sm["free_b"], g + 1)
                        act.activation(hh[:, j, :], rel[j % 2], ACT.Square).then_inc(sm["hid_hi"], 1)
                        g += 1
                    if c < NFC - 1:
                        for j in range(KD):
                            w_hi_ahead(g)
                            g += 1
                    else:
                        squares(2 * layer + 1, g)

            def norm(n_ln):
                act.wait_ge(sm["std_in"], n_ln + 1)
                act.activation(rs, var, ACT.Sqrt).then_inc(sm["stats_ok"], 1)
                nv = KD - len(LN_POOL)
                v = q = 0

                def affine(out, m):
                    return act.activation(out[:, m, :], xT[:, m, :], ACT.Identity, scale=colT[:, KD * n_ln + m:KD * n_ln + m + 1],
                                          bias=colT[:, 32 + KD * n_ln + m:33 + KD * n_ln + m])

                for m in range(KD):
                    if m in LN_POOL:
                        q += 1
                        act.wait_ge(sm["cen_p"], len(LN_POOL) * n_ln + q)
                    else:
                        v += 1
                        act.wait_ge(sm["cen_v"], nv * n_ln + v)
                    if n_ln % 2 == 0:
                        affine(xh, m).then_inc(sm["x_hi"], 1)
                        act.wait_ge(sm["x_hi"], KD * (n_ln // 2) + m + 1)
                    affine(xT, m).then_inc(sm["x_ready"], 1)

            for k in range(0, KD, 2):
                act.wait_ge(sm["tin"], k + 1)
                copy(xT[:, k, 0:S], ps[k % 6][:, :]).then_inc(sm["tin_a"], 1)

            for idx, t in enumerate(E_TILE):
                g = G_IN0 + idx
                tile_done(g)
                if idx == 0:
                    act.wait_ge(sm["small_in"], 16 * 10)
                    act.activation(gz[:, 0:H2], psA(g)[0:8, 0:H2], ACT.Identity, bias=gbc[0:8, :]).then_inc(sm["free_a"], 1)
                else:
                    copy(big[:, t, 0:H2], psA(g)[:, 0:H2], MH_SCALE if 16 <= t < 20 else 1.0).then_inc(sm["free_a"], 1)
                if idx == 2:
                    act.wait_ge(sm["nx_ok"], 1)
                    link(act.activation(lg, nx, ACT.Exp))
                    act.activation(lg, lg, ACT.Ln, bias=one[0:4, :]).then_inc(sm["sg_e"], 1)
                    act.wait_ge(sm["sp_ok"], 1)
                    act.activation(rowsP[0:MH, S:2 * S], nG, ACT.Exp)
                    act.activation(eS[0:MH, :], rowsS[0:MH, :], ACT.Exp).then_inc(sm["rows_ok"], 1)
                if idx >= 25:
                    act.wait_ge(sm["free_a"], g + 1)
                    act.wait_ge(sm["free_b"], g + 1)
                    act.activation(big[:, t, :], big[:, t, :], ACT.Exp, scale=-1.0).then_inc(sm["sg_e"], 1)
            act.wait_ge(sm["nnew_mm"], 1)
            copy(nno[0:MH * B, :], ps[4][0:MH * B, 0:P]).then_inc(sm["nnew_ev"], 1)
            act.wait_ge(sm["ucol_mm"], 1)
            copy(uo[0:B + 2, :], ps[5][0:B + 2, :]).then_inc(sm["ucol_ev"], 1)
            for h in range(MH):
                act.wait_ge(sm["pre_mm"], 4 * h + 1)
                if h:
                    act.wait_ge(sm["ws_ok"], h)
                link(copy(nml, ps[0][:, S - 1:S]))
                for i in range(QT):
                    if h:
                        act.wait_ge(sm["p_raw"], QT * (h - 1) + i + 1)
                    act.activation(Wt[:, OFF[i]:OFF[i] + S - P * i], ps[0][:, P * i:S], ACT.Exp,
                                   bias=aT[:, MH * i + h:MH * i + h + 1]).then_inc(sm["wt_ok"], 1)
                if h:
                    act.wait_ge(sm["cn_mm"], 2 * h)
                act.activation(wsc, aT.rearrange("p (i h) -> p i h", h=MH)[:, :, h], ACT.Exp, bias=nml).then_inc(sm["ws_ok"], 1)
                act.wait_ge(sm["pre_mm"], 4 * h + 4)
                copy(ktm, ps[3][:, :]).then_inc(sm["kt_ok"], 1)
                for n, (dst, src) in enumerate(((cst, ps[4][:, 0:P]), (nrow[0:1, :], ps[5][0:1, 0:P]))):
                    act.wait_ge(sm["cn_mm"], 2 * h + n + 1)
                    if h:
                        act.wait_ge(sm["store_c"], 16 * (MH + 2 * h))
                    copy(dst, src).then_inc(sm["cn_ev"], 1)
                if h == 2:
                    for u in range(2):
                        w_hi(u, ("store_c", 16 * (MH + 2 * h)))
            for u in range(2, NW):
                w_hi(u, ("y_split", KD))
            squares(0, G_OUT0)
            norm(0)
            mlp(0, G_MLP0)
            norm(1)

            for idx, name in enumerate(O_NAMES):
                g = G_IN1 + idx
                tile_done(g)
                m = 60 if name == "misc" else P
                copy(big[0:m, L[name], 0:H2], psA(g)[0:m, 0:H2], 0.125 if name[:2] in ("qn", "qd") else 1.0).then_inc(sm["free_a"], 1)
                if idx == 3:
                    act.wait_ge(sm["gate_e"], 1)
                    act.activation(gt[:, :, :], gt[:, :, :], ACT.Exp, scale=-1.0)
                    act.activation(gS[0:64, :], gS[0:64, :], ACT.Exp, scale=-1.0).then_inc(sm["gate_e"], 1)
                if 4 <= idx <= 6:
                    n = idx - 4
                    i = 3 - n
                    for e in range(4):
                        act.wait_ge(sm["isc_mm"], 4 * n + e + 1)
                        if 4 * n + e >= 2:
                            act.wait_ge(sm["isc_used"], 4 * n + e - 1)
                        act.activation(rl[e % 2][:, 0:P * (i + 1)], ps[4 + e][:, 0:P * (i + 1)], ACT.Relu,
                                       scale=IDX_SCALE).then_inc(sm["isc_r"], 1)
            for s in range(0, 8, 2):
                act.wait_ge(sm["tm_mm"], s + 1)
                copy(tm[:, :, P * s:P * s + P], ps[s % 4][:, :].rearrange("p (i c) -> p i c", i=QT)).then_inc(sm["tm_a"], 1)
            act.wait_ge(sm["tms_mm"], 1)
            for n in range(2):
                copy(tms[:, 512 * n:512 * n + 512], ps[4 + n][0:B, :]).then_inc(sm["tms_ev"], 1)

            def cached_keys(st, n0, newkey, m=P):
                x = n0 + st
                act.wait_ge(sm["bt_mm"], x + 1)
                if x >= 2:
                    act.wait_ge(sm["bs_mm"], x - 1 + (1 if x >= 6 else 0))
                copy(kTs[st % 2][0:m, :, 0:PAST], ps[4][0:m, :].rearrange("p (b k) -> p b k", b=2))
                copy(kTs[st % 2][0:m, :, PAST:LS], big[0:m, L[newkey], S + 2 * st:S + 2 * st + 2].rearrange("p (b o) -> p b o", o=1)).then_inc(sm["bt_ev"], 1)

            def exponentials(dst, n):
                act.wait_ge(sm["sc_ok"], n + 1)
                act.activation(dst, dst, ACT.Exp, bias=nms[0:64, :], accum_out=rss[0:64, :]).then_inc(sm["pe_ok"], 1)

            def sample_step(k):
                if k < 4:
                    cached_keys(k, 0, "ki4", 32)
                if k == 4:
                    act.wait_ge(sm["bs_mm"], 4)
                    act.activation(rS, ps[7][0:32, 0:LS], ACT.Relu, scale=IDX_SCALE).then_inc(sm["ix_r"], 1)
                if k == 8:
                    exponentials(sc4[0:64, :], 0)
                for x, (br, (base, n0, *_)) in enumerate(STEP.items()):
                    if base <= k < base + 4:
                        cached_keys(k - base, n0, "k" + br)
                    if k == base + 5:
                        exponentials(sbs, x + 1)

            act.wait_ge(sm["pc_x"], 1)
            act.activation(sc, sc, ACT.Exp).then_inc(sm["pc_e"], 1)
            act.wait_ge(sm["pct_mm"], 1)
            copy(PcT, ps[5][0:64, :]).then_inc(sm["pct_ev"], 1)

            for t in range(len(units) + 2):
                if t < len(units):
                    i, p, g, br, k0, o = units[t]
                    n = P * (i + 1 - k0)
                    act.wait_ge(sm["q_sc"], 0 + t + 1)
                    act.wait_ge(sm["q_m"], t + 1)
                    if t >= 2:
                        act.wait_ge(sm["q_t"], t - 1)
                    act.activation(Pb[t % 2][:, 0:n], sbb[t % 2][:, 0:n], ACT.Exp, bias=nmx[t % 2],
                                   accum_out=rsum[t % 2]).then_inc(sm["q_e"], 1)
                u = t - 2
                if u >= 0:
                    i, p, g, br, k0, o = units[u]
                    n = P * (i + 1 - k0)
                    act.wait_ge(sm["q_t"], u + 1)
                    if u >= 2:
                        act.wait_ge(sm["q_o"], u - 1)
                    copy(PTb[u % 2][:, 0:n], ps[2 + u % 2][:, 0:n]).then_inc(sm["q_te"], 1)
                if t >= START and (t - START) % EVERY == EVERY - 1:
                    sample_step((t - START) // EVERY)
                if t == EARLY:
                    for u in range(NS1, NS1 + 2):
                        w_hi(u, ("q_of", 16))
            for u in range(NS1 + 2, NS1 + NW):
                w_hi(u, ("y_split", 2 * KD))
            squares(2, G_OUT1)
            norm(2)
            mlp(1, G_MLP1)
            norm(3)
            for n in range(0, 2 * QT + 2, 2):
                i = n // 2
                m = P if i < QT else B
                act.wait_ge(sm["y_mm"], n + 1)
                copy(ytm[0:m, i, 0:512], ps[n % 4][0:m, :]).then_inc(sm["y_a"], 1)

        @block.vector
        def _(dve):
            link = chain(dve, sm["dve_step"])

            def tile_done(g):
                dve.wait_ge(sm["mm_done"], g + 1)

            def w_lo(u):
                dve.wait_ge(sm["w_hi"], u + 1)
                w_h, w_l = w_split(u)
                dve.tensor_tensor(w_l, w_raw(u), w_h.bitcast(F32), ALU.subtract).then_inc(sm["w_lo"], 1)

            def w_lo_ahead(g):
                if (split_of[g] + NW) // NS1 == split_of[g] // NS1:
                    w_lo(split_of[g] + NW)

            def residual(g0, scale=ALPHA):
                for m in range(KD):
                    g = g0 + m
                    tile_done(g)
                    for c0, bank, free in ((0, psA(g), "free_a"), (H2, psB(g), "free_b")):
                        x = xT[:, m, c0:c0 + H2]
                        last = (dve.tensor_tensor(x, x, bank[:, 0:H2], ALU.add) if scale is None
                                else dve.scalar_tensor_tensor(x, x, scale, bank[:, 0:H2], ALU.mult, ALU.add))
                        last.then_inc(sm[free], 1)
                    w_lo_ahead(g)

            def mlp(layer, g):
                for n, m in enumerate(XL_DVE):
                    dve.wait_ge(sm["x_ready"], 2 * KD * layer + m + 1)
                    dve.tensor_tensor(xl[:, m, :], xT[:, m, :], xh[:, m, :].bitcast(F32), ALU.subtract).then_inc(sm["xl_v"], 1)
                for c in range(NFC):
                    for j in range(KD):
                        n = KF * layer + KD * c + j
                        tile_done(g)
                        if n >= 2:
                            dve.wait_ge(sm["hid_sq"], n - 1)
                            dve.wait_ge(sm["hid_hi"], n - 1)
                        dve.tensor_scalar(rel[j % 2][:, H2:T], psB(g)[:, 0:H2], 0.0, None, ALU.max).then_inc(sm["free_b"], 1)
                        w_lo_ahead(g)
                        dve.wait_ge(sm["hid_sq"], n + 1)
                        dve.wait_ge(sm["hid_hi"], n + 1)
                        dve.tensor_tensor(hl[:, j, :], hid[j % 2], hh[:, j, :].bitcast(F32), ALU.subtract).then_inc(sm["hid_lo"], 1)
                        g += 1
                    residual(g, ALPHA if c == 0 else None)
                    g += KD

            def norm(n_ln):
                dve.wait_ge(sm["stats_mm"], n_ln + 1)
                dve.tensor_copy(mu[:, 0:H2], ps[4][:, 0:H2])
                link(dve.tensor_copy(mu[:, H2:T], ps[5][:, 0:H2]))
                link(dve.tensor_tensor(var, mu, mu, ALU.mult))
                dve.tensor_tensor(var[:, 0:H2], ps[6][:, 0:H2], var[:, 0:H2], ALU.subtract)
                link(dve.tensor_tensor(var[:, H2:T], ps[7][:, 0:H2], var[:, H2:T], ALU.subtract))
                dve.tensor_scalar(var, var, 0.0, LN_EPS, ALU.max, ALU.add).then_inc(sm["std_in"], 1)
                dve.wait_ge(sm["stats_ok"], n_ln + 1)
                dve.reciprocal(rs, rs).then_inc(sm["std_ok"], 1)
                dve.wait_ge(sm["std_ok"], n_ln + 1)
                for m in range(KD):
                    if m not in LN_POOL:
                        link(dve.tensor_tensor(xT[:, m, :], xT[:, m, :], mu, ALU.subtract))
                        dve.tensor_tensor(xT[:, m, :], xT[:, m, :], rs, ALU.mult).then_inc(sm["cen_v"], 1)

            for k in range(1, KD, 2):
                dve.wait_ge(sm["tin"], k + 1)
                dve.tensor_copy(xT[:, k, 0:S], ps[k % 6][:, :]).then_inc(sm["tin_b"], 1)
            dve.wait_ge(sm["tin"], KD + 1)
            dve.tensor_copy(xT[:, :, S:T], ps[6][:, 0:KD * B].rearrange("p (k b) -> p k b", k=KD)).then_inc(sm["tin_b"], 1)
            dve.wait_ge(sm["tin"], KD + 2)
            dve.tensor_copy(colT[:, :], ps[7][:, 0:112])
            dve.tensor_copy(wcT, ps[7][:, 112:240]).then_inc(sm["tin_b"], 1)
            dve.wait_ge(sm["tin_b"], KD // 2 + 2)

            def bc(kind):
                return bcS.rearrange("p (h k b) -> p h k b", h=MH, k=3)[:, :, kind, :]

            def hb(v):
                return v.rearrange("p (h b) -> p h b", h=MH)

            def gates():
                dve.wait_ge(sm["fg_mm"], 1)
                dve.tensor_copy(fgt[:, 0:H2], ps[4][0:4, 0:H2])
                link(dve.tensor_copy(fgt[:, H2:T], ps[5][0:4, 0:H2]))
                dve.scalar_tensor_tensor(nx, fgt, -1.0, fgt, ALU.mult, ALU.min).then_inc(sm["nx_ok"], 1)
                dve.wait_ge(sm["sg_e"], 1)
                link(dve.scalar_tensor_tensor(lg, fgt, 0.0, lg, ALU.min, ALU.subtract))
                link(dve.tensor_tensor_scan(Fc, ones[0:4, 0:1].to_broadcast([4, S]), lg[:, 0:S], 0.0, ALU.mult, ALU.add))
                dve.wait_ge(sm["free_a"], 1)
                link(dve.tensor_tensor(at_, gz[0:4, 0:S], Fc, ALU.subtract))
                link(dve.tensor_tensor_scan(Mr, at_, at_, 0.0, ALU.max, ALU.max))
                dve.tensor_scalar(rowsP[0:MH, 0:S], Mr, -1.0, None, ALU.mult)
                link(dve.scalar_tensor_tensor(nG, Fc, -1.0, Mr, ALU.mult, ALU.subtract))
                dve.tensor_scalar(mpc[0:MH, :], nG[:, S - 1:S], -1.0, None, ALU.mult)
                link(dve.tensor_tensor(interS[0:MH, :], lg[:, S:T], stm[0:MH, :], ALU.add))
                link(dve.tensor_tensor(mtS[0:MH, :], interS[0:MH, :], gz[0:4, S:T], ALU.max))
                dve.tensor_tensor(rowsS[0:MH, 0:B], interS[0:MH, :], mtS[0:MH, :], ALU.subtract)
                dve.tensor_tensor(rowsS[0:MH, B:2 * B], gz[0:4, S:T], mtS[0:MH, :], ALU.subtract)
                dve.tensor_scalar(rowsS[0:MH, 2 * B:3 * B], mtS[0:MH, :], -1.0, None, ALU.mult).then_inc(sm["sp_ok"], 1)

            def sample_products():
                dve.wait_ge(sm["h12_mm"], 1)
                dve.tensor_copy(aT, ps[4][:, 0:16])
                dve.tensor_copy(bcS, ps[5][:, 0:96])
                dve.tensor_copy(scT, ps[7][:, 0:64])
                dve.wait_ge(sm["free_b"], 13)
                n_hb = colT[:, 80:112].rearrange("p (b h) -> p h b", h=MH)
                dve.tensor_tensor(hb(prod[:, 0:32]), n_hb, big[:, 12:16, S:T], ALU.mult)
                dve.tensor_tensor(hb(prod[:, 32:64]), big[:, 16:20, S:T], big[:, 12:16, S:T],
                                  ALU.mult).then_inc(sm["prod_ok"], 1)

            def sample_weights():
                n_hb = colT[:, 80:112].rearrange("p (b h) -> p h b", h=MH)
                nn_hb = nnw.rearrange("p (b h) -> p h b", h=MH)
                dve.wait_ge(sm["dots_mm"], 1)
                link(dve.tensor_copy(dts, ps[4][:, 0:64]))
                dve.tensor_tensor(hb(swa), hb(dts[:, 32:64]), bc(1), ALU.mult)
                link(dve.tensor_tensor(hb(recS), hb(dts[:, 0:32]), bc(0), ALU.mult))
                link(dve.tensor_tensor(recS, recS, swa, ALU.add))
                link(dve.scalar_tensor_tensor(recS, recS, -1.0, recS, ALU.mult, ALU.max))
                link(dve.tensor_tensor(hb(recS), hb(recS), bc(2), ALU.max))
                dve.reciprocal(recS, recS)
                dve.tensor_tensor(nn_hb, n_hb, bc(0), ALU.mult)
                link(dve.tensor_tensor(hb(vwS), big[:, 16:20, S:T], bc(1), ALU.mult))
                link(dve.tensor_tensor(nn_hb, nn_hb, hb(vwS), ALU.add))
                dve.tensor_tensor(hb(vwS), big[:, 20:24, S:T], bc(1), ALU.mult).then_inc(sm["nnew_ok"], 1)
                dve.wait_ge(sm["nnew_ok"], 1)

            def sample_head(h):
                def bd(bank):
                    return bank[:, :].rearrange("p (b d) -> p b d", b=4)
                dve.wait_ge(sm["head_mm"], h + 1)
                if h == 0:
                    dve.wait_ge(sm["c_in"], 16 * MH)
                for j in range(2):
                    last = dve.tensor_tensor(tmpS[:, 4 * j:4 * j + 4, :], Ct[:, h, 4 * j:4 * j + 4, :], bd(ps[4 + j]), ALU.mult)
                link(last)
                dve.tensor_reduce(cq[:, B * h:B * h + B], tmpS, AX.X, ALU.add)
                link(dve.tensor_tensor(Ct[:, h], Ct[:, h], bc(0)[:, h, :].unsqueeze(2).to_broadcast([P, B, P]), ALU.mult))
                for j in range(2):
                    v = vwS[:, B * h + 4 * j:B * h + 4 * j + 4]
                    last = dve.tensor_tensor(tmpS[:, 4 * j:4 * j + 4, :], bd(ps[6 + j]), v.unsqueeze(2).to_broadcast([P, 4, P]), ALU.mult)
                last.then_inc(sm["head_used"], 1)
                dve.wait_ge(sm["head_used"], h + 1)
                dve.tensor_tensor(Ct[:, h], Ct[:, h], tmpS, ALU.add).then_inc(sm["c_new"], 1)
                dve.wait_ge(sm["c_new"], h + 1)

            def convolve(i):
                def w(j):
                    return colT[:, 64 + 4 * j + i:65 + 4 * j + i]
                u, y = big[:, i, :], ymix[:, i, :]
                old = scT.rearrange("p (c b j) -> p c b j", c=4, b=B)[:, i]
                dve.wait_ge(sm["u_ok"], i + 1)
                dve.wait_ge(sm["free_a"], G_IN0 + 22 + i)
                link(dve.tensor_scalar(y, u, w(2), colT[:, 76 + i:77 + i], ALU.mult, ALU.add))
                dve.scalar_tensor_tensor(y[:, 1:S], u[:, 0:S - 1], w(1), y[:, 1:S], ALU.mult, ALU.add)
                link(dve.scalar_tensor_tensor(y[:, S:T], old[:, :, 1], w(1), y[:, S:T], ALU.mult, ALU.add))
                dve.scalar_tensor_tensor(y[:, 2:S], u[:, 0:S - 2], w(0), y[:, 2:S], ALU.mult, ALU.add)
                link(dve.scalar_tensor_tensor(y[:, S:T], old[:, :, 0], w(0), y[:, S:T], ALU.mult, ALU.add))
                dve.tensor_tensor(y, y, big[:, 4 + i, :], ALU.mult).then_inc(sm["conv_ok"], 1)

            for idx, t in enumerate(E_TILE):
                g = G_IN0 + idx
                tile_done(g)
                if idx == 0:
                    dve.wait_ge(sm["small_in"], 16 * 10)
                    dve.tensor_scalar(gz[:, H2:T], psB(g)[0:8, 0:H2], gbc[0:8, :], None, ALU.add).then_inc(sm["free_b"], 1)
                    dve.wait_ge(sm["free_b"], 1)
                elif 16 <= t < 20:
                    dve.tensor_scalar(big[:, t, H2:T], psB(g)[:, 0:H2], MH_SCALE, None, ALU.mult).then_inc(sm["free_b"], 1)
                else:
                    dve.tensor_copy(big[:, t, H2:T], psB(g)[:, 0:H2]).then_inc(sm["free_b"], 1)
                if idx == 2:
                    gates()
                if idx == 12:
                    sample_products()
                if idx == 14:
                    sample_weights()
                if idx in (16, 18, 20, 22):
                    sample_head((idx - 16) // 2)
                if 21 <= idx <= 24:
                    dve.wait_ge(sm["free_b"], g + 1)
                    convolve(idx - 21)
                if idx >= 25:
                    dve.wait_ge(sm["sg_e"], idx - 23)
                    link(dve.tensor_scalar(big[:, t, :], big[:, t, :], 1.0, None, ALU.add))
                    link(dve.reciprocal(big[:, t, :], big[:, t, :]))
            dve.tensor_tensor(hb(hS), hb(cq), bc(0), ALU.mult)
            link(dve.tensor_tensor(hb(prod[:, 0:32]), big[:, 20:24, S:T], hb(swa), ALU.mult))
            link(dve.tensor_tensor(hS, hS, prod[:, 0:32], ALU.add))
            link(dve.tensor_tensor(hS, hS, recS, ALU.mult))
            dve.tensor_tensor(ymix[:, 4:8, S:T], hb(hS), big[:, 24:28, S:T], ALU.mult).then_inc(sm["smp_y"], 1)
            for h in range(MH):
                dve.wait_ge(sm["pre_mm"], 4 * h + 3)
                if h:
                    dve.wait_ge(sm["pv_mm"], QT * h)
                dve.tensor_copy(vtm, ps[2][:, :]).then_inc(sm["vt_ok"], 1)
                for i in range(QT):
                    dve.wait_ge(sm["s_mm"], QT * h + i + 1)
                    dve.wait_ge(sm["wt_ok"], QT * h + i + 1)
                    n = S - P * i
                    dve.tensor_tensor(Pt[:, OFF[i]:OFF[i] + n], ps[4 + i % 2][:, 0:n], Wt[:, OFF[i]:OFF[i] + n],
                                      ALU.mult).then_inc(sm["p_raw"], 1)
                dve.wait_ge(sm["ws_ok"], h + 1)
                dve.wait_ge(sm["vt_ok"], h + 1)
                if h:
                    dve.wait_ge(sm["cn_mm"], 2 * h)
                dve.tensor_tensor(vw.rearrange("p (i d) -> p i d", i=QT), vtm.rearrange("p (i d) -> p i d", i=QT),
                                  wsc.unsqueeze(2).to_broadcast([P, QT, P]), ALU.mult).then_inc(sm["vw_ok"], 1)
                dve.wait_ge(sm["pv_mm"], QT * h + QT)
                link(dve.tensor_scalar(dn, ps[6][:, :], -1.0, None, ALU.mult))
                link(dve.tensor_tensor(dn, dn, ps[6][:, :], ALU.max))
                link(dve.tensor_tensor(dn, dn, ps[1][:, :], ALU.max))
                link(dve.reciprocal(dn, dn))
                link(dve.tensor_tensor(dn, ps[7][:, :], dn, ALU.mult))
                dve.tensor_tensor(ymix[:, 4 + h, 0:S], dn, big[:, 24 + h, 0:S], ALU.mult).then_inc(sm["hd_fin"], 1)
                if h == 2:
                    for u in range(2):
                        w_lo(u)
            for u in range(2, NW):
                w_lo(u)
            residual(G_OUT0)
            norm(0)
            mlp(0, G_MLP0)
            norm(1)

            def small_odd():
                dve.wait_ge(sm["t1_mm"], 1)
                src = ps[4][:, 0:240].rearrange("p (i c) -> p i c", i=QT)
                dve.tensor_copy(mtm[:, :, :], src)
                dve.tensor_copy(gt[:, :, :], src[:, :, 0:24])
                dve.tensor_copy(mts[0:B, :], ps[5][0:B, 0:60]).then_inc(sm["t1_ev"], 1)
                i64, i32 = ident[0:64, 0:64], ident[0:32, 0:32]
                dve.tensor_reduce(mask64[0:64, :], i64.rearrange("p (b h) -> p h b", h=NH), AX.X, ALU.add)
                dve.tensor_reduce(mask32[0:32, :], i32.rearrange("p (b e) -> p e b", e=4), AX.X, ALU.add)
                dve.tensor_reduce(bsel32[0:32, :], i32.rearrange("p (b e) -> p b e", e=4), AX.X, ALU.add)
                dve.wait_ge(sm["sel_mm"], 1)
                dve.tensor_copy(gsel[0:64, :], ps[6][0:64, 0:60])
                dve.tensor_copy(ixE[0:32, :], ps[7][0:32, 0:60]).then_inc(sm["sel_ev"], 1)
                dve.wait_ge(sm["sel_ev"], 1)
                link(dve.tensor_tensor(g24[0:64, :].rearrange("p (h c) -> p h c", c=3),
                                       gsel[0:64, 0:24].rearrange("p (h c) -> p h c", c=3),
                                       mask64[0:64, :].unsqueeze(2).to_broadcast([64, NH, 3]), ALU.mult))
                dve.tensor_reduce(gS[0:64, :], g24[0:64, :].rearrange("p (h c) -> p c h", c=3), AX.X,
                                  ALU.add).then_inc(sm["gate_e"], 1)
                link(dve.tensor_tensor(wE[0:32, :], ixE[0:32, 56:60], mask32[0:32, :], ALU.mult))
                link(dve.tensor_reduce(wi32[0:32, :], wE[0:32, :], AX.X, ALU.add))
                dve.tensor_scalar(WI[0:32, :], bsel32[0:32, :], wi32[0:32, :], 0.5, ALU.mult, ALU.mult)
                link(dve.tensor_tensor(mask64[0:64, :], mask64[0:64, :], slope8[0:64, :], ALU.mult))
                dve.tensor_reduce(sl64[0:64, :], mask64[0:64, :], AX.X, ALU.add)
                dve.tensor_scalar(cm, D0[:, S - P:S], 0.5 * NEG, NEG, ALU.is_lt, ALU.mult)
                dve.tensor_scalar(Mc, Dc, 0.5 * NEG, None, ALU.is_ge)
                dve.wait_ge(sm["gate_e"], 2)
                dve.tensor_scalar(gt[:, :, :], gt[:, :, :], 1.0, None, ALU.add)
                link(dve.tensor_scalar(gS[0:64, :], gS[0:64, :], 1.0, None, ALU.add))
                dve.reciprocal(gt[:, :, :], gt[:, :, :])
                link(dve.reciprocal(gS[0:64, :], gS[0:64, :]))

            def indexer_scores(n):
                i = 3 - n
                w = P * (i + 1)
                tab = TAB[i]
                for e in range(4):
                    dve.wait_ge(sm["isc_r"], 4 * n + e + 1)
                    wie = mtm[:, i, 56 + e:57 + e]
                    last = (dve.tensor_scalar(tab, rl[0][:, 0:w], wie, None, ALU.mult) if e == 0
                            else dve.scalar_tensor_tensor(tab, rl[e % 2][:, 0:w], wie, tab, ALU.mult, ALU.add))
                    last.then_inc(sm["isc_used"], 1)
                    dve.wait_ge(sm["isc_used"], 4 * n + e + 1)
                dve.tensor_scalar(tab[:, 0:P * i], tab[:, 0:P * i], 0.5, None, ALU.mult)
                link(dve.scalar_tensor_tensor(tab[:, P * i:w], tab[:, P * i:w], 0.5, cm, ALU.mult, ALU.add))

            steps = [(i, r) for i in (3, 2, 1) for r in range(TOPK // 8)]

            def top_keys(n):
                for i, r in steps[:n]:
                    tab = TAB[i]
                    link(dve.max(m8, tab))
                    link(dve.match_replace(tab, m8, tab, TAKEN))
                    if r == TOPK // 8 - 1:
                        link(dve.tensor_scalar(tab, tab, 0.5 * TAKEN, NEG, ALU.is_gt, ALU.mult))
                        link(dve.tensor_tensor(tab, tab, D0[:, S - P * (i + 1):S], ALU.add))
                del steps[:n]

            for idx, name in enumerate(O_NAMES):
                g = G_IN1 + idx
                tile_done(g)
                m = 60 if name == "misc" else P
                if name[:2] in ("qn", "qd"):
                    dve.tensor_scalar(big[:, L[name], H2:T], psB(g)[:, 0:H2], 0.125, None, ALU.mult).then_inc(sm["free_b"], 1)
                else:
                    dve.tensor_copy(big[0:m, L[name], H2:T], psB(g)[0:m, 0:H2]).then_inc(sm["free_b"], 1)
                if idx == 3:
                    small_odd()
                if 4 <= idx <= 6:
                    indexer_scores(idx - 4)
                if idx >= 7:
                    top_keys(4)
            dve.wait_ge(sm["free_b"], G_OUT1)
            link(dve.memset(QI, 0.0))
            for e in range(4):
                r = slice(32 * e, 32 * e + 32)
                last = dve.tensor_copy(QI[0:32, e:e + 36 * 7 + 1:36], big[r, L["qi"], S:T])
            last.then_inc(sm["qb_ok"], 1)
            for s in range(1, 8, 2):
                dve.wait_ge(sm["tm_mm"], s + 1)
                dve.tensor_copy(tm[:, :, P * s:P * s + P], ps[s % 4][:, :].rearrange("p (i c) -> p i c", i=QT)).then_inc(sm["tm_b"], 1)
            for br in ("d", "n"):
                link(dve.memset(QB[br], 0.0))
                for g in range(2):
                    r = slice(HD * g, HD * g + HD)
                    for p in range(NP):
                        h = NP * g + p
                        last = dve.tensor_copy(QB[br][r, h:h + 72 * 7 + 1:72], big[r, L[f"q{br}0"] + p, S:T])
                last.then_inc(sm["qb_ok"], 1)
            dve.tensor_copy(vals[:, 32:40], big[:, L["vs"], S:T])
            dve.tensor_copy(vals[:, 40:48], big[:, L["vw"], S:T])
            link(dve.memset(KCZ, 0.0))
            for src, dst in (("kc", kcT), ("vc", vcT)):
                w = wcT[:, 0:BLK] if src == "kc" else wcT[:, BLK:2 * BLK]
                link(dve.tensor_tensor(tmpc.rearrange("p (j t) -> p j t", t=BLK),
                                       big[:, L[src], 0:S].rearrange("p (j t) -> p j t", t=BLK),
                                       w.unsqueeze(1).to_broadcast([P, NB, BLK]), ALU.mult))
                link(dve.tensor_reduce(dst, tmpc.rearrange("p (j t) -> p j t", t=BLK), AX.X, ALU.add))
            link(dve.memset(VF, 0.0))
            for g in range(2):
                r = slice(HD * g, HD * g + HD)
                last = dve.tensor_copy(KCZ[r, NB * g:NB * g + NB], kcT[r, :])
                for p in range(NP):
                    last = dve.tensor_copy(VF[r, p, 16 * p + NB * g:16 * p + NB * g + NB], vcT[r, :])
            last.then_inc(sm["kc_ok"], 1)
            c4 = "p (i c j) -> p i c j"
            slop = slopes.unsqueeze(1).unsqueeze(3).to_broadcast([P, QT, NH, NB])
            dcv = Dc.rearrange("p (i j) -> p i j", i=QT).unsqueeze(2).to_broadcast([P, QT, NH, NB])
            mcv = Mc.rearrange("p (i j) -> p i j", i=QT).unsqueeze(2).to_broadcast([P, QT, NH, NB])
            link(dve.tensor_tensor(sD.rearrange(c4, i=QT, c=NH), dcv, slop, ALU.mult))
            dve.wait_ge(sm["pc_mm"], 1)
            link(dve.tensor_tensor(sc, ps[7][:, 0:256], sD, ALU.add))
            link(dve.tensor_reduce(mxc, sc.rearrange("p (c j) -> p c j", j=NB), AX.X, ALU.max))
            dve.tensor_tensor(sc.rearrange("p (c j) -> p c j", j=NB), sc.rearrange("p (c j) -> p c j", j=NB),
                              mxc.unsqueeze(2).to_broadcast([P, 32, NB]), ALU.subtract).then_inc(sm["pc_x"], 1)
            dve.wait_ge(sm["vf_mm"], 1)
            dve.tensor_copy(VCb.rearrange("p q c -> p (q c)"), ps[4][0:64, :]).then_inc(sm["vf_ev"], 1)
            dve.wait_ge(sm["pc_e"], 1)
            link(dve.tensor_tensor(sc.rearrange(c4, i=QT, c=NH), sc.rearrange(c4, i=QT, c=NH), mcv, ALU.mult))
            link(dve.tensor_reduce(rcc, sc.rearrange("p (c j) -> p c j", j=NB), AX.X, ALU.add))
            link(dve.tensor_scalar(rcc, rcc, 1e-30, None, ALU.max))
            link(dve.reciprocal(rcc, rcc))
            link(dve.tensor_tensor(rcc.rearrange("x (i p g) -> x i p g", i=QT, p=NP),
                                   rcc.rearrange("x (i p g) -> x i p g", i=QT, p=NP),
                                   gt[:, :, :].rearrange("x i (g p c) -> x i p g c", g=2, p=NP)[:, :, :, :, 0], ALU.mult))
            dve.tensor_tensor(sc.rearrange("p (c j) -> p c j", j=NB), sc.rearrange("p (c j) -> p c j", j=NB),
                              rcc.unsqueeze(2).to_broadcast([P, 32, NB]), ALU.mult).then_inc(sm["pc_n"], 1)

            def weighted(dst, j, v):
                return dve.tensor_tensor(dst.rearrange("p (b h) -> p b h", h=NH),
                                         ps[7][:, 64 * j:64 * j + 64].rearrange("p (b h) -> p b h", h=NH),
                                         v.unsqueeze(2).to_broadcast([P, B, NH]), ALU.mult)

            def scores(dst, w, tab, n):
                dve.wait_ge(sm["bs_mm"], n)
                link(dve.scalar_tensor_tensor(dst, tab, sl64[0:64, :], ps[7][0:64, 0:w], ALU.mult, ALU.add))
                dve.tensor_reduce(nms[0:64, :], dst, AX.X, ALU.max, negate=True).then_inc(sm["sc_ok"], 1)

            def normalise(dst, n, gate):
                dve.wait_ge(sm["pe_ok"], n + 1)
                link(dve.tensor_scalar(rss[0:64, :], rss[0:64, :], 1e-30, None, ALU.max))
                link(dve.reciprocal(rcs[0:64, :], rss[0:64, :]))
                if gate is not None:
                    link(dve.tensor_tensor(rcs[0:64, :], rcs[0:64, :], gS[0:64, gate:gate + 1], ALU.mult))
                dve.tensor_scalar(dst, dst, rcs[0:64, :], None, ALU.mult).then_inc(sm["pn_ok"], 1)

            def sample_step(k):
                if k == 5:
                    dve.wait_ge(sm["cmp_mm"], 1)
                    dve.tensor_copy(cmps[0:32, :], ps[4][0:32, 0:256]).then_inc(sm["cmp_ev"], 1)
                    dve.wait_ge(sm["ixc_mm"], 1)
                    dve.tensor_copy(iscS, ps[7][0:B, 0:LS]).then_inc(sm["ixs_ev"], 1)
                    dve.wait_ge(sm["ixs_ev"], 1)
                if k == 6:
                    dve.wait_ge(sm["cmpt_mm"], 1)
                    dve.tensor_copy(kcTs, ps[4][:, 256:288])
                    dve.tensor_copy(vals[:, 0:32].rearrange("p (j b) -> p j b", b=B),
                                    ps[4][:, 288:320].rearrange("p (b j) -> p j b", b=B)).then_inc(sm["cmpt_ev"], 1)
                if k == 7:
                    scores(sc4[0:64, :], NBS, Dcs[0:64, :], 5)
                if 5 <= k <= 8:
                    for r in range(TOPK_S // 32):
                        link(dve.max(m8s[0:B, :], iscS))
                        link(dve.match_replace(iscS, m8s[0:B, :], iscS, TAKEN))
                if k == 8:
                    link(dve.tensor_scalar(iscS, iscS, 0.5 * TAKEN, NEG, ALU.is_gt, ALU.mult))
                    dve.tensor_tensor(iscS, iscS, Ds[0:B, :], ALU.add).then_inc(sm["dsb_in"], 1)
                if k == 9:
                    dve.wait_ge(sm["dsb_mm"], 1)
                    dve.tensor_copy(DdS, ps[7][0:64, 0:LS]).then_inc(sm["dsd_ev"], 1)
                    normalise(sc4[0:64, :], 0, 0)
                if k == 10:
                    dve.wait_ge(sm["pb_mm"], 1)
                    for j in range(NBS):
                        last = weighted(pbt[:, 64 * j:64 * j + 64], j, vals[:, B * j:B * j + B])
                    last.then_inc(sm["pb_ev"], 1)
                for x, (br, (base, n0, *_)) in enumerate(STEP.items()):
                    if k == base + 4:
                        scores(sbs, LS, {"s": Ds[0:64, :], "d": DdS, "w": Dws[0:64, :]}[br], n0 + 5)
                    if k == base + 6:
                        normalise(sbs, x + 1, {"s": 1, "d": None, "w": 2}[br])
                    if k == base + 7:
                        dve.wait_ge(sm["pt_mm"], x + 1)
                        if br == "d":
                            weighted(oD, 2, big[:, L["vd"], S:T])
                        else:
                            j = 4 if br == "s" else 5
                            weighted(pbt[:, 64 * j:64 * j + 64], 2, vals[:, B * j:B * j + B])
                        dve.tensor_copy(PTs[:, :, :], ps[7][:, 0:128].rearrange("p (t c) -> p t c", t=2)).then_inc(sm["pt_ev"], 1)
                    if k == base + 8:
                        dve.wait_ge(sm["pvs_mm"], x + 1)
                        acc = ps[7][:, 192:256]
                        dve.wait_ge(sm["pt_ev"], x + 1)
                        if br == "s":
                            dve.tensor_copy(oN, acc).then_inc(sm["pb_ev"], 1)
                        if br == "d":
                            dve.tensor_tensor(oD, oD, acc, ALU.add).then_inc(sm["pb_ev"], 1)
                        if br == "w":
                            link(dve.tensor_tensor(oN, oN, acc, ALU.add))
                            link(dve.tensor_reduce(rsN, pbt.rearrange("p (j c) -> p c j", j=6), AX.X, ALU.add))
                            link(dve.tensor_tensor(oN, oN, rsN, ALU.add))
                            for n, o in enumerate((oN, oD)):
                                for g in range(2):
                                    r = slice(HD * g, HD * g + HD)
                                    dve.tensor_copy(ymix[r, NP * n:NP * n + NP, S:T],
                                                    o[r, :].rearrange("x (b g p) -> x g p b", g=2, p=NP)[:, g])

            for t in range(len(units) + 4):
                if t < len(units):
                    i, p, g, br, k0, o = units[t]
                    n = P * (i + 1 - k0)
                    if br == "d" and steps:
                        top_keys(len(steps))
                    tab = (Dw[:, 3 * P - n:3 * P] if br == "w" else
                           D0[:, S - n:S] if br == "s" or i == 0 else TAB[i])
                    dve.wait_ge(sm["q_mm"], t + 1)
                    if t >= 2:
                        dve.wait_ge(sm["q_e"], t - 1)
                    dve.scalar_tensor_tensor(sbb[t % 2][:, 0:n], tab, SLOPE[NP * g + p], ps[t % 2][:, 0:n], ALU.mult,
                                             ALU.add).then_inc(sm["q_sc"], 1)
                u = t - 1
                if 0 <= u < len(units):
                    dve.wait_ge(sm["q_e"], u + 1)
                    dve.reciprocal(rrec[u % 2], rsum[u % 2]).then_inc(sm["q_g"], 1)
                if t < len(units):
                    dve.wait_ge(sm["q_sc"], t + 1)
                    dve.tensor_reduce(nmx[t % 2], sbb[t % 2][:, 0:n], AX.X, ALU.max, negate=True).then_inc(sm["q_m"], 1)
                u = t - 1
                if 0 <= u < len(units):
                    i, p, g, br, k0, o = units[u]
                    n = P * (i + 1 - k0)
                    dve.wait_ge(sm["q_g"], u + 1)
                    c = 3 * (NP * g + p) + (1 if br == "s" else 2)
                    gate = ones[:, 0:1] if br == "d" else gt[:, i, c:c + 1]
                    link(dve.scalar_tensor_tensor(rrec[u % 2], rrec[u % 2], 1e30, gate, ALU.min, ALU.mult))
                    dve.tensor_scalar(Pb[u % 2][:, 0:n], Pb[u % 2][:, 0:n], rrec[u % 2], None, ALU.mult).then_inc(sm["q_n"], 1)
                u = t - 4
                if u >= 0 and last_of[units[u][5]] == u:
                    i, p, g, br, k0, o = units[u]
                    dve.wait_ge(sm["q_o"], u + 1)
                    dve.tensor_copy(ymix[:, p + (NP if br == "d" else 0), P * i:P * i + P],
                                    ps[5 + o % 2][:, 0:P]).then_inc(sm["q_of"], 1)
                if t >= START and (t - START) % EVERY == EVERY - 1:
                    sample_step((t - START) // EVERY)
                if t == EARLY:
                    for u in range(NS1, NS1 + 2):
                        w_lo(u)
            for u in range(NS1 + 2, NS1 + NW):
                w_lo(u)
            residual(G_OUT1)
            norm(2)
            mlp(1, G_MLP1)
            norm(3)
            for n in range(1, 2 * QT + 2, 2):
                i = n // 2
                m = P if i < QT else B
                dve.wait_ge(sm["y_mm"], n + 1)
                dve.tensor_copy(ytm[0:m, i, 512:1024], ps[n % 4][0:m, :]).then_inc(sm["y_b"], 1)


_INS = ['x_prompt', 'x_sample', 'state_conv', 'state_C', 'state_n', 'state_m', 'cache_kv', 'cache_idx', 'cache_win',
        'page_table', 'w_in_e', 'gate_b_e', 'conv_w', 'conv_b', 'w_out_e', 'w_in_o', 'w_cmp', 'w_out_o', 'w_up',
        'w_down', 'ln_g', 'ln_b']
_OUTS = [('y_p', (1, S, D)), ('y_s', (B, 1, D)), ('conv_p', (1, 1, 2, 512)), ('conv_s', (1, B, 2, 512)),
         ('c_p', (1, 1, MH, P, P)), ('c_s', (1, B, MH, P, P)), ('n_p', (1, 1, MH, P)), ('n_s', (1, B, MH, P)),
         ('m_p', (1, 1, MH)), ('m_s', (1, B, MH)), ('kv_p', (1, 1, S, 6, 2, HD)), ('kv_s', (1, B, 1, 6, 2, HD)),
         ('idx_p', (1, 1, S, 32)), ('idx_s', (1, B, 1, 32)), ('win_p', (1, 1, PAST, 2, 2, HD)),
         ('win_s', (1, B, PAST, 2, 2, HD))]


def kernel(**inputs):
    import numpy as _np
    import concourse.bacc as _bacc
    from concourse.bass_utils import run_bass_kernel_spmd as _run

    nc = _bacc.Bacc("TRN2", target_bir_lowering=False, num_devices=1)
    arrays, args = {}, []
    for name in _INS:
        a = _np.ascontiguousarray(inputs[name])
        arrays[f"in_{name}"] = a
        args.append(nc.dram_tensor(f"in_{name}", a.shape, mybir.dt.from_np(a.dtype), kind="ExternalInput").ap())
    for name, shape in _OUTS:
        args.append(nc.dram_tensor(f"out_{name}", shape, F32, kind="ExternalOutput").ap())
    build(nc, *args)
    r = _run(nc, [arrays], core_ids=[0])
    return tuple(r.results[0][f"out_{name}"] for name, _ in _OUTS)
```

```python
from contextlib import ExitStack

import concourse.bass as bass
from concourse import mybir

F32 = mybir.dt.float32
F32R = mybir.dt.float32r
I32 = mybir.dt.int32
ALU = mybir.AluOpType
ACT = mybir.ActivationFunctionType
AX = mybir.AxisListType

P = 128
D = 1024
KD = D // P
S = 512
B = 8
T = S + B
H2 = T // 2
QT = S // P
FF = 4096
KF = FF // P
NFC = FF // D
MH = 4
NH = 8
HD = 64
NP = NH // 2
BLK = 64
NB = S // BLK
PAST = 256
PAGE = 128
NPG = PAST // PAGE
NT = B * NPG
NBS = PAST // BLK
LS = PAST + 1
TOPK = min(256, S // 4)
TOPK_S = min(256, LS // 4)
ALPHA = 4.0 ** 0.25
LN_EPS = 1e-5
NEG = -1e30
TAKEN = -3e38
MH_SCALE = 128.0 ** -0.5
SLOTS = ("kc", "vc", "ks", "vs", "kd", "vd", "kw", "vw")
IDX_SCALE = 32.0 ** -0.5
SLOPE = [2.0 ** -(h + 1) for h in range(NH)]
SLOT = 4096
NSLOT = 3
NW = 4
LN_POOL = (0, 1, 2, 3, 5, 6)
XT_ACT = (1, 3, 5, 7)
XL_POOL = (1, 3, 5)
XL_DVE = (0, 2, 4, 6, 7)
SPLIT_NORMS = (0, 1, 2)
SMALL = 5120


def build(nc, x_prompt, x_sample, state_conv, state_C, state_n, state_m, cache_kv, cache_idx, cache_win, page_table,
          w_in_e, gate_b_e, conv_w, conv_b, w_out_e, w_in_o, w_cmp, w_out_o, w_up, w_down, ln_g, ln_b,
          y_p, y_s, conv_p, conv_s, c_p, c_s, n_p, n_s, m_p, m_s, kv_p, kv_s, idx_p, idx_s, win_p, win_s):
    E_TILE = [None] + [12 + i for i in range(12)] + [0, 1, 2, 3, 8, 9, 10, 11, 4, 5, 6, 7, 24, 25, 26, 27]
    G_IN0 = 0
    G_OUT0 = G_IN0 + len(E_TILE)
    G_MLP0 = G_OUT0 + KD
    O_NAMES = ["misc", "ki4", "kd", "vd", "qi", "qd0", "qd1", "qd2", "qd3", "kc", "vc", "ks", "vs", "kw", "vw",
               "qn0", "qn1", "qn2", "qn3"]
    Z = {n: i for i, n in enumerate(O_NAMES)}
    L = {n: i for i, n in enumerate(["misc", "ki4", "kd", "vd", "qi", "kc", "vc", "ks", "qn0", "qn1", "qn2", "qn3",
                                     "qd0", "qd1", "qd2", "qd3", "vs", "kw", "vw"])}
    G_IN1 = G_MLP0 + 2 * KF
    G_OUT1 = G_IN1 + len(O_NAMES)
    G_MLP1 = G_OUT1 + KD

    with ExitStack() as ctx:
        def sb(name, shape, dt=F32):
            return ctx.enter_context(nc.sbuf_tensor(name, shape, dt))

        def sem(name):
            return ctx.enter_context(nc.semaphore(name))

        ring = sb("ring", [P, NSLOT, SLOT])
        xT = sb("xT", [P, KD, T])
        with ExitStack() as mixer:
            big = mixer.enter_context(nc.sbuf_tensor("big", [P, KF, T], F32))
            ymix = mixer.enter_context(nc.sbuf_tensor("ymix", [P, KD, T], F32))
            cbuf = mixer.enter_context(nc.sbuf_tensor("cbuf", [P, 4096], F32))
        with ExitStack() as odd:
            odd.enter_context(nc.sbuf_tensor("projections", [P, len(O_NAMES) * T], F32))
            xl1 = odd.enter_context(nc.sbuf_tensor("xl1", [P, KD, T], F32R))
            odd.enter_context(nc.sbuf_tensor("behind", [P, (KF - KD - len(O_NAMES)) * T], F32))
            xh1 = odd.enter_context(nc.sbuf_tensor("xh1", [P, KD, T], F32R))
        xh = sb("xh", [P, KD, T], F32R)
        xl = sb("xl", [P, KD, T], F32R)
        hh = sb("hh", [P, KD, T], F32R)
        hl = sb("hl", [P, KD, T], F32R)
        wr2 = sb("wr2", [P, 2, 2, KD, P], F32R)
        sb("gap", [P, KD * T - 4096])
        wr0 = sb("wr0", [P, 2, 2, KD, P], F32R)
        att = sb("att", [P, 6144])
        ident = sb("ident", [P, P])
        ones = sb("ones", [P, P])
        meanM = sb("meanM", [P, P])
        colT = sb("colT", [P, 112])
        small = sb("small", [P, SMALL])
        ps = [ctx.enter_context(nc.psum_tensor(f"ps{i}", [P, 512], F32)) for i in range(8)]

        taken = [0]

        def piece(n):
            a = taken[0]
            taken[0] += n
            assert taken[0] <= SMALL, taken[0]
            return small[:, a:a + n]

        names = """x_in cols_in scs_in wc_in c_in y_a y_b y_out pool_step consts_ok small_in page_in w_hi w_lo_p free_a
            free_b sq_done sum_r mu_ok cen_p y_split x_ready xl_p hid_lo hid_sq u_ok sp_ok outs
            c_new store_c nnew_ev ucol_ev p_raw p_ok cn_ev z_pool kiz_ok kz_ok mm_done cw_ok tm_a
            tm_b tms_ev cmp_mm pvs_mm x_hi xl_v hid_hi stats_mm tin_a tin_b tin fg_mm rows_ok h12_mm
            prod_ok dots_mm nnew_ok head_used head_mm nnew_mm ucol_mm wt_ok pre_mm vt_ok kt_ok s_mm
            den_ok num_ok pv_mm vw_ok cn_mm isc_r isc_mm t1_mm t1_ev sel_mm sel_ev tm_mm tms_mm
            bt_ev pct_ev bt_mm bs_mm qb_ok ix_r ixc_mm dsb_in dsb_mm cmp_ev cmpt_mm cmpt_ev ixs_ev
            pn_ok dsd_ev pb_mm pb_ev pt_mm pt_ev kc_ok pc_mm vf_mm vf_ev pc_n pct_mm q_sc q_mm q_n
            q_te q_t q_of q_o y_mm std_ok act_step std_in stats_ok cen_v y_hi nx_ok sg_e ws_ok
            hd_fin smp_y gate_e isc_used sc_ok pe_ok pc_x pc_e q_m q_e dve_step w_lo conv_ok q_g
            mm_half""".split()
        sm = {n: sem(n) for n in names}
        gat = [sem(f"gathered{i}") for i in range(5)]
        w_sem = [sem(f"w_slot{i}") for i in range(NSLOT)]

        def rows(w, c0, c1):
            return w[:, c0:c1].rearrange("(k p) n -> p k n", p=P)

        chunks = []

        def chunk(parts, freed):
            chunks.append((parts, freed))
            return len(chunks) - 1

        def cols_of(slot, a, k, n):
            return ring[:, slot, a:a + k * n].rearrange("p (k n) -> p k n", k=k)

        def wide(w, c0, n, last_g):
            c = len(chunks)
            return chunk([(cols_of(c % NSLOT, 0, KD, n), rows(w, c0, c0 + n))], ("mm_done", last_g + 1))

        SMP_DONE = NP * QT + 11
        plan = {}

        def tile_plan(g, c, n, col, width=P, a=0):
            v = cols_of(c % NSLOT, a, KD, n)
            plan[g] = (c, lambda k, v=v, col=col, width=width: v[:, k, col:col + width], v[:, :, col:col + width])

        wi = w_in_e[0]
        c = wide(wi, 28 * P, 8, G_IN0)
        tile_plan(G_IN0, c, 8, 0, 8)
        for j in range(7):
            g = G_IN0 + 1 + 4 * j
            c = wide(wi, E_TILE[g - G_IN0] * P, 512, g + 3)
            for i in range(4):
                tile_plan(g + i, c, 512, i * P)

        split = []
        split_of = {}
        low = []

        def split_chunk(parts_of, gs, views=None, by="w_lo"):
            c = len(chunks)
            before = sum(x[0] == by for x in low)
            for i in range(len(gs)):
                low.append((by, before + i + 1))
            chunk(parts_of(c % NSLOT), low[-1])
            for i, g in enumerate(gs):
                if views:
                    plan[g] = (c, None, views(c % NSLOT)[i])
                else:
                    tile_plan(g, c, P * max(len(gs), 2), i * P)
                split_of[g] = len(split)
                split.append(g)

        def out_chunks(base, parts_of):
            for j in range(2):
                split_chunk(lambda slot: parts_of(slot, 512 * j), range(base + 4 * j, base + 4 * j + 4))

        out_chunks(G_OUT0, lambda slot, c0: [(cols_of(slot, 0, KD, 512), rows(w_out_e[0], c0, c0 + 512))])

        def mlp_chunks(layer, g):
            for c in range(NFC):
                for w, r0, c0 in ((w_up[layer], 0, D * c), (w_down[layer], D * c, 0)):
                    for j in range(2):
                        split_chunk(lambda slot: [(cols_of(slot, 0, KD, 512),
                                                   rows(w[r0:r0 + D, :], c0 + 512 * j, c0 + 512 * j + 512))],
                                    range(g, g + 4))
                        g += 4

        mlp_chunks(0, G_MLP0)

        wo = w_in_o[0]
        def misc_views(slot):
            v = cols_of(slot, 0, KD, 60 + P)
            return [v[:, :, 0:P], v[:, :, 60:60 + P]]

        def misc_parts(slot):
            v = cols_of(slot, 0, KD, 60 + P)
            return ([(v[:, :, 0:24], rows(wo, 1280, 1304)), (v[:, :, 24:60], rows(wo, 2200, 2236))] +
                    [(v[:, :, 60 + 32 * e:92 + 32 * e], rows(wo, 2200, 2232)) for e in range(4)])

        def wide_split(c0, names, by="w_lo"):
            n = P * len(names)
            split_chunk(lambda slot: [(cols_of(slot, 0, KD, n), rows(wo, c0, c0 + n))], [G_IN1 + Z[x] for x in names], by=by)

        def pair_tiles(c0, names, by="w_lo"):
            def parts(slot):
                v = cols_of(slot, 0, KD, 512)
                return [(v[:, :, P * p + HD * g:P * p + HD * g + HD], rows(wo, c0 + HD * (NP * g + p), c0 + HD * (NP * g + p + 1)))
                        for p in range(NP) for g in range(2)]
            split_chunk(parts, [G_IN1 + Z[x] for x in names], by=by)

        split_chunk(misc_parts, [G_IN1, G_IN1 + 1], misc_views, "w_lo_p")
        wide_split(1816, ("kd", "vd", "qi"))
        pair_tiles(1304, ("qd0", "qd1", "qd2", "qd3"), "w_lo_p")
        wide_split(512, ("kc", "vc", "ks", "vs"), "w_lo_p")
        wide_split(1024, ("kw", "vw"), "w_lo_p")
        c = len(chunks) - 1
        chunks[c] = (chunks[c][0], ("pvs_mm", 3))
        CACHE_SLOT = c % NSLOT
        pair_tiles(0, ("qn0", "qn1", "qn2", "qn3"))
        c = len(chunks) - 1
        chunks[c] = (chunks[c][0], ("q_of", 2 * NP * QT))
        SCRATCH_SLOT = c % NSLOT

        def out_rows(slot, c0):
            w = w_out_o[0].rearrange("(s g q d) n -> s g d q n", s=2, g=2, q=NP)
            v = cols_of(slot, 0, KD, 512)
            return [(v[HD * g:HD * (g + 1), NP * s:NP * (s + 1), :], w[s, g, :, :, c0:c0 + 512])
                    for s in range(2) for g in range(2)]

        out_chunks(G_OUT1, out_rows)
        mlp_chunks(1, G_MLP1)

        loads = [0] * NSLOT
        chunk_value = []
        for c, (parts, _) in enumerate(chunks):
            loads[c % NSLOT] += 16 * len(parts)
            chunk_value.append(loads[c % NSLOT])

        NS1 = split_of[G_OUT1]
        GROUPS = ((0, NW), (split_of[G_IN1], 2), (NS1, NW), (len(split), 0))

        def group(u):
            return max(x for x in GROUPS if x[0] <= u)

        def ahead(g):
            u = split_of[g]
            first, n = group(u)
            return u + n if u + n < len(split) and group(u + n)[0] == first else None

        def xr(n_ln):
            return sum(len(XT_ACT) if n in SPLIT_NORMS else KD for n in range(n_ln))

        def w_split(u):
            first, n = group(u)
            return [(wr0 if (u - first) % n < 2 else wr2)[:, (u - first) % 2, part] for part in range(2)]

        def w_raw(u):
            return plan[split[u]][2]

        block = ctx.enter_context(nc.Block())

        def chain(eng, s):
            n = [0]

            def link(ins):
                n[0] += 1
                ins.then_inc(s, 1)
                eng.wait_ge(s, n[0])
            return link

        sel = piece(MH * P).rearrange("p (h m) -> p h m", h=MH)
        D0 = piece(S)
        Dw = piece(3 * P)
        Ds = piece(LS)
        Dws = piece(LS)
        Dc = piece(QT * NB)
        Mc = piece(QT * NB)
        Dcs = piece(NBS)
        BS = piece(62)
        selB = piece(B * NH)
        selE = piece(B * 4)
        slopes = piece(NH)
        slope8 = piece(NH)
        wcK = piece(2 * P)
        wcT = piece(2 * BLK)
        pages = ctx.enter_context(nc.sbuf_tensor("pages", [1, NT], I32))
        base = taken[0]

        xp_stage = ymix[:, :, :].rearrange("p a b -> p (a b)")[:, 0:QT * D].rearrange("p (t d) -> p t d", t=QT)
        xs_stage = att[0:B, 0:D]
        stg = att[0:112, 1024:1152]
        scs = att[0:2 * B, 1152:1152 + 512]
        stm = piece(B)
        gbc = piece(1)

        Ct = cbuf[:, :].rearrange("p (b h d) -> p h b d", h=MH, b=B)
        gz = att[0:8, 1664:1664 + T]
        fgt = att[0:4, 2184:2184 + T]
        nx = att[0:4, 2704:2704 + T]
        lg = att[0:4, 3224:3224 + T]
        Fc = att[0:4, 3744:3744 + S]
        at_ = att[0:4, 4256:4256 + S]
        Mr = att[0:4, 4768:4768 + S]
        nG = att[0:4, 5280:5280 + S]
        rowsP = piece(2 * S)
        rowsS = piece(3 * B)
        eS = piece(3 * B)
        interS = piece(B)
        mtS = piece(B)
        mpc = piece(1)
        aT = piece(QT * MH)
        bcS = piece(MH * 3 * B)
        scT = piece(4 * 2 * B)
        prod = piece(2 * MH * B)
        dts = piece(2 * MH * B)
        nnw = piece(MH * B)
        vwS = piece(MH * B)
        swa = piece(MH * B)
        recS = piece(MH * B)
        cq = piece(MH * B)
        hS = piece(MH * B)
        wsc = piece(QT)
        nml = piece(1)
        nno = piece(P)
        uo = piece(512)
        cst = piece(P)
        nrow = piece(P)
        OFF = [0, 512, 896, 1152]
        Wt = att[:, 0:1280]
        Pt = att[:, 1280:2560]
        vtm = att[:, 2560:3072]
        ktm = att[:, 3072:3584]
        vw = att[:, 3584:4096]
        tmpS = att[:, 4096:5120].rearrange("p (b d) -> p b d", b=B)
        dn = att[:, 5120:5632]
        num = att[:, 5632:6144]

        XH = {0: xh, 1: xh1, 2: xh}
        XL = {0: xl, 1: xl1, 2: xl}
        racc = att[:, 0:T]
        sacc = att[:, T:2 * T]
        sq = [att[:, (2 + i) * T:(3 + i) * T] for i in range(2)]
        mu = att[:, 4 * T:5 * T]
        rs = att[:, 5 * T:6 * T]
        rel = [att[:, (6 + i) * T:(7 + i) * T] for i in range(2)]
        var = att[:, 8 * T:9 * T]
        hid = [att[:, (9 + i) * T:(10 + i) * T] for i in range(2)]

        after0 = taken[0]
        taken[0] = base
        flat = big[:, :, :].rearrange("p a b -> p (a b)")
        o = len(O_NAMES) * T
        tm = flat[:, o:o + QT * 1024].rearrange("p (i c) -> p i c", i=QT)
        o += QT * 1024
        tms = flat[0:B, o:o + 1024]
        o += 1024
        TAB = [None, flat[:, o:o + 256], flat[:, o + 256:o + 640], flat[:, o + 640:o + 1152]]
        assert o + 1152 <= KF * T
        KZ = {n: att[:, 1024 * i:1024 * (i + 1)].rearrange("p (g k) -> p g k", g=2) for i, n in enumerate(("kd", "ks", "kw"))}
        kiz = att[:, 3072:3072 + 2048].rearrange("p (e k) -> p e k", e=4)
        rl = [att[:, 5120 + 512 * i:5632 + 512 * i] for i in range(2)]
        room = ring[:, SCRATCH_SLOT, :]
        kTs = [room[:, 2 * LS * i:2 * LS * (i + 1)].rearrange("p (b k) -> p b k", b=2) for i in range(2)]
        o = 4 * LS
        sbs = room[0:64, o:o + LS]
        iscS = room[0:B, o + LS:o + 2 * LS]
        rS = room[0:32, o + 2 * LS:o + 3 * LS]
        DdS = room[0:64, o + 3 * LS:o + 4 * LS]
        o += 4 * LS
        PTs = room[:, o:o + 128].rearrange("p (t c) -> p t c", t=2)
        QI = room[:, o + 128:o + 128 + 256]
        kidx = room[:, o + 384:o + 384 + 512].rearrange("p (t e) -> p t e", t=NT)
        o += 896
        VCb = room[0:64, o:o + 512].rearrange("p (q c) -> p q c", q=NP)
        PcT = room[0:64, o + 512:o + 1024]
        assert o + 1024 <= SLOT, o
        pbt = flat[:, len(O_NAMES) * T + QT * 1024 + 1024 + 1152:][:, 0:384]
        QB = {"d": piece(512), "n": piece(512)}
        mtm = piece(QT * 60).rearrange("p (i c) -> p i c", i=QT)
        gt = piece(QT * 24).rearrange("p (i c) -> p i c", i=QT)
        mts = piece(60)
        gsel = piece(60)
        gS = piece(3)
        g24 = piece(24)
        mask64 = piece(NH)
        sl64 = piece(1)
        mask32 = piece(4)
        bsel32 = piece(B)
        wE = piece(4)
        wi32 = piece(1)
        WI = piece(B)
        ixE = piece(60)
        m8 = piece(8)
        m8s = piece(8)
        nmx = [piece(1) for _ in range(2)]
        rsum = [piece(1) for _ in range(2)]
        rrec = [piece(1) for _ in range(2)]
        nms, rss, rcs = piece(1), piece(1), piece(1)
        kcT = piece(NB)
        vcT = piece(NB)
        KCZ = piece(2 * NB)
        kcTs = piece(B * NBS)
        vals = piece(6 * B)
        cmps = piece(2 * P)
        sc4 = piece(NBS)
        oN = piece(B * NH)
        mixc = piece(P)
        oD = piece(B * NH)
        rsN = piece(B * NH)
        assert taken[0] <= SMALL
        sc = big[:, L["kc"], 0:256]
        sD = big[:, L["kc"], 256:512]
        VF = big[:, L["vc"], 0:256].rearrange("p (q c) -> p q c", q=NP)
        mxc = big[:, L["vc"], 256:288]
        rcc = big[:, L["vc"], 288:320]
        tmpc = att[:, 3072:3584]
        Pb = [att[:, 3072 + 512 * i:3584 + 512 * i] for i in range(2)]
        PTb = [att[:, 4096 + 512 * i:4608 + 512 * i] for i in range(2)]
        sbb = [att[:, 5120 + 512 * i:5632 + 512 * i] for i in range(2)]
        cache = {"c": cbuf[:, :].rearrange("p (t x) -> p t x", t=NT),
                 "y": ring[:, CACHE_SLOT, :].rearrange("p (t x) -> p t x", t=NT)}
        STEP = {"s": (10, 4, "y", "n", 0), "d": (18, 8, "c", "d", 2), "w": (26, 12, "y", "n", 3)}
        EVERY, START = 2, 12

        units = []
        for branches in (("d",), ("s", "w")):
            for late, early in ((3, 0), (2, 1)):
                for p in range(NP):
                    o = 1 + max((x[5] for x in units), default=-1)
                    for br in branches:
                        for g in range(2):
                            for n, i in enumerate((late, early)):
                                units.append((i, p, g, br, max(0, i - 2) if br == "w" else 0, o + n))
        EARLY = len(units) - 16
        first_of = {}
        last_of = {}
        for u, x in enumerate(units):
            first_of.setdefault((x[5], x[2]), u)
            last_of[x[5]] = u

        cm = mixc
        ytm = flat[:, 0:5 * D].rearrange("p (i d) -> p i d", i=5)

        def psA(g):
            return ps[2 * (g % 2)]

        def psB(g):
            return ps[2 * (g % 2) + 1]

        @block.sync
        def _(sp):
            sp.dma_start(xp_stage, x_prompt[0].rearrange("(t p) d -> p t d", p=P)).then_inc(sm["x_in"], 16)
            sp.dma_start(xs_stage, x_sample.rearrange("b o d -> (b o) d")).then_inc(sm["x_in"], 16)
            sp.dma_start(stg[0:32, :], ln_g.rearrange("l s (k d) -> (l s k) d", d=P)).then_inc(sm["cols_in"], 16)
            sp.dma_start(stg[32:64, :], ln_b.rearrange("l s (k d) -> (l s k) d", d=P)).then_inc(sm["cols_in"], 16)
            sp.dma_start(stg[64:76, :], conv_w.rearrange("o j (c d) -> (o j c) d", d=P)).then_inc(sm["cols_in"], 16)
            sp.dma_start(stg[76:80, :], conv_b.rearrange("o (c d) -> (o c) d", d=P)).then_inc(sm["cols_in"], 16)
            sp.dma_start(stg[80:112, :], state_n.rearrange("o b h d -> (o b h) d")).then_inc(sm["cols_in"], 16)
            sp.dma_start(scs, state_conv.rearrange("o b j c -> (o b j) c")).then_inc(sm["scs_in"], 16)
            for c, (parts, _) in enumerate(chunks):
                if c >= NSLOT:
                    s, v = chunks[c - NSLOT][1]
                    sp.wait_ge(sm[s], v)
                for dst, src in parts:
                    sp.dma_start(dst, src).then_inc(w_sem[c % NSLOT], 16)
                if c == 0:
                    for half in range(2):
                        for s in range(2):
                            for g in range(2):
                                sp.dma_start(wcK[64 * half:64 * half + 64, P * s + HD * g:P * s + HD * g + HD],
                                             w_cmp[0, s]).then_inc(sm["wc_in"], 16)
                if c == 2:
                    for h in range(MH):
                        sp.dma_start(Ct[:, h, :, :], state_C[0, :, h].rearrange("b e d -> e b d")).then_inc(sm["c_in"], 16)

            for half in range(2):
                for i in range(QT):
                    if i % 2 == 0:
                        sp.wait_ge(sm["y_a"], 2 * half + i // 2 + 1)
                    else:
                        sp.wait_ge(sm["y_b"], 1 + 2 * half + i // 2 + 1)
                    sp.dma_start(y_p[0, P * i:P * (i + 1), 512 * half:512 * half + 512],
                                 ytm[:, i, 512 * half:512 * half + 512]).then_inc(sm["y_out"], 16)
            sp.wait_ge(sm["y_b"], 6)
            sp.dma_start(y_s.rearrange("b o d -> (b o) d"), ytm[0:B, QT, :]).then_inc(sm["y_out"], 16)
            sp.wait_ge(sm["y_out"], 16 * (2 * QT + 1))

        @block.gpsimd
        def _(pool):
            link = chain(pool, sm["pool_step"])
            link(pool.memset(ident[:, :], 0.0))
            pool.affine_select(out=ident[:, :], in_=ident[:, :], compare_op=ALU.not_equal, fill=1.0, base=0,
                               pattern=[[-1, P]], channel_multiplier=1).then_inc(sm["consts_ok"], 1)
            pool.dma_start(stm[0:MH, :], state_m[0].rearrange("b h -> h b"), allow_slow_non_contiguous=True).then_inc(sm["small_in"], 16)
            pool.dma_start(gbc[0:8, :], gate_b_e.rearrange("o c -> c o"), allow_slow_non_contiguous=True).then_inc(sm["small_in"], 16)
            pool.dma_start(pages[0:1, :], page_table.rearrange("(o b) t -> o (b t)", o=1)).then_inc(sm["page_in"], 16)
            pool.memset(ones[:, :], 1.0)
            pool.memset(meanM[:, :], 1.0 / D).then_inc(sm["consts_ok"], 1)
            link(pool.memset(sel[:, :, :], 0.0))
            pool.affine_select(out=sel[:, :, :], in_=sel[:, :, :], compare_op=ALU.not_equal, fill=1.0, base=0,
                               pattern=[[-1, MH], [0, P]], channel_multiplier=1)
            link(pool.iota(D0, pattern=[[1, S]], base=-(S - P), channel_multiplier=-1, allow_small_or_imprecise_dtypes=True))
            link(pool.affine_select(out=D0, in_=D0, compare_op=ALU.is_ge, fill=NEG, base=S - P,
                                    pattern=[[-1, S]], channel_multiplier=1))
            pool.affine_select(out=Dw, in_=D0[:, P:S], compare_op=ALU.is_gt, fill=NEG, base=0,
                               pattern=[[1, 3 * P]], channel_multiplier=-1)
            pool.iota(Ds, pattern=[[1, LS]], base=-PAST, channel_multiplier=0, allow_small_or_imprecise_dtypes=True)
            link(pool.iota(Dws, pattern=[[1, LS]], base=-PAST, channel_multiplier=0, allow_small_or_imprecise_dtypes=True))
            pool.memset(Dws[:, 0:1], NEG)
            link(pool.iota(Dc.rearrange("p (i j) -> p i j", i=QT), pattern=[[-P, QT], [BLK, NB]], base=BLK - 1,
                           channel_multiplier=-1, allow_small_or_imprecise_dtypes=True))
            pool.affine_select(out=Dc.rearrange("p (i j) -> p i j", i=QT), in_=Dc.rearrange("p (i j) -> p i j", i=QT),
                               compare_op=ALU.is_ge, fill=NEG, base=-(BLK - 1), pattern=[[P, QT], [-BLK, NB]],
                               channel_multiplier=1)
            pool.iota(Dcs, pattern=[[BLK, NBS]], base=BLK - 1 - PAST, channel_multiplier=0,
                      allow_small_or_imprecise_dtypes=True)
            link(pool.memset(BS, 0.0))
            link(pool.memset(BS[0:64, 30:31], 1.0))
            link(pool.memset(BS[64:128, 31:32], 1.0))
            link(pool.memset(selB, 0.0))
            pool.affine_select(out=selB.rearrange("p (b h) -> p b h", b=B), in_=selB.rearrange("p (b h) -> p b h", b=B),
                               compare_op=ALU.not_equal, fill=1.0, base=0, pattern=[[-1, B], [0, NH]], channel_multiplier=1)
            link(pool.memset(selE, 0.0))
            pool.affine_select(out=selE.rearrange("p (b h) -> p b h", b=B), in_=selE.rearrange("p (b h) -> p b h", b=B),
                               compare_op=ALU.not_equal, fill=1.0, base=0, pattern=[[-1, B], [0, 4]], channel_multiplier=1)
            for h in range(NH):
                g, p = divmod(h, NP)
                pool.memset(slopes[:, 2 * p + g:2 * p + g + 1], SLOPE[h])
                last = pool.memset(slope8[:, h:h + 1], SLOPE[h])
            last.then_inc(sm["consts_ok"], 1)

            def low_part(u):
                pool.wait_ge(sm["w_hi"], u + 1)
                w_h, w_l = w_split(u)
                pool.tensor_tensor(w_l, w_raw(u), w_h.bitcast(F32), ALU.subtract).then_inc(sm["w_lo_p"], 1)

            def sums(n_ln, g0):
                for m in range(KD - 1):
                    pool.wait_ge(sm["free_a"], g0 + m + 1)
                    pool.wait_ge(sm["free_b"], g0 + m + 1)
                    if m == 0:
                        link(pool.tensor_copy(racc, xT[:, 0, :]))
                    else:
                        link(pool.tensor_tensor(racc, racc, xT[:, m, :], ALU.add))
                    pool.wait_ge(sm["sq_done"], KD * n_ln + m + 1)
                    last = (pool.tensor_copy(sacc, sq[0]) if m == 0
                            else pool.tensor_tensor(sacc, sacc, sq[m % 2], ALU.add))
                    last.then_inc(sm["sum_r"], 1)
                    pool.wait_ge(sm["sum_r"], (KD - 1) * n_ln + m + 1)
                if n_ln == 1:
                    for u in range(2):
                        low_part(split_of[G_IN1] + u)
                pool.wait_ge(sm["mu_ok"], n_ln + 1)
                for m in LN_POOL:
                    pool.tensor_tensor(xT[:, m, :], xT[:, m, :], mu, ALU.subtract).then_inc(sm["cen_p"], 1)

            def split_y(k, s, v):
                pool.wait_ge(sm[s], v)
                pool.tensor_tensor(xl[:, k, :], ymix[:, k, :], xh[:, k, :].bitcast(F32), ALU.subtract).then_inc(sm["y_split"], 1)

            def x_low(n_ln):
                for m in XL_POOL:
                    pool.wait_ge(sm["x_ready"], xr(n_ln) + XT_ACT.index(m) + 1)
                    pool.tensor_tensor(XL[n_ln][:, m, :], xT[:, m, :], XH[n_ln][:, m, :].bitcast(F32), ALU.subtract).then_inc(sm["xl_p"], 1)

            def mlp(layer, g):
                for c in range(NFC):
                    for j in range(KD):
                        n = KF * layer + KD * c + j
                        pool.wait_ge(sm["free_a"], g + 1)
                        pool.wait_ge(sm["free_b"], g + 1)
                        if n >= 2:
                            pool.wait_ge(sm["hid_lo"], n - 1)
                        pool.tensor_tensor(hid[j % 2], rel[j % 2], rel[j % 2], ALU.mult).then_inc(sm["hid_sq"], 1)
                        g += 1
                    g += KD

            for i in range(4):
                g = G_IN0 + 17 + i
                pool.wait_ge(sm["free_a"], g + 1)
                pool.wait_ge(sm["free_b"], g + 1)
                pool.tensor_tensor(big[:, i, :], big[:, i, :], big[:, 8 + i, :], ALU.mult).then_inc(sm["u_ok"], 1)
            pool.wait_ge(sm["sp_ok"], 1)
            pool.dma_start(m_p.rearrange("o b h -> h (o b)"), mpc[0:MH, :], allow_slow_non_contiguous=True).then_inc(sm["outs"], 16)
            pool.dma_start(m_s[0].rearrange("b h -> h b"), mtS[0:MH, :], allow_slow_non_contiguous=True).then_inc(sm["outs"], 16)
            for h in range(MH):
                pool.wait_ge(sm["c_new"], h + 1)
                pool.dma_start(c_s[0, :, h].rearrange("b e d -> e b d"), Ct[:, h, :, :]).then_inc(sm["store_c"], 16)
            pool.wait_ge(sm["nnew_ev"], 1)
            pool.dma_start(n_s.rearrange("o b h d -> (o b h) d"), nno[0:MH * B, :]).then_inc(sm["outs"], 16)
            pool.wait_ge(sm["ucol_ev"], 1)
            pool.dma_start(conv_p.rearrange("o b j c -> (o b j) c"), uo[0:2, :]).then_inc(sm["outs"], 16)
            pool.dma_start(conv_s[0, :, 1, :], uo[2:2 + B, :]).then_inc(sm["outs"], 16)
            pool.dma_start(conv_s[0, :, 0, :], state_conv[0, :, 1, :]).then_inc(sm["outs"], 16)
            for h in range(MH):
                for i in range(QT):
                    pool.wait_ge(sm["p_raw"], QT * h + i + 1)
                    d = Pt[:, OFF[i]:OFF[i] + P]
                    pool.affine_select(out=d, in_=d, compare_op=ALU.is_ge, fill=0.0, base=0, pattern=[[1, P]],
                                       channel_multiplier=-1).then_inc(sm["p_ok"], 1)
                split_y(h, "y_hi", max(1, 2 * h))
                if h:
                    split_y(MH + h - 1, "y_hi", 2 * h + 1)
                pool.wait_ge(sm["cn_ev"], 2 * h + 2)
                pool.dma_start(c_p[0, 0, h], cst).then_inc(sm["store_c"], 16)
                pool.dma_start(n_p[0, :, h, :], nrow[0:1, :]).then_inc(sm["store_c"], 16)
            split_y(KD - 1, "y_hi", KD)
            sums(0, G_OUT0)
            x_low(0)
            mlp(0, G_MLP0)
            sums(1, G_MLP0 + 2 * KF - KD)
            x_low(1)

            pool.wait_ge(sm["x_ready"], xr(2))
            pool.memset(kiz[:, :, :], 0.0)
            last = pool.memset(att[:, 0:3072], 0.0)
            last.then_inc(sm["z_pool"], 1)
            pool.wait_ge(sm["z_pool"], 1)

            def tile_ready(name):
                pool.wait_ge(sm["free_a"], G_IN1 + Z[name] + 1)
                pool.wait_ge(sm["free_b"], G_IN1 + Z[name] + 1)

            tile_ready("ki4")
            for e in range(4):
                pool.tensor_copy(kiz[32 * e:32 * e + 32, e, :], big[32 * e:32 * e + 32, L["ki4"], 0:S]).then_inc(sm["kiz_ok"], 1)
                pool.wait_ge(sm["kiz_ok"], e + 1)
            pool.wait_ge(sm["page_in"], 16)

            def gather(n, src_of, dst):
                for t in range(NT):
                    r = pool.value_load(pages[0:1, t:t + 1], min_val=0, max_val=cache_kv.shape[1] - 1)
                    pool.dma_start(dst[:, t, :], src_of(r)).then_inc(gat[n], 16)

            kv_rows = cache_kv[0].rearrange("n p s g d -> n p (s g d)")

            def kv_page(c0):
                return lambda r: kv_rows[bass.ds(r, 1), :, c0:c0 + 256].rearrange("n p x -> p (n x)")

            def padded(n, name):
                tile_ready(name)
                for g in range(2):
                    pool.tensor_copy(KZ[name][HD * g:HD * g + HD, g, :],
                                     big[HD * g:HD * g + HD, L[name], 0:S]).then_inc(sm["kz_ok"], 1)
                    pool.wait_ge(sm["kz_ok"], 2 * n + g + 1)

            padded(0, "kd")
            for name in O_NAMES[Z["qd0"]:Z["vw"] + 1]:
                low_part(split_of[G_IN1 + Z[name]])
            padded(1, "ks")
            padded(2, "kw")
            by, n = low[split_of[G_IN1 + Z["vw"]]]
            pool.wait_ge(sm[by], n)
            gather(0, kv_page(2 * P), cache["y"])
            by, n = low[split_of[G_IN1 + Z["qn3"]]]
            pool.wait_ge(sm[by], n)
            gather(4, lambda r: cache_idx[0][bass.ds(r, 1), :, :].rearrange("n p e -> p (n e)"), kidx)
            pool.wait_ge(sm["mm_done"], G_OUT1)
            gather(1, kv_page(0), cache["c"])
            pool.wait_ge(gat[1], 16 * NT)
            for t in range(NT):
                last = pool.tensor_tensor(cache["c"][:, t, :], cache["c"][:, t, :], wcK, ALU.mult)
            last.then_inc(sm["cw_ok"], 1)
            pool.wait_ge(sm["cw_ok"], 1)
            pool.wait_ge(sm["tm_a"], 4)
            pool.wait_ge(sm["tm_b"], 4)
            pool.dma_start(kv_p[0, 0].rearrange("(i p) s g d -> p i (s g d)", p=P), tm[:, :, 0:768]).then_inc(sm["outs"], 16)
            pool.dma_start(win_p[0, 0].rearrange("(i p) s g d -> p i (s g d)", p=P), tm[:, 2:4, 768:1024]).then_inc(sm["outs"], 16)
            pool.wait_ge(sm["tms_ev"], 2)
            pool.dma_start(kv_s[0].rearrange("b t s g d -> (b t) (s g d)"), tms[:, 0:768]).then_inc(sm["outs"], 16)
            pool.dma_start(win_s[0, :, PAST - 1].rearrange("b s g d -> b (s g d)"), tms[:, 768:1024]).then_inc(sm["outs"], 16)
            pool.dma_start(win_s[0, :, 0:PAST - 1].rearrange("b t s g d -> b t (s g d)"),
                           cache_win[0, :, 1:PAST].rearrange("b t s g d -> b t (s g d)")).then_inc(sm["outs"], 16)
            pool.dma_start(idx_p[0, 0].rearrange("(i p) e -> p i e", p=P), mtm[:, :, 24:56]).then_inc(sm["outs"], 16)
            pool.dma_start(idx_s[0].rearrange("b t e -> (b t) e"), mts[0:B, 24:56]).then_inc(sm["outs"], 16)
            pool.wait_ge(sm["cmp_mm"], 1)
            gather(2, kv_page(4 * P), cache["c"])
            pool.wait_ge(sm["pvs_mm"], 1)
            pool.dma_start(cache["y"], cache_win[0].rearrange("b (t p) s g d -> p (b t) (s g d)", p=P)).then_inc(gat[3], 16)
            pool.wait_ge(sm["outs"], 16 * 13)
            for k in range(KD):
                split_y((k + NP) % KD, "y_hi", KD + k + 1)
            sums(2, G_OUT1)
            x_low(2)
            mlp(1, G_MLP1)
            sums(3, G_MLP1 + 2 * KF - KD)
            pool.wait_ge(sm["store_c"], 16 * 3 * MH)

        @block.tensor
        def _(pe):
            def tr(out, in_, n):
                return pe.matmul(out, in_, ident[0:n, 0:n], start=True, stop=True, is_transpose=True,
                                 skip_group_check=True)

            def mm(out, lhsT, rhs, start=True, stop=True):
                return pe.matmul(out, lhsT, rhs, start=start, stop=stop, skip_group_check=True)

            loaded = [-1]

            def chunk_here(c):
                if c > loaded[0]:
                    pe.wait_ge(w_sem[c % NSLOT], chunk_value[c])
                    loaded[0] = c

            def banks_free(g):
                if g >= 2:
                    pe.wait_ge(sm["free_a"], g - 1)
                    pe.wait_ge(sm["free_b"], g - 1)

            def tile(g, rhs, m):
                banks_free(g)
                chunk_here(plan[g][0])
                for k in range(KD):
                    for half, bank in ((0, psA(g)), (1, psB(g))):
                        last = pe.matmul(bank[0:m, 0:H2], plan[g][1](k), rhs[:, k, half * H2:(half + 1) * H2],
                                         start=(k == 0), stop=(k == KD - 1))
                last.then_inc(sm["mm_done"], 1)

            def split_tiles(gs, hi, lo, ready_hi=None, ready_lo=None):
                for g in gs:
                    banks_free(g)
                    pe.wait_ge(sm["w_hi"], split_of[g] + 1)
                    by, n = low[split_of[g]]
                    pe.wait_ge(sm[by], n)
                for k in range(KD):
                    for part, ready, x in ((0, ready_hi, hi), (0, ready_lo, lo), (1, None, hi)):
                        if ready:
                            ready(k)
                        first, final = k == 0 and x is hi and part == 0, k == KD - 1 and part == 1
                        for g in gs:
                            w = w_split(split_of[g])[part]
                            for half, bank in ((0, psA(g)), (1, psB(g))):
                                last = pe.matmul(bank[:, 0:H2], w[:, k, :], x[:, k, half * H2:(half + 1) * H2],
                                                 start=first, stop=final)
                            if final:
                                last.then_inc(sm["mm_done"], 1)

            def x_hi_here(n_ln):
                return lambda k: pe.wait_ge(sm["x_hi"], KD * SPLIT_NORMS.index(n_ln) + k + 1)

            def x_lo_here(n_ln):
                n = SPLIT_NORMS.index(n_ln)

                def ready(k):
                    if k in XL_POOL:
                        pe.wait_ge(sm["xl_p"], len(XL_POOL) * n + XL_POOL.index(k) + 1)
                    else:
                        pe.wait_ge(sm["xl_v"], len(XL_DVE) * n + XL_DVE.index(k) + 1)
                return ready

            def hidden_here(layer, c):
                def ready(k):
                    pe.wait_ge(sm["hid_hi"], KF * layer + KD * c + k + 1)
                    pe.wait_ge(sm["hid_lo"], KF * layer + KD * c + k + 1)
                return ready

            def mlp(layer, g):
                for c in range(NFC):
                    if c == 0:
                        split_tiles((g, g + 1), xh, xl, x_hi_here(2 * layer), x_lo_here(2 * layer))
                        g += 2
                    for j in range(2 if c == 0 else 0, KD):
                        split_tiles((g,), xh, xl)
                        g += 1
                    for j in range(KD):
                        split_tiles((g,), hh, hl, hidden_here(layer, c) if j == 0 else None)
                        g += 1

            def norm_sums(n_ln, g0):
                pe.wait_ge(sm["sum_r"], (KD - 1) * (n_ln + 1))
                for final, parts in ((False, ((4, racc), (6, sacc))), (True, ((4, xT[:, KD - 1, :]), (6, sq[(KD - 1) % 2])))):
                    for n, src in parts:
                        if final and n == 4:
                            pe.wait_ge(sm["free_b"], g0 + KD)
                        if final and n == 6:
                            pe.wait_ge(sm["sq_done"], KD * (n_ln + 1))
                        for half in range(2):
                            last = mm(ps[n + half][:, 0:H2], meanM[:, :], src[:, half * H2:(half + 1) * H2],
                                      start=not final, stop=final)
                last.then_inc(sm["stats_mm"], 1)

            pe.wait_ge(sm["consts_ok"], 1)
            pe.wait_ge(sm["x_in"], 32)
            for k in range(KD):
                if k >= 6:
                    pe.wait_ge(sm["tin_a"] if k % 2 == 0 else sm["tin_b"], (k - 6) // 2 + 1)
                for t in range(QT):
                    last = tr(ps[k % 6][:, P * t:P * t + P], xp_stage[:, t, P * k:P * k + P], P)
                last.then_inc(sm["tin"], 1)
            for k in range(KD):
                last = tr(ps[6][:, B * k:B * k + B], xs_stage[:, P * k:P * k + P], B)
            last.then_inc(sm["tin"], 1)
            pe.wait_ge(sm["cols_in"], 80)
            tr(ps[7][:, 0:112], stg, 112).then_inc(sm["tin"], 1)
            pe.wait_ge(sm["tin_a"], KD // 2)
            pe.wait_ge(sm["tin_b"], KD // 2 + 2)

            for idx in range(len(E_TILE)):
                tile(G_IN0 + idx, xT, 8 if idx == 0 else P)
                if idx == 5:
                    pe.wait_ge(sm["wc_in"], 16 * 8)
                    for s in range(2):
                        last = tr(ps[7][:, BLK * s:BLK * (s + 1)], wcK[0:64, P * s:P * s + P], 64)
                    last.then_inc(sm["tin"], 1)
                if idx == 2:
                    pe.wait_ge(sm["consts_ok"], 3)
                    pe.wait_ge(sm["free_a"], 1)
                    pe.wait_ge(sm["free_b"], 1)
                    for half in range(2):
                        last = mm(ps[4 + half][0:4, 0:H2], ident[0:8, 4:8], gz[:, half * H2:(half + 1) * H2])
                    last.then_inc(sm["fg_mm"], 1)
                if idx == 12:
                    pe.wait_ge(sm["scs_in"], 16)
                    pe.wait_ge(sm["rows_ok"], 1)
                    pe.wait_ge(sm["tin_b"], KD // 2 + 3)
                    for i in range(QT):
                        tr(ps[4][:, MH * i:MH * i + MH], at_[:, P * i:P * i + P], MH)
                    for h in range(MH):
                        mm(ps[5][:, 24 * h:24 * h + 24], sel[0:MH, h, :], eS[0:MH, :])
                    for i in range(4):
                        last = tr(ps[7][:, 16 * i:16 * i + 16], scs[:, P * i:P * i + P], 2 * B)
                    last.then_inc(sm["h12_mm"], 1)
                if idx == 14:
                    pe.wait_ge(sm["prod_ok"], 1)
                    mm(ps[4][:, 0:64], ones[:, :], prod).then_inc(sm["dots_mm"], 1)
                if idx in (16, 18, 20, 22):
                    h = (idx - 16) // 2
                    if h == 0:
                        pe.wait_ge(sm["nnew_ok"], 1)
                    else:
                        pe.wait_ge(sm["head_used"], h)
                    for n, t0 in ((4, 12), (6, 16)):
                        for b in range(B):
                            last = tr(ps[n + b // 4][:, P * (b % 4):P * (b % 4) + P],
                                      big[:, t0 + h, S + b:S + b + 1].to_broadcast([P, P]), P)
                    last.then_inc(sm["head_mm"], 1)
                if idx == 25:
                    pe.wait_ge(sm["head_used"], MH)
                    tr(ps[4][0:MH * B, 0:P], nnw, P).then_inc(sm["nnew_mm"], 1)
                    pe.wait_ge(sm["u_ok"], 4)
                    for i in range(4):
                        last = tr(ps[5][0:B + 2, P * i:P * i + P], big[:, i, S - 2:T], P)
                    last.then_inc(sm["ucol_mm"], 1)

            pe.wait_ge(sm["free_a"], G_OUT0)
            pe.wait_ge(sm["free_b"], G_OUT0)
            pe.wait_ge(sm["nnew_ev"], 1)
            pe.wait_ge(sm["ucol_ev"], 1)
            pe.wait_ge(sm["c_new"], MH)
            for h in range(MH):
                if h:
                    pe.wait_ge(sm["wt_ok"], QT * h)
                mm(ps[0][:, :], sel[0:MH, h, :], rowsP[0:MH, 0:S]).then_inc(sm["pre_mm"], 1)
                if h:
                    pe.wait_ge(sm["vt_ok"], h)
                    pe.wait_ge(sm["kt_ok"], h)
                for n, t0 in ((2, 20), (3, 16)):
                    for i in range(QT):
                        last = tr(ps[n][:, P * i:P * i + P], big[:, t0 + h, P * i:P * i + P], P)
                    last.then_inc(sm["pre_mm"], 1)
                if h:
                    pe.wait_ge(sm["cn_ev"], 2 * h)
                for i in range(QT + 1):
                    if i < QT:
                        if i >= 2:
                            pe.wait_ge(sm["p_raw"], QT * h + i - 1)
                        mm(ps[4 + i % 2][:, 0:S - P * i], big[:, 16 + h, P * i:P * i + P],
                           big[:, 12 + h, P * i:S]).then_inc(sm["s_mm"], 1)
                    if i >= 1:
                        j = i - 1
                        pe.wait_ge(sm["p_ok"], QT * h + j + 1)
                        if j == 0:
                            pe.wait_ge(sm["vt_ok"], h + 1)
                            if h:
                                pe.wait_ge(sm["den_ok"], h)
                                pe.wait_ge(sm["num_ok"], h)
                            mm(ps[1][:, :], sel[0:MH, h, :], rowsP[0:MH, S:2 * S]).then_inc(sm["pre_mm"], 1)
                        pp = Pt[:, OFF[j]:OFF[j] + S - P * j]
                        mm(ps[6][:, P * j:S], ones[:, :], pp, start=(j == 0), stop=(j == QT - 1))
                        mm(ps[7][:, P * j:S], vtm[:, P * j:P * j + P], pp, start=(j == 0),
                           stop=(j == QT - 1)).then_inc(sm["pv_mm"], 1)
                pe.wait_ge(sm["vw_ok"], h + 1)
                pe.wait_ge(sm["kt_ok"], h + 1)
                for j in range(QT):
                    last = mm(ps[4][:, 0:P], vw[:, P * j:P * j + P], ktm[:, P * j:P * j + P], start=(j == 0),
                              stop=(j == QT - 1))
                last.then_inc(sm["cn_mm"], 1)
                for j in range(QT):
                    last = mm(ps[5][0:1, 0:P], wsc[:, j:j + 1], ktm[:, P * j:P * j + P], start=(j == 0),
                              stop=(j == QT - 1))
                last.then_inc(sm["cn_mm"], 1)

            def y_here(layer):
                order = (0, 1, 4, 2, 5, 3, 6, 7) if layer == 0 else (4, 5, 6, 7, 0, 1, 2, 3)
                return lambda k: pe.wait_ge(sm["y_split"], KD * layer + max(order.index(j) for j in range(k + 1)) + 1)

            for j in range(KD):
                split_tiles((G_OUT0 + j,), xh, xl, y_here(0) if j == 0 else None)
            pe.wait_ge(sm["cn_ev"], 2 * MH)
            norm_sums(0, G_OUT0)
            mlp(0, G_MLP0)
            norm_sums(1, G_MLP0 + 2 * KF - KD)

            for idx, name in enumerate(O_NAMES):
                if idx == 0:
                    split_tiles((G_IN1, G_IN1 + 1), xh1, xl1, x_hi_here(1), x_lo_here(1))
                if idx > 1:
                    split_tiles((G_IN1 + idx,), xh1, xl1)
                if 4 <= idx <= 6:
                    n = idx - 4
                    i = 3 - n
                    g = G_IN1 + Z["qi"]
                    pe.wait_ge(sm["free_a"], g + 1)
                    pe.wait_ge(sm["free_b"], g + 1)
                    pe.wait_ge(sm["kiz_ok"], 4)
                    for e in range(4):
                        if n:
                            pe.wait_ge(sm["isc_r"], 4 * (n - 1) + e + 1)
                        mm(ps[4 + e][:, 0:P * (i + 1)], big[:, L["qi"], P * i:P * i + P],
                           kiz[:, e, 0:P * (i + 1)]).then_inc(sm["isc_mm"], 1)
                if idx == 3:
                    pe.wait_ge(sm["free_a"], G_IN1 + 1)
                    pe.wait_ge(sm["free_b"], G_IN1 + 1)
                    for i in range(QT):
                        tr(ps[4][:, 60 * i:60 * i + 60], big[0:60, L["misc"], P * i:P * i + P], 60)
                    tr(ps[5][0:B, 0:60], big[0:60, L["misc"], S:T], 60).then_inc(sm["t1_mm"], 1)
                    pe.wait_ge(sm["t1_ev"], 1)
                    mm(ps[6][0:64, 0:60], selB[0:B, :], mts[0:B, :])
                    mm(ps[7][0:32, 0:60], selE[0:B, :], mts[0:B, :]).then_inc(sm["sel_mm"], 1)
                    pe.wait_ge(sm["sel_ev"], 1)

            pe.wait_ge(sm["free_a"], G_OUT1)
            pe.wait_ge(sm["free_b"], G_OUT1)
            pe.wait_ge(sm["isc_r"], 12)
            for s, name in enumerate(SLOTS):
                if s >= 4:
                    pe.wait_ge(sm["tm_a"] if s % 2 == 0 else sm["tm_b"], (s - 4) // 2 + 1)
                for i in range(QT):
                    last = tr(ps[s % 4][:, P * i:P * i + P], big[:, L[name], P * i:P * i + P], P)
                last.then_inc(sm["tm_mm"], 1)
            for s, name in enumerate(SLOTS):
                last = tr(ps[4 + s // 4][0:B, P * (s % 4):P * (s % 4) + P], big[:, L[name], S:T], P)
            last.then_inc(sm["tms_mm"], 1)
            pe.wait_ge(sm["tm_a"], 4)
            pe.wait_ge(sm["tm_b"], 4)
            pe.wait_ge(sm["tms_ev"], 2)

            def cached_keys(st, n0, lhs_of, src_of, key_rows, acc_rows):
                if 0 <= st < 4:
                    if n0 + st:
                        pe.wait_ge(sm["bt_ev"], n0 + st)
                    else:
                        pe.wait_ge(sm["pct_ev"], 1)
                    for b in range(2):
                        for t in range(2):
                            last = tr(ps[4][0:key_rows, 256 * b + P * t:256 * b + P * t + P], src_of(2 * (2 * st + b) + t), P)
                    last.then_inc(sm["bt_mm"], 1)
                if 1 <= st <= 4:
                    pe.wait_ge(sm["bt_ev"], n0 + st)
                    for b in range(2):
                        bb = 2 * (st - 1) + b
                        last = mm(ps[7][0:acc_rows, 0:LS], lhs_of(bb), kTs[(st - 1) % 2][0:key_rows, b, :],
                                  start=(bb == 0), stop=(bb == B - 1))
                    last.then_inc(sm["bs_mm"], 1)

            def new_col(j, col):
                return tr(ps[7][:, 64 * j:64 * j + 64], col.to_broadcast([64, P]), 64)

            def sample_step(k):
                if k == 0:
                    pe.wait_ge(gat[4], 16 * NT)
                    pe.wait_ge(sm["qb_ok"], 3)
                if k <= 4:
                    cached_keys(k, 0, lambda b: QI[0:32, 32 * b:32 * b + 32], lambda t: kidx[:, t, :], 32, 32)
                if k == 5:
                    pe.wait_ge(sm["ix_r"], 1)
                    mm(ps[7][0:B, 0:LS], WI[0:32, :], rS).then_inc(sm["ixc_mm"], 1)
                if k == 9:
                    pe.wait_ge(sm["dsb_in"], 1)
                    mm(ps[7][0:64, 0:LS], selB[0:B, :], iscS).then_inc(sm["dsb_mm"], 1)
                if k == 5:
                    pe.wait_ge(sm["cw_ok"], 1)
                    pe.wait_ge(sm["bt_ev"], 4)
                    compress_cached(0)
                if k == 6:
                    pe.wait_ge(sm["cmp_ev"], 1)
                    for s in range(2):
                        last = tr(ps[4][:, 256 + 32 * s:288 + 32 * s], cmps[0:32, P * s:P * s + P], 32)
                    last.then_inc(sm["cmpt_mm"], 1)
                if k == 7:
                    pe.wait_ge(sm["cmpt_ev"], 1)
                    pe.wait_ge(sm["ixs_ev"], 1)
                    for b in range(B):
                        last = mm(ps[7][0:64, 0:NBS], QB["n"][:, 64 * b:64 * b + 64], kcTs[:, NBS * b:NBS * (b + 1)],
                                  start=(b == 0), stop=(b == B - 1))
                    last.then_inc(sm["bs_mm"], 1)
                if k == 10:
                    pe.wait_ge(sm["pn_ok"], 1)
                    pe.wait_ge(sm["dsd_ev"], 1)
                    for j in range(NBS):
                        last = new_col(j, sc4[0:64, j:j + 1])
                    last.then_inc(sm["pb_mm"], 1)
                for x, (br, (base, n0, where, q, n)) in enumerate(STEP.items()):
                    cb = cache[where]
                    if base <= k <= base + 4:
                        if k == base:
                            pe.wait_ge(gat[n], 16 if br == "w" else 16 * NT)
                        if k == base + 1:
                            pe.wait_ge(sm["pb_ev"], x + 1)
                        cached_keys(k - base, n0, lambda b, q=q: QB[q][:, 64 * b:64 * b + 64],
                                    lambda t, cb=cb: cb[:, t, 0:P], P, 64)
                    if k == base + 7:
                        pe.wait_ge(sm["pn_ok"], x + 2)
                        for t in range(2):
                            tr(ps[7][:, 64 * t:64 * t + 64], sbs[:, P * t:P * t + P], 64)
                        new_col(2, sbs[:, PAST:LS]).then_inc(sm["pt_mm"], 1)
                    if k == base + 8:
                        pe.wait_ge(sm["pt_ev"], x + 1)
                        cached_values(cb, 0)

            def compress_cached(half):
                for t in range(half * NT // 2, (half + 1) * NT // 2):
                    last = mm(ps[4][0:32, 0:256], BS[:, 30 - 2 * t:62 - 2 * t], cache["c"][:, t, :],
                              start=(t == 0), stop=(t == NT - 1))
                return last

            def cached_values(cb, half):
                for b in range(half * B // 2, (half + 1) * B // 2):
                    for t in range(2):
                        last = mm(ps[7][:, 192 + 8 * b:200 + 8 * b], cb[:, 2 * b + t, P:2 * P],
                                  PTs[:, t, 8 * b:8 * b + 8], start=(b == 0 and t == 0), stop=True)
                return last

            def sample_rest(k):
                if k == 5:
                    compress_cached(1).then_inc(sm["cmp_mm"], 1)
                for base, n0, where, q, n in STEP.values():
                    if k == base + 8:
                        cached_values(cache[where], 1).then_inc(sm["pvs_mm"], 1)

            def compressed_step(t):
                if 1 <= t <= QT:
                    pe.wait_ge(sm["kc_ok"], 1)
                    i = t - 1
                    for p in range(NP):
                        last = mm(ps[7][:, 64 * i + 16 * p:64 * i + 16 * p + 16], big[:, L["qn0"] + p, P * i:P * i + P], KCZ)
                    last.then_inc(sm["pc_mm"], 1)
                if t == QT:
                    for p in range(NP):
                        last = tr(ps[4][0:64, P * p:P * p + P], VF[:, p, :], P)
                    last.then_inc(sm["vf_mm"], 1)
                if t == 8:
                    pe.wait_ge(sm["vf_ev"], 1)
                    pe.wait_ge(sm["pc_n"], 1)
                    for i in range(QT):
                        last = tr(ps[4][0:64, P * i:P * i + P], sc[:, 64 * i:64 * i + 64], P)
                    last.then_inc(sm["pct_mm"], 1)

            VS = {"s": SLOTS.index("vs"), "w": SLOTS.index("vw"), "d": SLOTS.index("vd")}
            def unit_scores(u):
                i, p, g, br, k0, o = units[u]
                if u >= 2:
                    pe.wait_ge(sm["q_sc"], u - 1)
                if u == 0:
                    pe.wait_ge(sm["kz_ok"], 6)
                qn = "qd0" if br == "d" else "qn0"
                mm(ps[u % 2][:, 0:P * (i + 1 - k0)], big[:, L[qn] + p, P * i:P * i + P],
                   KZ["k" + br][:, g, P * k0:P * (i + 1)]).then_inc(sm["q_mm"], 1)

            unit_scores(0)
            for t in range(len(units) + 3):
                u = t - 2
                if 0 <= u < len(units):
                    i, p, g, br, k0, o = units[u]
                    pe.wait_ge(sm["q_n"], u + 1)
                    if u >= 2:
                        pe.wait_ge(sm["q_te"], u - 1)
                    for b in range(i + 1 - k0):
                        last = tr(ps[2 + u % 2][:, P * b:P * b + P], Pb[u % 2][:, P * b:P * b + P], P)
                    last.then_inc(sm["q_t"], 1)
                if t + 1 < len(units):
                    unit_scores(t + 1)
                u = t - 3
                if 0 <= u < len(units):
                    i, p, g, br, k0, o = units[u]
                    acc = ps[5 + o % 2]
                    if u == first_of[(o, 0)]:
                        if o >= 2:
                            pe.wait_ge(sm["q_of"], o - 1)
                        if br != "d":
                            pe.wait_ge(sm["pct_ev"], 1)
                            mm(acc[:, 0:P], VCb[:, p, :], PcT[:, P * i:P * i + P], stop=False)
                    pe.wait_ge(sm["q_te"], u + 1)
                    for b in range(i + 1 - k0):
                        v = tm[:, k0 + b, P * VS[br] + HD * g:P * VS[br] + HD * g + HD]
                        last = mm(acc[HD * g:HD * g + HD, 0:P], v, PTb[u % 2][:, P * b:P * b + P],
                                  start=(br == "d" and b == 0), stop=(b == i - k0))
                    last.then_inc(sm["q_o"], 1)
                compressed_step(t)
                if t >= START:
                    if (t - START) % EVERY == 0:
                        sample_step((t - START) // EVERY)
                    if (t - START) % EVERY == 1:
                        sample_rest((t - START) // EVERY)

            split_tiles((G_OUT1, G_OUT1 + 1), xh, xl, y_here(1))
            for j in range(2, KD):
                split_tiles((G_OUT1 + j,), xh, xl)
            norm_sums(2, G_OUT1)
            mlp(1, G_MLP1)
            norm_sums(3, G_MLP1 + 2 * KF - KD)

            for k in range(KD):
                half, kk = divmod(k, 4)
                pe.wait_ge(sm["x_ready"], xr(3) + k + 1)
                if k == 4:
                    pe.wait_ge(sm["y_b"], 1)
                for i in range(QT):
                    last = tr(ps[(i if half == 0 else 4 + i)][:, P * kk:P * kk + P], xT[:, k, P * i:P * i + P], P)
                    if kk == 3:
                        last.then_inc(sm["y_mm"], 1)
                if kk == 3 and half == 0:
                    pe.wait_ge(sm["std_ok"], 4)
                    for q in range(4):
                        last = tr(ps[4][0:B, P * q:P * q + P], xT[:, q, S:T], P)
                    last.then_inc(sm["y_mm"], 1)
            pe.wait_ge(sm["y_a"], 1)
            for q in range(4):
                last = tr(ps[0][0:B, P * q:P * q + P], xT[:, 4 + q, S:T], P)
            last.then_inc(sm["y_mm"], 1)

        @block.scalar
        def _(act):
            link = chain(act, sm["act_step"])
            one = ones[:, 0:1]

            def copy(out, in_, scale=1.0):
                return act.activation(out, in_, ACT.Copy, scale=scale)

            def tile_done(g):
                act.wait_ge(sm["mm_done"], g + 1)

            def w_hi(u, extra=None):
                c = plan[split[u]][0]
                act.wait_ge(w_sem[c % NSLOT], chunk_value[c])
                if extra:
                    act.wait_ge(sm[extra[0]], extra[1])
                else:
                    first, n = group(u)
                    if u - first >= n:
                        tile_done(split[u - n])
                copy(w_split(u)[0], w_raw(u)).then_inc(sm["w_hi"], 1)

            def w_hi_ahead(g):
                if ahead(g) is not None:
                    w_hi(ahead(g))

            def squares(n_ln, g0):
                for m in range(KD):
                    act.wait_ge(sm["free_a"], g0 + m + 1)
                    act.wait_ge(sm["free_b"], g0 + m + 1)
                    if m >= 2:
                        act.wait_ge(sm["sum_r"], (KD - 1) * n_ln + m - 1)
                    act.activation(sq[m % 2], xT[:, m, :], ACT.Square).then_inc(sm["sq_done"], 1)
                    w_hi_ahead(g0 + m)

            def mlp(layer, g):
                for c in range(NFC):
                    for j in range(KD):
                        n = KF * layer + KD * c + j
                        tile_done(g)
                        if n >= 2:
                            act.wait_ge(sm["hid_sq"], n - 1)
                            act.wait_ge(sm["hid_hi"], n - 1)
                        act.activation(rel[j % 2][:, 0:H2], psA(g)[:, 0:H2], ACT.Relu).then_inc(sm["free_a"], 1)
                        w_hi_ahead(g)
                        act.wait_ge(sm["free_a"], g + 1)
                        act.wait_ge(sm["free_b"], g + 1)
                        act.activation(hh[:, j, :], rel[j % 2], ACT.Square).then_inc(sm["hid_hi"], 1)
                        g += 1
                    if c < NFC - 1:
                        for j in range(KD):
                            w_hi_ahead(g)
                            g += 1
                    else:
                        squares(2 * layer + 1, g)

            def norm(n_ln):
                act.wait_ge(sm["std_in"], n_ln + 1)
                act.activation(rs, var, ACT.Sqrt).then_inc(sm["stats_ok"], 1)

                def affine(out, m):
                    return act.activation(out[:, m, :], xT[:, m, :], ACT.Identity, scale=colT[:, KD * n_ln + m:KD * n_ln + m + 1],
                                          bias=colT[:, 32 + KD * n_ln + m:33 + KD * n_ln + m])

                for m in range(KD + 1):
                    if m < KD:
                        act.wait_ge(sm["cen_v"], KD * n_ln + m + 1)
                        if n_ln not in SPLIT_NORMS:
                            affine(xT, m).then_inc(sm["x_ready"], 1)
                        else:
                            affine(XH[n_ln], m).then_inc(sm["x_hi"], 1)
                    if n_ln in SPLIT_NORMS and m - 1 in XT_ACT:
                        act.wait_ge(sm["x_hi"], KD * SPLIT_NORMS.index(n_ln) + m)
                        affine(xT, m - 1).then_inc(sm["x_ready"], 1)

            def y_hi(k, s, v):
                act.wait_ge(sm[s], v)
                copy(xh[:, k, :], ymix[:, k, :]).then_inc(sm["y_hi"], 1)

            for k in range(0, KD, 2):
                act.wait_ge(sm["tin"], k + 1)
                copy(xT[:, k, 0:S], ps[k % 6][:, :]).then_inc(sm["tin_a"], 1)

            for idx, t in enumerate(E_TILE):
                g = G_IN0 + idx
                tile_done(g)
                if idx == 0:
                    act.wait_ge(sm["small_in"], 16 * 2)
                    act.activation(gz[:, 0:H2], psA(g)[0:8, 0:H2], ACT.Identity, bias=gbc[0:8, :]).then_inc(sm["free_a"], 1)
                else:
                    copy(big[:, t, 0:H2], psA(g)[:, 0:H2], MH_SCALE if 16 <= t < 20 else 1.0).then_inc(sm["free_a"], 1)
                if idx == 2:
                    act.wait_ge(sm["nx_ok"], 1)
                    link(act.activation(lg, nx, ACT.Exp))
                    act.activation(lg, lg, ACT.Ln, bias=one[0:4, :]).then_inc(sm["sg_e"], 1)
                    act.wait_ge(sm["sp_ok"], 1)
                    act.activation(rowsP[0:MH, S:2 * S], nG, ACT.Exp)
                    act.activation(eS[0:MH, :], rowsS[0:MH, :], ACT.Exp).then_inc(sm["rows_ok"], 1)
                if idx >= 25:
                    act.wait_ge(sm["free_a"], g + 1)
                    act.wait_ge(sm["free_b"], g + 1)
                    act.activation(big[:, t, :], big[:, t, :], ACT.Exp, scale=-1.0).then_inc(sm["sg_e"], 1)
            act.wait_ge(sm["nnew_mm"], 1)
            copy(nno[0:MH * B, :], ps[4][0:MH * B, 0:P]).then_inc(sm["nnew_ev"], 1)
            act.wait_ge(sm["ucol_mm"], 1)
            copy(uo[0:B + 2, :], ps[5][0:B + 2, :]).then_inc(sm["ucol_ev"], 1)
            for h in range(MH):
                act.wait_ge(sm["pre_mm"], 4 * h + 1)
                if h:
                    act.wait_ge(sm["ws_ok"], h)
                link(copy(nml, ps[0][:, S - 1:S]))
                for i in range(QT):
                    if h:
                        act.wait_ge(sm["p_raw"], QT * (h - 1) + i + 1)
                    act.activation(Wt[:, OFF[i]:OFF[i] + S - P * i], ps[0][:, P * i:S], ACT.Exp,
                                   bias=aT[:, MH * i + h:MH * i + h + 1]).then_inc(sm["wt_ok"], 1)
                if h:
                    act.wait_ge(sm["cn_mm"], 2 * h)
                act.activation(wsc, aT.rearrange("p (i h) -> p i h", h=MH)[:, :, h], ACT.Exp, bias=nml).then_inc(sm["ws_ok"], 1)
                act.wait_ge(sm["pre_mm"], 4 * h + 3)
                copy(ktm, ps[3][:, :]).then_inc(sm["kt_ok"], 1)
                y_hi(h, "conv_ok", h + 1)
                act.wait_ge(sm["pv_mm"], QT * h + QT)
                if h:
                    act.wait_ge(sm["hd_fin"], h)
                copy(num, ps[7][:, :]).then_inc(sm["num_ok"], 1)
                if h == 1:
                    act.wait_ge(sm["smp_y"], 1)
                if h:
                    y_hi(MH + h - 1, "hd_fin", h)
                for n, (dst, src) in enumerate(((cst, ps[4][:, 0:P]), (nrow[0:1, :], ps[5][0:1, 0:P]))):
                    act.wait_ge(sm["cn_mm"], 2 * h + n + 1)
                    if h:
                        act.wait_ge(sm["store_c"], 16 * (MH + 2 * h))
                    copy(dst, src).then_inc(sm["cn_ev"], 1)
                if h == 2:
                    for u in range(2):
                        w_hi(u, ("store_c", 16 * (MH + 2 * h)))
            y_hi(KD - 1, "hd_fin", MH)
            for u in range(2, NW):
                w_hi(u, ("y_split", KD))
            squares(0, G_OUT0)
            norm(0)
            mlp(0, G_MLP0)
            for u in range(2):
                w_hi(split_of[G_IN1] + u)
            norm(1)

            for idx, name in enumerate(O_NAMES):
                g = G_IN1 + idx
                tile_done(g)
                m = 60 if name == "misc" else P
                copy(big[0:m, L[name], 0:H2], psA(g)[0:m, 0:H2], 0.125 if name[:2] in ("qn", "qd") else 1.0).then_inc(sm["free_a"], 1)
                w_hi_ahead(g)
                if idx == 3:
                    act.wait_ge(sm["gate_e"], 1)
                    act.activation(gt[:, :, :], gt[:, :, :], ACT.Exp, scale=-1.0)
                    act.activation(gS[0:64, :], gS[0:64, :], ACT.Exp, scale=-1.0).then_inc(sm["gate_e"], 1)
                if 4 <= idx <= 6:
                    n = idx - 4
                    i = 3 - n
                    for e in range(4):
                        act.wait_ge(sm["isc_mm"], 4 * n + e + 1)
                        if 4 * n + e >= 2:
                            act.wait_ge(sm["isc_used"], 4 * n + e - 1)
                        act.activation(rl[e % 2][:, 0:P * (i + 1)], ps[4 + e][:, 0:P * (i + 1)], ACT.Relu,
                                       scale=IDX_SCALE).then_inc(sm["isc_r"], 1)
            for s in range(0, 8, 2):
                act.wait_ge(sm["tm_mm"], s + 1)
                copy(tm[:, :, P * s:P * s + P], ps[s % 4][:, :].rearrange("p (i c) -> p i c", i=QT)).then_inc(sm["tm_a"], 1)
            act.wait_ge(sm["tms_mm"], 1)
            for n in range(2):
                copy(tms[:, 512 * n:512 * n + 512], ps[4 + n][0:B, :]).then_inc(sm["tms_ev"], 1)

            def cached_keys(st, n0, newkey, m=P):
                x = n0 + st
                act.wait_ge(sm["bt_mm"], x + 1)
                if x >= 2:
                    act.wait_ge(sm["bs_mm"], x - 1 + (1 if x >= 6 else 0))
                copy(kTs[st % 2][0:m, :, 0:PAST], ps[4][0:m, :].rearrange("p (b k) -> p b k", b=2))
                copy(kTs[st % 2][0:m, :, PAST:LS], big[0:m, L[newkey], S + 2 * st:S + 2 * st + 2].rearrange("p (b o) -> p b o", o=1)).then_inc(sm["bt_ev"], 1)

            def exponentials(dst, n):
                act.wait_ge(sm["sc_ok"], n + 1)
                act.activation(dst, dst, ACT.Exp, bias=nms[0:64, :], accum_out=rss[0:64, :]).then_inc(sm["pe_ok"], 1)

            def sample_step(k):
                if k < 4:
                    cached_keys(k, 0, "ki4", 32)
                if k == 4:
                    act.wait_ge(sm["bs_mm"], 4)
                    act.activation(rS, ps[7][0:32, 0:LS], ACT.Relu, scale=IDX_SCALE).then_inc(sm["ix_r"], 1)
                if k == 8:
                    exponentials(sc4[0:64, :], 0)
                for x, (br, (base, n0, *_)) in enumerate(STEP.items()):
                    if base <= k < base + 4:
                        cached_keys(k - base, n0, "k" + br)
                    if k == base + 5:
                        exponentials(sbs, x + 1)

            def compressed_step(t):
                if t == 5:
                    act.wait_ge(sm["pc_x"], 1)
                    act.activation(sc, sc, ACT.Exp).then_inc(sm["pc_e"], 1)
                if t == 9:
                    act.wait_ge(sm["pct_mm"], 1)
                    copy(PcT, ps[4][0:64, :]).then_inc(sm["pct_ev"], 1)

            for t in range(len(units) + 2):
                if t < len(units):
                    i, p, g, br, k0, o = units[t]
                    n = P * (i + 1 - k0)
                    act.wait_ge(sm["q_sc"], 0 + t + 1)
                    act.wait_ge(sm["q_m"], t + 1)
                    if t >= 2:
                        act.wait_ge(sm["q_t"], t - 1)
                    act.activation(Pb[t % 2][:, 0:n], sbb[t % 2][:, 0:n], ACT.Exp, bias=nmx[t % 2],
                                   accum_out=rsum[t % 2]).then_inc(sm["q_e"], 1)
                u = t - 2
                if u >= 0:
                    i, p, g, br, k0, o = units[u]
                    n = P * (i + 1 - k0)
                    act.wait_ge(sm["q_t"], u + 1)
                    if u >= 2:
                        act.wait_ge(sm["q_o"], u - 1)
                    copy(PTb[u % 2][:, 0:n], ps[2 + u % 2][:, 0:n]).then_inc(sm["q_te"], 1)
                compressed_step(t)
                if t >= START and (t - START) % EVERY == EVERY - 1:
                    sample_step((t - START) // EVERY)
                if t == EARLY:
                    for u in range(NS1, NS1 + 2):
                        w_hi(u, ("q_of", 16))
                if 4 <= t - EARLY < 4 + NP:
                    y_hi(NP + t - EARLY - 4, "q_of", SMP_DONE)
            for k in range(NP):
                y_hi(k, "q_of", (2 * QT - 2) * NP + 2 * k + 2)
            for u in range(NS1 + 2, NS1 + NW):
                w_hi(u, ("y_split", 2 * KD))
            squares(2, G_OUT1)
            norm(2)
            mlp(1, G_MLP1)
            norm(3)
            for half in range(2):
                for i in (0, 2):
                    act.wait_ge(sm["y_mm"], (QT + 1) * half + i + 1)
                    copy(ytm[:, i, 512 * half:512 * half + 512], ps[4 * half + i][:, :]).then_inc(sm["y_a"], 1)

        @block.vector
        def _(dve):
            link = chain(dve, sm["dve_step"])

            def tile_done(g):
                dve.wait_ge(sm["mm_done"], g + 1)

            def w_lo(u):
                if low[u][0] != "w_lo":
                    return
                dve.wait_ge(sm["w_hi"], u + 1)
                w_h, w_l = w_split(u)
                dve.tensor_tensor(w_l, w_raw(u), w_h.bitcast(F32), ALU.subtract).then_inc(sm["w_lo"], 1)

            def w_lo_ahead(g):
                if ahead(g) is not None:
                    w_lo(ahead(g))

            def residual(g0, scale=ALPHA):
                for m in range(KD):
                    g = g0 + m
                    tile_done(g)
                    for c0, bank, free in ((0, psA(g), "free_a"), (H2, psB(g), "free_b")):
                        x = xT[:, m, c0:c0 + H2]
                        last = (dve.tensor_tensor(x, x, bank[:, 0:H2], ALU.add) if scale is None
                                else dve.scalar_tensor_tensor(x, x, scale, bank[:, 0:H2], ALU.mult, ALU.add))
                        last.then_inc(sm[free], 1)
                    w_lo_ahead(g)

            def mlp(layer, g):
                for c in range(NFC):
                    for j in range(KD):
                        n = KF * layer + KD * c + j
                        tile_done(g)
                        if n >= 2:
                            dve.wait_ge(sm["hid_sq"], n - 1)
                            dve.wait_ge(sm["hid_hi"], n - 1)
                        dve.tensor_scalar(rel[j % 2][:, H2:T], psB(g)[:, 0:H2], 0.0, None, ALU.max).then_inc(sm["free_b"], 1)
                        w_lo_ahead(g)
                        dve.wait_ge(sm["hid_sq"], n + 1)
                        dve.wait_ge(sm["hid_hi"], n + 1)
                        dve.tensor_tensor(hl[:, j, :], hid[j % 2], hh[:, j, :].bitcast(F32), ALU.subtract).then_inc(sm["hid_lo"], 1)
                        g += 1
                    residual(g, ALPHA if c == 0 else None)
                    g += KD

            def norm(n_ln):
                dve.wait_ge(sm["stats_mm"], n_ln + 1)
                dve.tensor_copy(mu[:, 0:H2], ps[4][:, 0:H2])
                dve.tensor_copy(mu[:, H2:T], ps[5][:, 0:H2]).then_inc(sm["mu_ok"], 1)
                dve.wait_ge(sm["mu_ok"], n_ln + 1)
                link(dve.tensor_tensor(var, mu, mu, ALU.mult))
                dve.tensor_tensor(var[:, 0:H2], ps[6][:, 0:H2], var[:, 0:H2], ALU.subtract)
                link(dve.tensor_tensor(var[:, H2:T], ps[7][:, 0:H2], var[:, H2:T], ALU.subtract))
                dve.tensor_scalar(var, var, 0.0, LN_EPS, ALU.max, ALU.add).then_inc(sm["std_in"], 1)

                def centre(m):
                    link(dve.tensor_tensor(xT[:, m, :], xT[:, m, :], mu, ALU.subtract))

                mine = [m for m in range(KD) if m not in LN_POOL]
                centre(mine[0])
                dve.wait_ge(sm["stats_ok"], n_ln + 1)
                dve.reciprocal(rs, rs).then_inc(sm["std_ok"], 1)
                dve.wait_ge(sm["std_ok"], n_ln + 1)
                lows = 0
                for m in range(KD + 1):
                    if m < KD:
                        if m in LN_POOL:
                            dve.wait_ge(sm["cen_p"], len(LN_POOL) * n_ln + LN_POOL.index(m) + 1)
                        elif m != mine[0]:
                            centre(m)
                        dve.tensor_tensor(xT[:, m, :], xT[:, m, :], rs, ALU.mult).then_inc(sm["cen_v"], 1)
                    if n_ln in SPLIT_NORMS and m >= 1:
                        n = SPLIT_NORMS.index(n_ln)
                        q = m - 1
                        if q not in XT_ACT:
                            dve.wait_ge(sm["x_hi"], KD * n + q + 1)
                            dve.wait_ge(sm["cen_v"], KD * n_ln + q + 1)
                            link(dve.tensor_scalar(xT[:, q, :], xT[:, q, :], colT[:, KD * n_ln + q:KD * n_ln + q + 1],
                                                   colT[:, 32 + KD * n_ln + q:33 + KD * n_ln + q], ALU.mult, ALU.add))
                        elif q in XL_DVE:
                            dve.wait_ge(sm["x_ready"], xr(n_ln) + XT_ACT.index(q) + 1)
                        if q in XL_DVE:
                            dve.tensor_tensor(XL[n_ln][:, q, :], xT[:, q, :], XH[n_ln][:, q, :].bitcast(F32), ALU.subtract).then_inc(sm["xl_v"], 1)

            for k in range(1, KD, 2):
                dve.wait_ge(sm["tin"], k + 1)
                dve.tensor_copy(xT[:, k, 0:S], ps[k % 6][:, :]).then_inc(sm["tin_b"], 1)
            dve.wait_ge(sm["tin"], KD + 1)
            dve.tensor_copy(xT[:, :, S:T], ps[6][:, 0:KD * B].rearrange("p (k b) -> p k b", k=KD)).then_inc(sm["tin_b"], 1)
            dve.wait_ge(sm["tin"], KD + 2)
            dve.tensor_copy(colT[:, :], ps[7][:, 0:112]).then_inc(sm["tin_b"], 1)
            dve.wait_ge(sm["tin_b"], KD // 2 + 2)

            def bc(kind):
                return bcS.rearrange("p (h k b) -> p h k b", h=MH, k=3)[:, :, kind, :]

            def hb(v):
                return v.rearrange("p (h b) -> p h b", h=MH)

            def gates():
                dve.wait_ge(sm["fg_mm"], 1)
                dve.tensor_copy(fgt[:, 0:H2], ps[4][0:4, 0:H2])
                link(dve.tensor_copy(fgt[:, H2:T], ps[5][0:4, 0:H2]))
                dve.scalar_tensor_tensor(nx, fgt, -1.0, fgt, ALU.mult, ALU.min).then_inc(sm["nx_ok"], 1)
                dve.wait_ge(sm["sg_e"], 1)
                link(dve.scalar_tensor_tensor(lg, fgt, 0.0, lg, ALU.min, ALU.subtract))
                link(dve.tensor_tensor_scan(Fc, ones[0:4, 0:1].to_broadcast([4, S]), lg[:, 0:S], 0.0, ALU.mult, ALU.add))
                dve.wait_ge(sm["free_a"], 1)
                link(dve.tensor_tensor(at_, gz[0:4, 0:S], Fc, ALU.subtract))
                link(dve.tensor_tensor_scan(Mr, at_, at_, 0.0, ALU.max, ALU.max))
                dve.tensor_scalar(rowsP[0:MH, 0:S], Mr, -1.0, None, ALU.mult)
                link(dve.scalar_tensor_tensor(nG, Fc, -1.0, Mr, ALU.mult, ALU.subtract))
                dve.tensor_scalar(mpc[0:MH, :], nG[:, S - 1:S], -1.0, None, ALU.mult)
                link(dve.tensor_tensor(interS[0:MH, :], lg[:, S:T], stm[0:MH, :], ALU.add))
                link(dve.tensor_tensor(mtS[0:MH, :], interS[0:MH, :], gz[0:4, S:T], ALU.max))
                dve.tensor_tensor(rowsS[0:MH, 0:B], interS[0:MH, :], mtS[0:MH, :], ALU.subtract)
                dve.tensor_tensor(rowsS[0:MH, B:2 * B], gz[0:4, S:T], mtS[0:MH, :], ALU.subtract)
                dve.tensor_scalar(rowsS[0:MH, 2 * B:3 * B], mtS[0:MH, :], -1.0, None, ALU.mult).then_inc(sm["sp_ok"], 1)

            def sample_products():
                dve.wait_ge(sm["h12_mm"], 1)
                dve.tensor_copy(aT, ps[4][:, 0:16])
                dve.tensor_copy(bcS, ps[5][:, 0:96])
                dve.tensor_copy(scT, ps[7][:, 0:64])
                dve.wait_ge(sm["free_b"], 13)
                n_hb = colT[:, 80:112].rearrange("p (b h) -> p h b", h=MH)
                dve.tensor_tensor(hb(prod[:, 0:32]), n_hb, big[:, 12:16, S:T], ALU.mult)
                dve.tensor_tensor(hb(prod[:, 32:64]), big[:, 16:20, S:T], big[:, 12:16, S:T],
                                  ALU.mult).then_inc(sm["prod_ok"], 1)

            def sample_weights():
                n_hb = colT[:, 80:112].rearrange("p (b h) -> p h b", h=MH)
                nn_hb = nnw.rearrange("p (b h) -> p h b", h=MH)
                dve.wait_ge(sm["dots_mm"], 1)
                link(dve.tensor_copy(dts, ps[4][:, 0:64]))
                dve.tensor_tensor(hb(swa), hb(dts[:, 32:64]), bc(1), ALU.mult)
                link(dve.tensor_tensor(hb(recS), hb(dts[:, 0:32]), bc(0), ALU.mult))
                link(dve.tensor_tensor(recS, recS, swa, ALU.add))
                link(dve.scalar_tensor_tensor(recS, recS, -1.0, recS, ALU.mult, ALU.max))
                link(dve.tensor_tensor(hb(recS), hb(recS), bc(2), ALU.max))
                dve.reciprocal(recS, recS)
                dve.tensor_tensor(nn_hb, n_hb, bc(0), ALU.mult)
                link(dve.tensor_tensor(hb(vwS), big[:, 16:20, S:T], bc(1), ALU.mult))
                link(dve.tensor_tensor(nn_hb, nn_hb, hb(vwS), ALU.add))
                dve.tensor_tensor(hb(vwS), big[:, 20:24, S:T], bc(1), ALU.mult).then_inc(sm["nnew_ok"], 1)
                dve.wait_ge(sm["nnew_ok"], 1)

            def sample_head(h):
                def bd(bank):
                    return bank[:, :].rearrange("p (b d) -> p b d", b=4)
                dve.wait_ge(sm["head_mm"], h + 1)
                if h == 0:
                    dve.wait_ge(sm["c_in"], 16 * MH)
                for j in range(2):
                    last = dve.tensor_tensor(tmpS[:, 4 * j:4 * j + 4, :], Ct[:, h, 4 * j:4 * j + 4, :], bd(ps[4 + j]), ALU.mult)
                link(last)
                dve.tensor_reduce(cq[:, B * h:B * h + B], tmpS, AX.X, ALU.add)
                link(dve.tensor_tensor(Ct[:, h], Ct[:, h], bc(0)[:, h, :].unsqueeze(2).to_broadcast([P, B, P]), ALU.mult))
                for j in range(2):
                    v = vwS[:, B * h + 4 * j:B * h + 4 * j + 4]
                    last = dve.tensor_tensor(tmpS[:, 4 * j:4 * j + 4, :], bd(ps[6 + j]), v.unsqueeze(2).to_broadcast([P, 4, P]), ALU.mult)
                last.then_inc(sm["head_used"], 1)
                dve.wait_ge(sm["head_used"], h + 1)
                dve.tensor_tensor(Ct[:, h], Ct[:, h], tmpS, ALU.add).then_inc(sm["c_new"], 1)
                dve.wait_ge(sm["c_new"], h + 1)

            def convolve(i):
                def w(j):
                    return colT[:, 64 + 4 * j + i:65 + 4 * j + i]
                u, y = big[:, i, :], ymix[:, i, :]
                old = scT.rearrange("p (c b j) -> p c b j", c=4, b=B)[:, i]
                dve.wait_ge(sm["u_ok"], i + 1)
                dve.wait_ge(sm["free_a"], G_IN0 + 22 + i)
                link(dve.tensor_scalar(y, u, w(2), colT[:, 76 + i:77 + i], ALU.mult, ALU.add))
                dve.scalar_tensor_tensor(y[:, 1:S], u[:, 0:S - 1], w(1), y[:, 1:S], ALU.mult, ALU.add)
                link(dve.scalar_tensor_tensor(y[:, S:T], old[:, :, 1], w(1), y[:, S:T], ALU.mult, ALU.add))
                dve.scalar_tensor_tensor(y[:, 2:S], u[:, 0:S - 2], w(0), y[:, 2:S], ALU.mult, ALU.add)
                link(dve.scalar_tensor_tensor(y[:, S:T], old[:, :, 0], w(0), y[:, S:T], ALU.mult, ALU.add))
                dve.tensor_tensor(y, y, big[:, 4 + i, :], ALU.mult).then_inc(sm["conv_ok"], 1)

            for idx, t in enumerate(E_TILE):
                g = G_IN0 + idx
                tile_done(g)
                if idx == 0:
                    dve.wait_ge(sm["small_in"], 16 * 2)
                    dve.tensor_scalar(gz[:, H2:T], psB(g)[0:8, 0:H2], gbc[0:8, :], None, ALU.add).then_inc(sm["free_b"], 1)
                    dve.wait_ge(sm["free_b"], 1)
                elif 16 <= t < 20:
                    dve.tensor_scalar(big[:, t, H2:T], psB(g)[:, 0:H2], MH_SCALE, None, ALU.mult).then_inc(sm["free_b"], 1)
                else:
                    dve.tensor_copy(big[:, t, H2:T], psB(g)[:, 0:H2]).then_inc(sm["free_b"], 1)
                if idx == 2:
                    gates()
                if idx == 5:
                    dve.wait_ge(sm["tin"], KD + 3)
                    dve.tensor_copy(wcT, ps[7][:, 0:2 * BLK]).then_inc(sm["tin_b"], 1)
                if idx == 12:
                    sample_products()
                if idx == 14:
                    sample_weights()
                if idx in (16, 18, 20, 22):
                    sample_head((idx - 16) // 2)
                if 21 <= idx <= 24:
                    dve.wait_ge(sm["free_b"], g + 1)
                    convolve(idx - 21)
                if idx >= 25:
                    dve.wait_ge(sm["sg_e"], idx - 23)
                    link(dve.tensor_scalar(big[:, t, :], big[:, t, :], 1.0, None, ALU.add))
                    link(dve.reciprocal(big[:, t, :], big[:, t, :]))
            dve.tensor_tensor(hb(hS), hb(cq), bc(0), ALU.mult)
            link(dve.tensor_tensor(hb(prod[:, 0:32]), big[:, 20:24, S:T], hb(swa), ALU.mult))
            link(dve.tensor_tensor(hS, hS, prod[:, 0:32], ALU.add))
            link(dve.tensor_tensor(hS, hS, recS, ALU.mult))
            dve.tensor_tensor(ymix[:, 4:8, S:T], hb(hS), big[:, 24:28, S:T], ALU.mult).then_inc(sm["smp_y"], 1)

            def divide(h):
                dve.wait_ge(sm["den_ok"], h + 1)
                link(dve.reciprocal(dn, dn))
                dve.wait_ge(sm["num_ok"], h + 1)
                link(dve.tensor_tensor(dn, num, dn, ALU.mult))
                dve.tensor_tensor(ymix[:, 4 + h, 0:S], dn, big[:, 24 + h, 0:S], ALU.mult).then_inc(sm["hd_fin"], 1)
                dve.wait_ge(sm["hd_fin"], h + 1)

            for h in range(MH):
                dve.wait_ge(sm["pre_mm"], 4 * h + 2)
                if h:
                    dve.wait_ge(sm["pv_mm"], QT * h)
                dve.tensor_copy(vtm, ps[2][:, :]).then_inc(sm["vt_ok"], 1)
                for i in range(QT):
                    dve.wait_ge(sm["s_mm"], QT * h + i + 1)
                    dve.wait_ge(sm["wt_ok"], QT * h + i + 1)
                    n = S - P * i
                    dve.tensor_tensor(Pt[:, OFF[i]:OFF[i] + n], ps[4 + i % 2][:, 0:n], Wt[:, OFF[i]:OFF[i] + n],
                                      ALU.mult).then_inc(sm["p_raw"], 1)
                    if h and i == 1:
                        divide(h - 1)
                dve.wait_ge(sm["ws_ok"], h + 1)
                dve.wait_ge(sm["vt_ok"], h + 1)
                if h:
                    dve.wait_ge(sm["cn_mm"], 2 * h)
                dve.tensor_tensor(vw.rearrange("p (i d) -> p i d", i=QT), vtm.rearrange("p (i d) -> p i d", i=QT),
                                  wsc.unsqueeze(2).to_broadcast([P, QT, P]), ALU.mult).then_inc(sm["vw_ok"], 1)
                dve.wait_ge(sm["pv_mm"], QT * h + QT)
                link(dve.tensor_scalar(dn, ps[6][:, :], -1.0, None, ALU.mult))
                link(dve.tensor_tensor(dn, dn, ps[6][:, :], ALU.max))
                dve.tensor_tensor(dn, dn, ps[1][:, :], ALU.max).then_inc(sm["den_ok"], 1)
                if h == 2:
                    for u in range(2):
                        w_lo(u)
            divide(MH - 1)
            for u in range(2, NW):
                w_lo(u)
            residual(G_OUT0)
            norm(0)
            mlp(0, G_MLP0)
            for u in range(2):
                w_lo(split_of[G_IN1] + u)
            norm(1)

            def small_odd():
                dve.wait_ge(sm["t1_mm"], 1)
                src = ps[4][:, 0:240].rearrange("p (i c) -> p i c", i=QT)
                dve.tensor_copy(mtm[:, :, :], src)
                dve.tensor_copy(gt[:, :, :], src[:, :, 0:24])
                dve.tensor_copy(mts[0:B, :], ps[5][0:B, 0:60]).then_inc(sm["t1_ev"], 1)
                i64, i32 = ident[0:64, 0:64], ident[0:32, 0:32]
                dve.tensor_reduce(mask64[0:64, :], i64.rearrange("p (b h) -> p h b", h=NH), AX.X, ALU.add)
                dve.tensor_reduce(mask32[0:32, :], i32.rearrange("p (b e) -> p e b", e=4), AX.X, ALU.add)
                dve.tensor_reduce(bsel32[0:32, :], i32.rearrange("p (b e) -> p b e", e=4), AX.X, ALU.add)
                dve.wait_ge(sm["sel_mm"], 1)
                dve.tensor_copy(gsel[0:64, :], ps[6][0:64, 0:60])
                dve.tensor_copy(ixE[0:32, :], ps[7][0:32, 0:60]).then_inc(sm["sel_ev"], 1)
                dve.wait_ge(sm["sel_ev"], 1)
                link(dve.tensor_tensor(g24[0:64, :].rearrange("p (h c) -> p h c", c=3),
                                       gsel[0:64, 0:24].rearrange("p (h c) -> p h c", c=3),
                                       mask64[0:64, :].unsqueeze(2).to_broadcast([64, NH, 3]), ALU.mult))
                dve.tensor_reduce(gS[0:64, :], g24[0:64, :].rearrange("p (h c) -> p c h", c=3), AX.X,
                                  ALU.add).then_inc(sm["gate_e"], 1)
                link(dve.tensor_tensor(wE[0:32, :], ixE[0:32, 56:60], mask32[0:32, :], ALU.mult))
                link(dve.tensor_reduce(wi32[0:32, :], wE[0:32, :], AX.X, ALU.add))
                dve.tensor_scalar(WI[0:32, :], bsel32[0:32, :], wi32[0:32, :], 0.5, ALU.mult, ALU.mult)
                link(dve.tensor_tensor(mask64[0:64, :], mask64[0:64, :], slope8[0:64, :], ALU.mult))
                dve.tensor_reduce(sl64[0:64, :], mask64[0:64, :], AX.X, ALU.add)
                dve.tensor_scalar(cm, D0[:, S - P:S], 0.5 * NEG, NEG, ALU.is_lt, ALU.mult)
                dve.tensor_scalar(Mc, Dc, 0.5 * NEG, None, ALU.is_ge)
                dve.wait_ge(sm["gate_e"], 2)
                dve.tensor_scalar(gt[:, :, :], gt[:, :, :], 1.0, None, ALU.add)
                link(dve.tensor_scalar(gS[0:64, :], gS[0:64, :], 1.0, None, ALU.add))
                dve.reciprocal(gt[:, :, :], gt[:, :, :])
                link(dve.reciprocal(gS[0:64, :], gS[0:64, :]))

            def indexer_scores(n):
                i = 3 - n
                w = P * (i + 1)
                tab = TAB[i]
                for e in range(4):
                    dve.wait_ge(sm["isc_r"], 4 * n + e + 1)
                    wie = mtm[:, i, 56 + e:57 + e]
                    last = (dve.tensor_scalar(tab, rl[0][:, 0:w], wie, None, ALU.mult) if e == 0
                            else dve.scalar_tensor_tensor(tab, rl[e % 2][:, 0:w], wie, tab, ALU.mult, ALU.add))
                    last.then_inc(sm["isc_used"], 1)
                    dve.wait_ge(sm["isc_used"], 4 * n + e + 1)
                dve.tensor_scalar(tab[:, 0:P * i], tab[:, 0:P * i], 0.5, None, ALU.mult)
                link(dve.scalar_tensor_tensor(tab[:, P * i:w], tab[:, P * i:w], 0.5, cm, ALU.mult, ALU.add))

            steps = [(i, r) for i in (3, 2, 1) for r in range(TOPK // 8)]

            def top_keys(n):
                for i, r in steps[:n]:
                    tab = TAB[i]
                    link(dve.max(m8, tab))
                    link(dve.match_replace(tab, m8, tab, TAKEN))
                    if r == TOPK // 8 - 1:
                        link(dve.tensor_scalar(tab, tab, 0.5 * TAKEN, NEG, ALU.is_gt, ALU.mult))
                        link(dve.tensor_tensor(tab, tab, D0[:, S - P * (i + 1):S], ALU.add))
                del steps[:n]

            def compress(src, dst):
                w = wcT[:, 0:BLK] if src == "kc" else wcT[:, BLK:2 * BLK]
                dve.wait_ge(sm["free_a"], G_IN1 + Z[src] + 1)
                dve.wait_ge(sm["free_b"], G_IN1 + Z[src] + 1)
                link(dve.tensor_tensor(tmpc.rearrange("p (j t) -> p j t", t=BLK),
                                       big[:, L[src], 0:S].rearrange("p (j t) -> p j t", t=BLK),
                                       w.unsqueeze(1).to_broadcast([P, NB, BLK]), ALU.mult))
                link(dve.tensor_reduce(dst, tmpc.rearrange("p (j t) -> p j t", t=BLK), AX.X, ALU.add))

            c4 = "p (i c j) -> p i c j"
            slop = slopes.unsqueeze(1).unsqueeze(3).to_broadcast([P, QT, NH, NB])
            dcv = Dc.rearrange("p (i j) -> p i j", i=QT).unsqueeze(2).to_broadcast([P, QT, NH, NB])
            mcv = Mc.rearrange("p (i j) -> p i j", i=QT).unsqueeze(2).to_broadcast([P, QT, NH, NB])

            def place_compressed():
                dve.memset(KCZ, 0.0)
                link(dve.memset(VF, 0.0))
                for g in range(2):
                    r = slice(HD * g, HD * g + HD)
                    last = dve.tensor_copy(KCZ[r, NB * g:NB * g + NB], kcT[r, :])
                    for p in range(NP):
                        last = dve.tensor_copy(VF[r, p, 16 * p + NB * g:16 * p + NB * g + NB], vcT[r, :])
                last.then_inc(sm["kc_ok"], 1)
                link(dve.tensor_tensor(sD.rearrange(c4, i=QT, c=NH), dcv, slop, ALU.mult))

            def place_queries(br):
                link(dve.memset(QB[br], 0.0))
                for g in range(2):
                    r = slice(HD * g, HD * g + HD)
                    for p in range(NP):
                        h = NP * g + p
                        last = dve.tensor_copy(QB[br][r, h:h + 72 * 7 + 1:72], big[r, L[f"q{br}0"] + p, S:T])
                last.then_inc(sm["qb_ok"], 1)

            def sample_queries(t):
                if t == 2:
                    link(dve.memset(QI, 0.0))
                    for e in range(4):
                        r = slice(32 * e, 32 * e + 32)
                        last = dve.tensor_copy(QI[0:32, e:e + 36 * 7 + 1:36], big[r, L["qi"], S:T])
                    last.then_inc(sm["qb_ok"], 1)
                if t == 3:
                    place_queries("n")
                if t == 7:
                    dve.tensor_copy(vals[:, 32:40], big[:, L["vs"], S:T])
                    link(dve.tensor_copy(vals[:, 40:48], big[:, L["vw"], S:T]))

            for idx, name in enumerate(O_NAMES):
                g = G_IN1 + idx
                tile_done(g)
                m = 60 if name == "misc" else P
                if name[:2] in ("qn", "qd"):
                    dve.tensor_scalar(big[:, L[name], H2:T], psB(g)[:, 0:H2], 0.125, None, ALU.mult).then_inc(sm["free_b"], 1)
                else:
                    dve.tensor_copy(big[0:m, L[name], H2:T], psB(g)[0:m, 0:H2]).then_inc(sm["free_b"], 1)
                w_lo_ahead(g)
                if idx == 3:
                    small_odd()
                if 4 <= idx <= 6:
                    indexer_scores(idx - 4)
                if idx in (5, 6):
                    top_keys(2)
                if 7 <= idx < len(O_NAMES) - 1:
                    top_keys(4)
                if idx == Z["qd3"] + 1:
                    dve.wait_ge(sm["free_b"], G_IN1 + Z["qd3"] + 1)
                    place_queries("d")
                if idx == Z["kc"] + 1:
                    compress("kc", kcT)
                if idx == Z["vc"] + 1:
                    compress("vc", vcT)
            dve.wait_ge(sm["free_b"], G_OUT1)
            for s in range(1, 8, 2):
                dve.wait_ge(sm["tm_mm"], s + 1)
                dve.tensor_copy(tm[:, :, P * s:P * s + P], ps[s % 4][:, :].rearrange("p (i c) -> p i c", i=QT)).then_inc(sm["tm_b"], 1)
            def compressed_step(t):
                if t == 0:
                    place_compressed()
                if t == 4:
                    dve.wait_ge(sm["pc_mm"], QT)
                    link(dve.tensor_tensor(sc, ps[7][:, 0:256], sD, ALU.add))
                    link(dve.tensor_reduce(mxc, sc.rearrange("p (c j) -> p c j", j=NB), AX.X, ALU.max))
                    dve.tensor_tensor(sc.rearrange("p (c j) -> p c j", j=NB), sc.rearrange("p (c j) -> p c j", j=NB),
                                      mxc.unsqueeze(2).to_broadcast([P, 32, NB]), ALU.subtract).then_inc(sm["pc_x"], 1)
                if t == 5:
                    dve.wait_ge(sm["vf_mm"], 1)
                    dve.tensor_copy(VCb.rearrange("p q c -> p (q c)"), ps[4][0:64, :]).then_inc(sm["vf_ev"], 1)
                if t == 6:
                    dve.wait_ge(sm["pc_e"], 1)
                    link(dve.tensor_tensor(sc.rearrange(c4, i=QT, c=NH), sc.rearrange(c4, i=QT, c=NH), mcv, ALU.mult))
                    link(dve.tensor_reduce(rcc, sc.rearrange("p (c j) -> p c j", j=NB), AX.X, ALU.add))
                    link(dve.tensor_scalar(rcc, rcc, 1e-30, None, ALU.max))
                    link(dve.reciprocal(rcc, rcc))
                    link(dve.tensor_tensor(rcc.rearrange("x (i p g) -> x i p g", i=QT, p=NP),
                                           rcc.rearrange("x (i p g) -> x i p g", i=QT, p=NP),
                                           gt[:, :, :].rearrange("x i (g p c) -> x i p g c", g=2, p=NP)[:, :, :, :, 0], ALU.mult))
                    dve.tensor_tensor(sc.rearrange("p (c j) -> p c j", j=NB), sc.rearrange("p (c j) -> p c j", j=NB),
                                      rcc.unsqueeze(2).to_broadcast([P, 32, NB]), ALU.mult).then_inc(sm["pc_n"], 1)

            def weighted(dst, j, v):
                return dve.tensor_tensor(dst.rearrange("p (b h) -> p b h", h=NH),
                                         ps[7][:, 64 * j:64 * j + 64].rearrange("p (b h) -> p b h", h=NH),
                                         v.unsqueeze(2).to_broadcast([P, B, NH]), ALU.mult)

            def scores(dst, w, tab, n):
                dve.wait_ge(sm["bs_mm"], n)
                link(dve.scalar_tensor_tensor(dst, tab, sl64[0:64, :], ps[7][0:64, 0:w], ALU.mult, ALU.add))
                dve.tensor_reduce(nms[0:64, :], dst, AX.X, ALU.max, negate=True).then_inc(sm["sc_ok"], 1)

            def normalise(dst, n, gate):
                dve.wait_ge(sm["pe_ok"], n + 1)
                link(dve.tensor_scalar(rss[0:64, :], rss[0:64, :], 1e-30, None, ALU.max))
                link(dve.reciprocal(rcs[0:64, :], rss[0:64, :]))
                if gate is not None:
                    link(dve.tensor_tensor(rcs[0:64, :], rcs[0:64, :], gS[0:64, gate:gate + 1], ALU.mult))
                dve.tensor_scalar(dst, dst, rcs[0:64, :], None, ALU.mult).then_inc(sm["pn_ok"], 1)

            def sample_step(k):
                if k == 5:
                    dve.wait_ge(sm["cmp_mm"], 1)
                    dve.tensor_copy(cmps[0:32, :], ps[4][0:32, 0:256]).then_inc(sm["cmp_ev"], 1)
                    dve.wait_ge(sm["ixc_mm"], 1)
                    dve.tensor_copy(iscS, ps[7][0:B, 0:LS]).then_inc(sm["ixs_ev"], 1)
                    dve.wait_ge(sm["ixs_ev"], 1)
                if k == 6:
                    dve.wait_ge(sm["cmpt_mm"], 1)
                    dve.tensor_copy(kcTs, ps[4][:, 256:288])
                    dve.tensor_copy(vals[:, 0:32].rearrange("p (j b) -> p j b", b=B),
                                    ps[4][:, 288:320].rearrange("p (b j) -> p j b", b=B)).then_inc(sm["cmpt_ev"], 1)
                if k == 7:
                    scores(sc4[0:64, :], NBS, Dcs[0:64, :], 5)
                if 5 <= k <= 8:
                    for r in range(TOPK_S // 32):
                        link(dve.max(m8s[0:B, :], iscS))
                        link(dve.match_replace(iscS, m8s[0:B, :], iscS, TAKEN))
                if k == 8:
                    link(dve.tensor_scalar(iscS, iscS, 0.5 * TAKEN, NEG, ALU.is_gt, ALU.mult))
                    dve.tensor_tensor(iscS, iscS, Ds[0:B, :], ALU.add).then_inc(sm["dsb_in"], 1)
                if k == 9:
                    dve.wait_ge(sm["dsb_mm"], 1)
                    dve.tensor_copy(DdS, ps[7][0:64, 0:LS]).then_inc(sm["dsd_ev"], 1)
                    normalise(sc4[0:64, :], 0, 0)
                if k == 10:
                    dve.wait_ge(sm["pb_mm"], 1)
                    for j in range(NBS):
                        last = weighted(pbt[:, 64 * j:64 * j + 64], j, vals[:, B * j:B * j + B])
                    last.then_inc(sm["pb_ev"], 1)
                for x, (br, (base, n0, *_)) in enumerate(STEP.items()):
                    if k == base + 4:
                        scores(sbs, LS, {"s": Ds[0:64, :], "d": DdS, "w": Dws[0:64, :]}[br], n0 + 5)
                    if k == base + 6:
                        normalise(sbs, x + 1, {"s": 1, "d": None, "w": 2}[br])
                    if k == base + 7:
                        dve.wait_ge(sm["pt_mm"], x + 1)
                        if br == "d":
                            weighted(oD, 2, big[:, L["vd"], S:T])
                        else:
                            j = 4 if br == "s" else 5
                            weighted(pbt[:, 64 * j:64 * j + 64], 2, vals[:, B * j:B * j + B])
                        dve.tensor_copy(PTs[:, :, :], ps[7][:, 0:128].rearrange("p (t c) -> p t c", t=2)).then_inc(sm["pt_ev"], 1)
                    if k == base + 8:
                        dve.wait_ge(sm["pvs_mm"], x + 1)
                        acc = ps[7][:, 192:256]
                        dve.wait_ge(sm["pt_ev"], x + 1)
                        if br == "s":
                            dve.tensor_copy(oN, acc).then_inc(sm["pb_ev"], 1)
                        if br == "d":
                            dve.tensor_tensor(oD, oD, acc, ALU.add).then_inc(sm["pb_ev"], 1)
                        if br == "w":
                            link(dve.tensor_tensor(oN, oN, acc, ALU.add))
                            link(dve.tensor_reduce(rsN, pbt.rearrange("p (j c) -> p c j", j=6), AX.X, ALU.add))
                            link(dve.tensor_tensor(oN, oN, rsN, ALU.add))
                            for n, o in enumerate((oN, oD)):
                                for g in range(2):
                                    r = slice(HD * g, HD * g + HD)
                                    dve.tensor_copy(ymix[r, NP * n:NP * n + NP, S:T],
                                                    o[r, :].rearrange("x (b g p) -> x g p b", g=2, p=NP)[:, g])

            for t in range(len(units) + 4):
                if t < len(units):
                    i, p, g, br, k0, o = units[t]
                    n = P * (i + 1 - k0)
                    if br == "d" and steps:
                        top_keys(len(steps))
                    tab = (Dw[:, 3 * P - n:3 * P] if br == "w" else
                           D0[:, S - n:S] if br == "s" or i == 0 else TAB[i])
                    dve.wait_ge(sm["q_mm"], t + 1)
                    if t >= 2:
                        dve.wait_ge(sm["q_e"], t - 1)
                    dve.scalar_tensor_tensor(sbb[t % 2][:, 0:n], tab, SLOPE[NP * g + p], ps[t % 2][:, 0:n], ALU.mult,
                                             ALU.add).then_inc(sm["q_sc"], 1)
                u = t - 1
                if 0 <= u < len(units):
                    dve.wait_ge(sm["q_e"], u + 1)
                    dve.reciprocal(rrec[u % 2], rsum[u % 2]).then_inc(sm["q_g"], 1)
                if t < len(units):
                    dve.wait_ge(sm["q_sc"], t + 1)
                    dve.tensor_reduce(nmx[t % 2], sbb[t % 2][:, 0:n], AX.X, ALU.max, negate=True).then_inc(sm["q_m"], 1)
                u = t - 1
                if 0 <= u < len(units):
                    i, p, g, br, k0, o = units[u]
                    n = P * (i + 1 - k0)
                    dve.wait_ge(sm["q_g"], u + 1)
                    c = 3 * (NP * g + p) + (1 if br == "s" else 2)
                    gate = ones[:, 0:1] if br == "d" else gt[:, i, c:c + 1]
                    link(dve.scalar_tensor_tensor(rrec[u % 2], rrec[u % 2], 1e30, gate, ALU.min, ALU.mult))
                    dve.tensor_scalar(Pb[u % 2][:, 0:n], Pb[u % 2][:, 0:n], rrec[u % 2], None, ALU.mult).then_inc(sm["q_n"], 1)
                u = t - 4
                if u >= 0 and last_of[units[u][5]] == u:
                    i, p, g, br, k0, o = units[u]
                    dve.wait_ge(sm["q_o"], u + 1)
                    dve.tensor_copy(ymix[:, p + (NP if br == "d" else 0), P * i:P * i + P],
                                    ps[5 + o % 2][:, 0:P]).then_inc(sm["q_of"], 1)
                compressed_step(t)
                sample_queries(t)
                if t >= START and (t - START) % EVERY == EVERY - 1:
                    sample_step((t - START) // EVERY)
                if t == EARLY:
                    for u in range(NS1, NS1 + 2):
                        w_lo(u)
            for u in range(NS1 + 2, NS1 + NW):
                w_lo(u)
            residual(G_OUT1)
            norm(2)
            mlp(1, G_MLP1)
            norm(3)
            dve.wait_ge(sm["y_mm"], QT + 1)
            dve.tensor_copy(ytm[0:B, QT, 0:512], ps[4][0:B, :]).then_inc(sm["y_b"], 1)
            for half in range(2):
                for i in (1, 3):
                    dve.wait_ge(sm["y_mm"], (QT + 1) * half + i + 1)
                    dve.tensor_copy(ytm[:, i, 512 * half:512 * half + 512], ps[4 * half + i][:, :]).then_inc(sm["y_b"], 1)
            dve.wait_ge(sm["y_mm"], 2 * QT + 2)
            dve.tensor_copy(ytm[0:B, QT, 512:1024], ps[0][0:B, :]).then_inc(sm["y_b"], 1)


_INS = ['x_prompt', 'x_sample', 'state_conv', 'state_C', 'state_n', 'state_m', 'cache_kv', 'cache_idx', 'cache_win',
        'page_table', 'w_in_e', 'gate_b_e', 'conv_w', 'conv_b', 'w_out_e', 'w_in_o', 'w_cmp', 'w_out_o', 'w_up',
        'w_down', 'ln_g', 'ln_b']
_OUTS = [('y_p', (1, S, D)), ('y_s', (B, 1, D)), ('conv_p', (1, 1, 2, 512)), ('conv_s', (1, B, 2, 512)),
         ('c_p', (1, 1, MH, P, P)), ('c_s', (1, B, MH, P, P)), ('n_p', (1, 1, MH, P)), ('n_s', (1, B, MH, P)),
         ('m_p', (1, 1, MH)), ('m_s', (1, B, MH)), ('kv_p', (1, 1, S, 6, 2, HD)), ('kv_s', (1, B, 1, 6, 2, HD)),
         ('idx_p', (1, 1, S, 32)), ('idx_s', (1, B, 1, 32)), ('win_p', (1, 1, PAST, 2, 2, HD)),
         ('win_s', (1, B, PAST, 2, 2, HD))]


def kernel(**inputs):
    import numpy as _np
    import concourse.bacc as _bacc
    from concourse.bass_utils import run_bass_kernel_spmd as _run

    nc = _bacc.Bacc("TRN2", target_bir_lowering=False, num_devices=1)
    arrays, args = {}, []
    for name in _INS:
        a = _np.ascontiguousarray(inputs[name])
        arrays[f"in_{name}"] = a
        args.append(nc.dram_tensor(f"in_{name}", a.shape, mybir.dt.from_np(a.dtype), kind="ExternalInput").ap())
    for name, shape in _OUTS:
        args.append(nc.dram_tensor(f"out_{name}", shape, F32, kind="ExternalOutput").ap())
    build(nc, *args)
    r = _run(nc, [arrays], core_ids=[0])
    return tuple(r.results[0][f"out_{name}"] for name, _ in _OUTS)
```
